# Optimizing a Trainium2 kernel written in Bass

```python
import math
import jax, jax.numpy as jnp
from jax import lax
import numpy as np

D_MODEL = 1024
BATCH = 1
SEQ = 2048
DEPTH = 1

D_MIX = 2 * D_MODEL
S5_WIDTH = D_MIX // 4
S5_GROUP = 16
S5_GROUPS = S5_WIDTH // S5_GROUP
S5_STATE = 64
S5_DT_MIN = 1e-3
S5_DT_MAX = 1e-1
SSD_HEADDIM = 64
SSD_WIDTH = 3 * D_MIX // 8
SSD_HEADS = SSD_WIDTH // SSD_HEADDIM
SSD_GROUPS = 2
SSD_STATE = 128
SSD_CONV = 4
SSD_CHUNK = 128
SSD_XBC = SSD_WIDTH + 2 * SSD_GROUPS * SSD_STATE
MLSTM_WIDTH = D_MIX - S5_WIDTH - SSD_WIDTH
MLSTM_HEADS = 6
MLSTM_VDIM = MLSTM_WIDTH // MLSTM_HEADS
MLSTM_QKDIM = MLSTM_VDIM // 2
MLSTM_QK = MLSTM_HEADS * MLSTM_QKDIM
MLSTM_CONV = 4
MLSTM_CHUNK = 64
D_FF = ((8 * D_MODEL // 3 + 255) // 256) * 256
NORM_EPS = 1e-6
IN_SPLIT_SIZES = (S5_WIDTH, SSD_WIDTH, SSD_XBC, SSD_HEADS, 2 * MLSTM_QK, MLSTM_WIDTH,
                  MLSTM_HEADS, MLSTM_HEADS, MLSTM_WIDTH)
D_IN = sum(IN_SPLIT_SIZES)

kernel_name = "hybrid_s5_ssd_mlstm_parallel_heads"

def _f32(a):
    return a.astype(jnp.float32)

def rmsnorm(x, g):
    xf = _f32(x)
    y = xf * lax.rsqrt(jnp.mean(xf * xf, axis=-1, keepdims=True) + NORM_EPS) * _f32(g)
    return y.astype(x.dtype)

def causal_conv(x, w, b):
    k = w.shape[0]
    y = lax.conv_general_dilated(x, w[:, None, :], window_strides=(1,), padding=[(k - 1, 0)],
                                 dimension_numbers=('NWC', 'WIO', 'NWC'),
                                 feature_group_count=x.shape[-1])
    return y + b

def s5_mixer(u, lam_re, lam_im, log_step, b_re, b_im, c_re, c_im, d_skip, w_glu, b_glu):
    bsz, seq, _ = u.shape
    ug = u.reshape(bsz, seq, S5_GROUPS, S5_GROUP)
    step = jnp.exp(log_step)[:, None]
    mag = jnp.exp(lam_re * step)
    ang = lam_im * step
    a_re = mag * jnp.cos(ang)
    a_im = mag * jnp.sin(ang)
    den = lam_re * lam_re + lam_im * lam_im
    nr = a_re - 1.0
    f_re = (nr * lam_re + a_im * lam_im) / den
    f_im = (a_im * lam_re - nr * lam_im) / den
    bb_re = f_re[..., None] * b_re - f_im[..., None] * b_im
    bb_im = f_re[..., None] * b_im + f_im[..., None] * b_re
    bu_re = jnp.einsum('blgh,gph->lbgp', ug, bb_re)
    bu_im = jnp.einsum('blgh,gph->lbgp', ug, bb_im)
    shp = (seq, 1, S5_GROUPS, S5_STATE)
    ar_t = jnp.broadcast_to(a_re[None, None], shp)
    ai_t = jnp.broadcast_to(a_im[None, None], shp)

    def combine(left, right):
        ar_l, ai_l, br_l, bi_l = left
        ar_r, ai_r, br_r, bi_r = right
        ar = ar_r * ar_l - ai_r * ai_l
        ai = ar_r * ai_l + ai_r * ar_l
        br = ar_r * br_l - ai_r * bi_l + br_r
        bi = ar_r * bi_l + ai_r * br_l + bi_r
        return ar, ai, br, bi

    _, _, s_re, s_im = lax.associative_scan(combine, (ar_t, ai_t, bu_re, bu_im), axis=0)
    y = jnp.einsum('lbgp,ghp->blgh', s_re, c_re) - jnp.einsum('lbgp,ghp->blgh', s_im, c_im)
    y = (y + d_skip * ug).reshape(bsz, seq, S5_WIDTH)
    g = jax.nn.gelu(y)
    return g * jax.nn.sigmoid(g @ w_glu + b_glu)

def ssd_mixer(z, xbc, dt_raw, conv_w, conv_b, dt_bias, a_log, d_skip, norm_g):
    bsz, seq, _ = z.shape
    hpg = SSD_HEADS // SSD_GROUPS
    q = SSD_CHUNK
    nc = seq // q
    xbc = jax.nn.silu(causal_conv(xbc, conv_w, conv_b))
    xs, bm, cm = jnp.split(xbc, [SSD_WIDTH, SSD_WIDTH + SSD_GROUPS * SSD_STATE], axis=-1)
    dt = jax.nn.softplus(dt_raw + dt_bias)
    a = -jnp.exp(a_log).reshape(SSD_GROUPS, hpg)
    x = xs.reshape(bsz, nc, q, SSD_GROUPS, hpg, SSD_HEADDIM)
    bm = bm.reshape(bsz, nc, q, SSD_GROUPS, SSD_STATE)
    cm = cm.reshape(bsz, nc, q, SSD_GROUPS, SSD_STATE)
    dtc = dt.reshape(bsz, nc, q, SSD_GROUPS, hpg)
    xdt = x * dtc[..., None]
    acs = jnp.cumsum(dtc * a, axis=2)
    causal = jnp.tril(jnp.ones((q, q), dtype=bool))
    seg = acs[:, :, :, None] - acs[:, :, None]
    decay = jnp.exp(jnp.where(causal[:, :, None, None], seg, -jnp.inf))
    cb = jnp.einsum('bclgn,bcsgn->bclsg', cm, bm)
    y_diag = jnp.einsum('bclsg,bclsgj,bcsgjp->bclgjp', cb, decay, xdt)
    decay_end = jnp.exp(acs[:, :, -1:] - acs)
    states = jnp.einsum('bcsgn,bcsgj,bcsgjp->bcgjpn', bm, decay_end, xdt)
    chunk_decay = jnp.exp(acs[:, :, -1])

    def step(h, inp):
        st, dec = inp
        return h * dec[..., None, None] + st, h

    h0 = jnp.zeros((bsz, SSD_GROUPS, hpg, SSD_HEADDIM, SSD_STATE), xdt.dtype)
    _, h_prev = lax.scan(step, h0, (jnp.moveaxis(states, 1, 0), jnp.moveaxis(chunk_decay, 1, 0)))
    h_prev = jnp.moveaxis(h_prev, 0, 1)
    y_off = jnp.einsum('bclgn,bcgjpn,bclgj->bclgjp', cm, h_prev, jnp.exp(acs))
    y = y_diag + y_off + x * d_skip.reshape(SSD_GROUPS, hpg)[..., None]
    y = y.reshape(bsz, seq, SSD_WIDTH) * jax.nn.silu(z)
    y = rmsnorm(y.reshape(bsz, seq, SSD_GROUPS, SSD_WIDTH // SSD_GROUPS),
                norm_g.reshape(SSD_GROUPS, SSD_WIDTH // SSD_GROUPS))
    return y.reshape(bsz, seq, SSD_WIDTH)

def mlstm_mixer(qk, v, i_raw, f_raw, o_raw, conv_w, conv_b, b_i, b_f):
    bsz, seq, _ = v.shape
    hh, dk, dv, t = MLSTM_HEADS, MLSTM_QKDIM, MLSTM_VDIM, MLSTM_CHUNK
    nc = seq // t
    qk = jax.nn.silu(causal_conv(qk, conv_w, conv_b))
    q, k = jnp.split(qk, [MLSTM_QK], axis=-1)
    q = q.reshape(bsz, nc, t, hh, dk)
    k = k.reshape(bsz, nc, t, hh, dk) * (dk ** -0.5)
    v = v.reshape(bsz, nc, t, hh, dv)
    log_i = (i_raw + b_i).reshape(bsz, nc, t, hh)
    log_f = jax.nn.log_sigmoid(f_raw + b_f).reshape(bsz, nc, t, hh)
    bcum = jnp.cumsum(log_f, axis=2)
    causal = jnp.tril(jnp.ones((t, t), dtype=bool))
    dmat = bcum[:, :, :, None, :] - bcum[:, :, None, :, :] + log_i[:, :, None, :, :]
    dmat = jnp.where(causal[:, :, None], dmat, -jnp.inf)
    w_end = bcum[:, :, -1:, :] - bcum + log_i
    a_loc = jnp.max(w_end, axis=2)
    e_end = jnp.exp(w_end - a_loc[:, :, None])
    c_loc = jnp.einsum('bcsh,bcshk,bcshv->bchkv', e_end, k, v)
    n_loc = jnp.einsum('bcsh,bcshk->bchk', e_end, k)
    g_chunk = bcum[:, :, -1]

    def step(carry, inp):
        c_st, n_st, m_st = carry
        c_l, n_l, a_l, g = inp
        m_new = jnp.maximum(g + m_st, a_l)
        s_old = jnp.exp(g + m_st - m_new)
        s_new = jnp.exp(a_l - m_new)
        c_new = s_old[..., None, None] * c_st + s_new[..., None, None] * c_l
        n_new = s_old[..., None] * n_st + s_new[..., None] * n_l
        return (c_new, n_new, m_new), (c_st, n_st, m_st)

    init = (jnp.zeros((bsz, hh, dk, dv), v.dtype), jnp.zeros((bsz, hh, dk), v.dtype),
            jnp.zeros((bsz, hh), v.dtype))
    xs = (jnp.moveaxis(c_loc, 1, 0), jnp.moveaxis(n_loc, 1, 0),
          jnp.moveaxis(a_loc, 1, 0), jnp.moveaxis(g_chunk, 1, 0))
    _, (c_prev, n_prev, m_prev) = lax.scan(step, init, xs)
    c_prev = jnp.moveaxis(c_prev, 0, 1)
    n_prev = jnp.moveaxis(n_prev, 0, 1)
    m_prev = jnp.moveaxis(m_prev, 0, 1)
    w_inter = bcum + m_prev[:, :, None, :]
    m_row = jnp.maximum(w_inter, jnp.max(dmat, axis=3))
    s_inter = jnp.exp(w_inter - m_row)
    p = jnp.exp(dmat - m_row[:, :, :, None, :])
    qk_s = jnp.einsum('bcthk,bcshk->bctsh', q, k) * p
    num = (jnp.einsum('bctsh,bcshv->bcthv', qk_s, v)
           + s_inter[..., None] * jnp.einsum('bcthk,bchkv->bcthv', q, c_prev))
    den = jnp.sum(qk_s, axis=3) + s_inter * jnp.einsum('bcthk,bchk->bcth', q, n_prev)
    den = jnp.maximum(jnp.abs(den), jnp.exp(-m_row))
    h = (num / den[..., None]).reshape(bsz, seq, MLSTM_WIDTH)
    return jax.nn.sigmoid(o_raw) * h

def hybrid_layer(x, norm_pre_mix, w_in, s5_lambda_re, s5_lambda_im, s5_log_step, s5_b_re, s5_b_im,
                 s5_c_re, s5_c_im, s5_d, s5_w_glu, s5_b_glu, ssd_conv_w, ssd_conv_b, ssd_dt_bias,
                 ssd_a_log, ssd_d, ssd_norm, mlstm_conv_w, mlstm_conv_b, mlstm_b_i, mlstm_b_f,
                 w_out, norm_post_mix, norm_pre_ffn, w_gate, w_up, w_down, norm_post_ffn):
    h = rmsnorm(x, norm_pre_mix)
    proj = _f32(h @ w_in)
    offs = list(np.cumsum(IN_SPLIT_SIZES)[:-1])
    u, z, xbc, dt_raw, qk, v, i_raw, f_raw, o_raw = jnp.split(proj, [int(o) for o in offs], axis=-1)
    y_a = s5_mixer(u, _f32(s5_lambda_re), _f32(s5_lambda_im), _f32(s5_log_step), _f32(s5_b_re),
                   _f32(s5_b_im), _f32(s5_c_re), _f32(s5_c_im), _f32(s5_d), _f32(s5_w_glu), _f32(s5_b_glu))
    y_b = ssd_mixer(z, xbc, dt_raw, _f32(ssd_conv_w), _f32(ssd_conv_b), _f32(ssd_dt_bias),
                    _f32(ssd_a_log), _f32(ssd_d), _f32(ssd_norm))
    y_c = mlstm_mixer(qk, v, i_raw, f_raw, o_raw, _f32(mlstm_conv_w), _f32(mlstm_conv_b),
                      _f32(mlstm_b_i), _f32(mlstm_b_f))
    mix = jnp.concatenate([y_a, y_b, y_c], axis=-1).astype(x.dtype) @ w_out
    x = x + rmsnorm(mix, norm_post_mix)
    h = rmsnorm(x, norm_pre_ffn)
    ff = (jax.nn.silu(h @ w_gate) * (h @ w_up)) @ w_down
    return x + rmsnorm(ff, norm_post_ffn)

def setup_inputs(seed: int = 0) -> dict:
    key = jax.random.key(seed)
    ks = iter(jax.random.split(key, 32))
    nrm = lambda shape, s: jax.random.normal(next(ks), shape, jnp.float32) * s
    gain = lambda shape: 1.0 + nrm(shape, 0.02)
    L_ = DEPTH
    n_idx = jnp.arange(S5_STATE, dtype=jnp.float32)
    log_dt_ssd = jax.random.uniform(next(ks), (L_, SSD_HEADS), jnp.float32,
                                    math.log(1e-3), math.log(1e-1))
    dt_ssd = jnp.exp(log_dt_ssd)
    return {
        "x": nrm((BATCH, SEQ, D_MODEL), 1.0),
        "norm_pre_mix": gain((L_, D_MODEL)),
        "w_in": nrm((L_, D_MODEL, D_IN), D_MODEL ** -0.5),
        "s5_lambda_re": -0.5 + nrm((L_, S5_GROUPS, S5_STATE), 0.01),
        "s5_lambda_im": jnp.pi * n_idx + nrm((L_, S5_GROUPS, S5_STATE), 0.01),
        "s5_log_step": jax.random.uniform(next(ks), (L_, S5_GROUPS), jnp.float32,
                                          math.log(S5_DT_MIN), math.log(S5_DT_MAX)),
        "s5_b_re": nrm((L_, S5_GROUPS, S5_STATE, S5_GROUP), (2 * S5_GROUP) ** -0.5),
        "s5_b_im": nrm((L_, S5_GROUPS, S5_STATE, S5_GROUP), (2 * S5_GROUP) ** -0.5),
        "s5_c_re": nrm((L_, S5_GROUPS, S5_GROUP, S5_STATE), (2 * S5_STATE) ** -0.5),
        "s5_c_im": nrm((L_, S5_GROUPS, S5_GROUP, S5_STATE), (2 * S5_STATE) ** -0.5),
        "s5_d": nrm((L_, S5_GROUPS, S5_GROUP), 1.0),
        "s5_w_glu": nrm((L_, S5_WIDTH, S5_WIDTH), S5_WIDTH ** -0.5),
        "s5_b_glu": nrm((L_, S5_WIDTH), 0.01),
        "ssd_conv_w": nrm((L_, SSD_CONV, SSD_XBC), SSD_CONV ** -0.5),
        "ssd_conv_b": nrm((L_, SSD_XBC), 0.01),
        "ssd_dt_bias": dt_ssd + jnp.log(-jnp.expm1(-dt_ssd)),
        "ssd_a_log": jnp.log(jax.random.uniform(next(ks), (L_, SSD_HEADS), jnp.float32, 1.0, 16.0)),
        "ssd_d": 1.0 + nrm((L_, SSD_HEADS), 0.1),
        "ssd_norm": gain((L_, SSD_WIDTH)),
        "mlstm_conv_w": nrm((L_, MLSTM_CONV, 2 * MLSTM_QK), MLSTM_CONV ** -0.5),
        "mlstm_conv_b": nrm((L_, 2 * MLSTM_QK), 0.01),
        "mlstm_b_i": nrm((L_, MLSTM_HEADS), 0.1),
        "mlstm_b_f": jnp.linspace(3.0, 6.0, MLSTM_HEADS, dtype=jnp.float32) + nrm((L_, MLSTM_HEADS), 0.1),
        "w_out": nrm((L_, D_MIX, D_MODEL), D_MIX ** -0.5),
        "norm_post_mix": gain((L_, D_MODEL)),
        "norm_pre_ffn": gain((L_, D_MODEL)),
        "w_gate": nrm((L_, D_MODEL, D_FF), D_MODEL ** -0.5),
        "w_up": nrm((L_, D_MODEL, D_FF), D_MODEL ** -0.5),
        "w_down": nrm((L_, D_FF, D_MODEL), D_FF ** -0.5),
        "norm_post_ffn": gain((L_, D_MODEL)),
    }

def reference(x, norm_pre_mix, w_in, s5_lambda_re, s5_lambda_im, s5_log_step, s5_b_re, s5_b_im,
              s5_c_re, s5_c_im, s5_d, s5_w_glu, s5_b_glu, ssd_conv_w, ssd_conv_b, ssd_dt_bias,
              ssd_a_log, ssd_d, ssd_norm, mlstm_conv_w, mlstm_conv_b, mlstm_b_i, mlstm_b_f,
              w_out, norm_post_mix, norm_pre_ffn, w_gate, w_up, w_down, norm_post_ffn):
    for l in range(DEPTH):
        x = hybrid_layer(x, norm_pre_mix[l], w_in[l], s5_lambda_re[l], s5_lambda_im[l], s5_log_step[l],
                         s5_b_re[l], s5_b_im[l], s5_c_re[l], s5_c_im[l], s5_d[l], s5_w_glu[l],
                         s5_b_glu[l], ssd_conv_w[l], ssd_conv_b[l], ssd_dt_bias[l], ssd_a_log[l],
                         ssd_d[l], ssd_norm[l], mlstm_conv_w[l], mlstm_conv_b[l], mlstm_b_i[l],
                         mlstm_b_f[l], w_out[l], norm_post_mix[l], norm_pre_ffn[l], w_gate[l],
                         w_up[l], w_down[l], norm_post_ffn[l])
    return x


_drawn_inputs = setup_inputs


def setup_inputs(seed=0):
    import zlib

    import numpy as np

    out = dict(_drawn_inputs(seed))
    spreads = {}
    factors = {'s5_lambda_re': 64.0,
     's5_lambda_im': 30.904,
     's5_log_step': 31.352,
     's5_b_re': 43.368,
     's5_b_im': 43.56,
     's5_c_re': 43.048,
     's5_c_im': 43.312,
     's5_b_glu': 64.0,
     'ssd_conv_b': 5.16,
     'ssd_norm': 3.878,
     'mlstm_conv_b': 30.948,
     'mlstm_b_i': 64.0,
     'norm_post_mix': 3.47,
     'norm_pre_ffn': 3.367,
     'norm_post_ffn': 18.262}
    for name, (base, spread) in spreads.items():
        noise = np.random.default_rng([zlib.crc32(name.encode()), seed]).standard_normal(out[name].shape)
        drawn = base * np.exp(spread * noise) if base else spread * noise
        out[name] = __import__('jax').numpy.asarray(drawn.astype(out[name].dtype))
    for name, factor in factors.items():
        out[name] = (out[name] * factor).astype(out[name].dtype)
    return out
```

```python
import math
from contextlib import ExitStack

import concourse.bass as bass
import numpy as np
from concourse import mybir

F32 = mybir.dt.float32
F32R = mybir.dt.float32r
ALU = mybir.AluOpType
ACT = mybir.ActivationFunctionType
AX = mybir.AxisListType
ds = bass.ds

P = 128
T, D = 2048, 1024
KD = D // P
TT = T // P
NB = 512
BLK = T // NB
EPS = 1e-6
S5W, S5G, S5H, S5P = 512, 32, 16, 64
XW, HS, HD, NG, NS = 768, 12, 64, 2, 128
VW, HM, DK, DV = 768, 6, 64, 128
DMIX = 2048
FF = 2816
FT = FF // P
UT, CT, CTT = 4, 16, 12
TOKC = 384
J = 8
NCH = T // J


def scope(nc, ctx):
    sems = []

    def give_back():
        if sems:
            nc.clear_and_free_semaphores(sems)
            nc.all_engine_barrier()

    ctx.callback(give_back)

    def sb(name, shape, dt=F32):
        return ctx.enter_context(nc.sbuf_tensor(name, shape, dt))

    def ps(name, shape, dt=F32):
        return ctx.enter_context(nc.psum_tensor(name, shape, dt))

    def sem(name):
        sems.append(nc.alloc_semaphore(name=name))
        return sems[-1]

    return sb, ps, sem


def step(eng, ins, sem, value):
    ins.then_inc(sem, 1)
    eng.wait_ge(sem, value)


class Chain:

    def __init__(self, eng, sem):
        self.eng, self.sem, self.base, self.k = eng, sem, 0, 0

    def round(self, i, per_round):
        self.start = self.base + self.k
        self.base, self.k, self.per_round = self.start + i * per_round, 0, per_round

    def end(self, rounds):
        assert self.k == self.per_round, (self.k, self.per_round)
        self.base, self.k = self.start + rounds * self.per_round, 0

    def __call__(self, ins):
        self.k += 1
        step(self.eng, ins, self.sem, self.base + self.k)

def phase_norm(nc, x, gain_pre, ident, h_hi, h_lo):
    x_tiles = x[0].rearrange("(n p) d -> n p d", p=P)
    with ExitStack() as ctx:
        sb, ps, sem = scope(nc, ctx)
        xt, xn, junk, hraw = (sb("n_" + s, [P, 2, D]) for s in ("x", "xn", "junk", "hraw"))
        gain, ident_sb = sb("n_gain", [P, KD]), sb("n_ident", [P, P])
        stat = sb("n_stat", [P, 2, 4])
        banks = ps("n_banks", [P, 2, 2, NB])
        ssq_ok, mean_ok, root_ok, xn_ok, tr_ok, hraw_ok, hi_ok, lo_ok = (
            sem("n_" + s) for s in ("ssq_ok", "mean_ok", "root_ok", "xn_ok", "tr_ok", "hraw_ok", "hi_ok", "lo_ok"))
        const_in, x_in, dve_chain = sem("n_const_in"), (sem("n_x_in0"), sem("n_x_in1")), sem("n_dve_chain")
        block = ctx.enter_context(nc.Block())
        half = TT // 2

        @block.sync
        def _(sp):
            sp.dma_start(gain[:], gain_pre).then_inc(const_in, 16)
            sp.dma_start(ident_sb[:], ident).then_inc(const_in, 16)
            with sp.Fori(0, half) as i:
                for b in range(2):
                    n = i * 2 + b
                    sp.wait_ge(xn_ok, n + 1)
                    sp.dma_start(xt[:, b, :], x_tiles[ds(n, 1)].rearrange("a p d -> (a p) d")).then_inc(x_in[b], 16)

        @block.scalar
        def _(act):
            for s in (ssq_ok, root_ok, hi_ok):
                act.sem_inc(s, 2)
            with act.Fori(0, half) as i:
                for b in range(2):
                    n = i * 2 + b
                    act.wait_ge(x_in[b], i * 16 + 16)
                    act.wait_ge(xn_ok, n + 1)
                    step(act, nc.scalar.activation(junk[:, b, :], xt[:, b, :], ACT.Square,
                                                   accum_out=stat[:, b, 0:1]), ssq_ok, n + 3)
                    act.wait_ge(mean_ok, n + 3)
                    step(act, nc.scalar.activation(stat[:, b, 2:3], stat[:, b, 1:2], ACT.Sqrt), root_ok, n + 3)
                    act.wait_ge(hraw_ok, n + 3)
                    step(act, nc.scalar.activation(h_hi[:, :, ds(n * P, P)],
                                                   hraw[:, b, :].rearrange("p (k t) -> p k t", k=KD), ACT.Copy),
                         hi_ok, n + 3)

        @block.tensor
        def _(pe):
            pe.sem_inc(tr_ok, 2)
            pe.wait_ge(const_in, 32)
            with pe.Fori(0, half) as i:
                for b in range(2):
                    n = i * 2 + b
                    pe.wait_ge(xn_ok, n + 3)
                    pe.wait_ge(hraw_ok, n + 1)
                    for k in range(KD):
                        last = nc.tensor.transpose(banks[:, b, k // 4, (k % 4) * P:(k % 4 + 1) * P],
                                                   xn[:, b, k * P:(k + 1) * P], ident_sb[:])
                    last.then_inc(tr_ok, 1)

        @block.vector
        def _(dve):
            for s in (mean_ok, xn_ok, hraw_ok, lo_ok):
                dve.sem_inc(s, 2)
            chain = Chain(dve, dve_chain)
            dve.wait_ge(const_in, 32)
            with dve.Fori(0, half) as i:
                chain.round(i, 4)
                for b in range(2):
                    n = i * 2 + b
                    dve.wait_ge(ssq_ok, n + 3)
                    step(dve, nc.vector.tensor_scalar(stat[:, b, 1:2], stat[:, b, 0:1], 1.0 / D, EPS, ALU.mult,
                                                      ALU.add), mean_ok, n + 3)
                    dve.wait_ge(root_ok, n + 3)
                    chain(nc.vector.reciprocal(stat[:, b, 3:4], stat[:, b, 2:3]))
                    dve.wait_ge(tr_ok, n + 1)
                    step(dve, nc.vector.tensor_scalar(xn[:, b, :], xt[:, b, :], stat[:, b, 3:4], None, ALU.mult),
                         xn_ok, n + 3)
                    dve.wait_ge(tr_ok, n + 3)
                    for q in range(2):
                        g4 = gain[:, q * 4:q * 4 + 4].unsqueeze(2).to_broadcast([P, 4, P])
                        ins = nc.vector.tensor_tensor(
                            hraw[:, b, q * NB:(q + 1) * NB].rearrange("p (k t) -> p k t", k=4),
                            banks[:, b, q, :].rearrange("p (k t) -> p k t", k=4), g4, ALU.mult)
                        if q == 0:
                            chain(ins)
                        else:
                            step(dve, ins, hraw_ok, n + 3)
                    dve.wait_ge(hi_ok, n + 3)
                    step(dve, nc.vector.tensor_tensor(h_lo[:, :, ds(n * P, P)],
                                                      hraw[:, b, :].rearrange("p (k t) -> p k t", k=KD),
                                                      h_hi[:, :, ds(n * P, P)].bitcast(F32), ALU.subtract),
                         lo_ok, n + 3)
            chain.end(half)

def phase_channels(nc, w_chan, conv_w, conv_b, ident, h_hi, h_lo, u_dram, conv_dram, tok_dram, gate_rows):
    with ExitStack() as ctx:
        sb, ps, sem = scope(nc, ctx)
        w_raw = sb("c_w_raw", [P, 2, KD, P])
        w_hi, w_lo = sb("c_w_hi", [P, 2, KD, P], F32R), sb("c_w_lo", [P, 2, KD, P], F32R)
        row = sb("c_row", [P, 2, T + 4])
        conv = sb("c_conv", [P, 2, T])
        tok = sb("c_tok", [P, 2, TT // 2, P])
        cw, cb, ident_sb = sb("c_cw", [P, CT, 4]), sb("c_cb", [P, CT]), sb("c_ident", [P, P])
        banks, tr_banks = ps("c_banks", [P, BLK, NB]), ps("c_tr_banks", [P, 2, NB])
        w_in = (sem("c_w_in0"), sem("c_w_in1"))
        const_in, whi_ok, wlo_ok, mm_ok, evac_ok, acc_ok, silu_ok, tr_ok, tok_ok = (
            sem("c_" + s) for s in ("const_in", "whi_ok", "wlo_ok", "mm_ok", "evac_ok", "acc_ok", "silu_ok",
                                    "tr_ok", "tok_ok"))
        row_out, tok_out = (sem("c_row_out0"), sem("c_row_out1")), (sem("c_tok_out0"), sem("c_tok_out1"))
        dve_chain = sem("c_dve_chain")
        block = ctx.enter_context(nc.Block())
        TILES = UT + CT + 1
        GATE = TILES - 1
        r_u, r_t, r_c = UT // 2, CTT // 2, (CT - CTT) // 2

        @block.sync
        def _(sp):
            sp.dma_start(cw[:], conv_w).then_inc(const_in, 16)
            sp.dma_start(cb[:], conv_b).then_inc(const_in, 16)
            sp.dma_start(ident_sb[:], ident).then_inc(const_in, 16)

            def load(n, b):
                sp.wait_ge(wlo_ok, n + 1)
                sp.dma_start(w_raw[:, b].rearrange("p k m -> p (k m)"),
                             w_chan[ds(n, 1)].rearrange("a p m -> (a p) m")).then_inc(w_in[b], 16)

            with sp.Fori(0, GATE // 2) as i:
                for b in range(2):
                    load(i * 2 + b, b)
            load(GATE, 0)

        @block.gpsimd
        def _(pool):
            with pool.Fori(0, r_u) as i:
                for b in range(2):
                    n = i * 2 + b
                    pool.wait_ge(evac_ok, 4 * n + 4 + 8)
                    pool.dma_start(u_dram[:, ds(n * P, P), :].rearrange("j p c -> p j c"),
                                   row[:, b, 0:T].rearrange("p (j c) -> p j c", j=J)).then_inc(row_out[b], 16)
            with pool.Fori(0, r_t) as i:
                for b in range(2):
                    n = i * 2 + b
                    pool.wait_ge(silu_ok, n + 3)
                    pool.dma_start(conv_dram[ds(n, 1)].rearrange("a p t -> (a p) t"), conv[:, b, :]
                                   ).then_inc(row_out[b], 16)
                    for half in range(2):
                        pool.wait_ge(tok_ok, 4 * n + 2 * half + 2)
                        pool.dma_start(tok_dram[half * T // 2:(half + 1) * T // 2, ds(n * P, P)]
                                       .rearrange("(a p) m -> p a m", p=P), tok[:, half]).then_inc(tok_out[half], 16)
            with pool.Fori(0, r_c) as i:
                for b in range(2):
                    n = i * 2 + b + CTT
                    pool.wait_ge(silu_ok, n + 3)
                    pool.dma_start(conv_dram[ds(n, 1)].rearrange("a p t -> (a p) t"), conv[:, b, :]
                                   ).then_inc(row_out[b], 16)
            for b in range(2):
                pool.wait_ge(row_out[b], 16 * (UT + CT) // 2)
                pool.wait_ge(tok_out[b], 16 * CTT)

        @block.scalar
        def _(act):
            act.sem_inc(whi_ok, 2)
            act.sem_inc(evac_ok, 8)
            act.sem_inc(silu_ok, 2)

            def upper(n, b, nth):
                act.wait_ge(w_in[b], nth * 16)
                act.wait_ge(mm_ok, 4 * n + 4)
                step(act, nc.scalar.activation(w_hi[:, b], w_raw[:, b], ACT.Copy), whi_ok, n + 3)

            upper(0, 0, 1)
            with act.Fori(0, r_u) as i:
                for b in range(2):
                    n = i * 2 + b
                    upper(n + 1, 1 - b, i + 1 + b)
                    act.wait_ge(row_out[b], i * 16)
                    for q in range(BLK):
                        act.wait_ge(mm_ok, 4 * n + q + 1 + 8)
                        step(act, nc.scalar.activation(
                            row[:, b, 0:T].rearrange("p (j c) -> p c j", j=J)[:, q * NB // J:(q + 1) * NB // J, :],
                            banks[:, q, :].rearrange("p (c j) -> p c j", j=J), ACT.Copy), evac_ok, 4 * n + q + 1 + 8)

            def conv_tiles(first, rounds):
                with act.Fori(0, rounds) as i:
                    for b in range(2):
                        m = i * 2 + b + first
                        n = m + UT
                        upper(n + 1, 1 - b, i + (first + UT) // 2 + 1 + b)
                        act.wait_ge(acc_ok, m + 1)
                        if first == 0:
                            act.wait_ge(row_out[b], 16 * r_u)
                            act.wait_ge(acc_ok, 2)
                        for q in range(BLK):
                            act.wait_ge(mm_ok, 4 * n + q + 1 + 8)
                            step(act, nc.scalar.activation(row[:, b, 3 + q * NB:3 + (q + 1) * NB], banks[:, q, :],
                                                           ACT.Copy), evac_ok, 4 * n + q + 1 + 8)
                        act.wait_ge(acc_ok, m + 3)
                        step(act, nc.scalar.activation(conv[:, b, :], conv[:, b, :], ACT.Silu), silu_ok, m + 3)

            conv_tiles(0, r_t)
            conv_tiles(CTT, r_c)
            for q in range(BLK):
                act.wait_ge(mm_ok, 4 * GATE + q + 1 + 8)
                step(act, nc.scalar.activation(gate_rows[:, q * NB:(q + 1) * NB], banks[:, q, :], ACT.Copy),
                     evac_ok, 4 * GATE + q + 1 + 8)

        @block.vector
        def _(dve):
            dve.sem_inc(wlo_ok, 2)
            chain = Chain(dve, dve_chain)

            def lower(n, b):
                dve.wait_ge(whi_ok, n + 3)
                dve.wait_ge(mm_ok, 4 * n + 4)
                step(dve, nc.vector.tensor_tensor(w_lo[:, b], w_raw[:, b], w_hi[:, b].bitcast(F32), ALU.subtract),
                     wlo_ok, n + 3)

            lower(0, 0)
            with dve.Fori(0, r_u) as i:
                for b in range(2):
                    lower(i * 2 + b + 1, 1 - b)
            for b in range(2):
                dve.wait_ge(row_out[b], 16 * r_u)
                chain(nc.vector.memset(row[:, b, 0:3], 0.0))
            dve.sem_inc(acc_ok, 2)
            dve.wait_ge(const_in, 48)

            def conv_tiles(first, rounds, transposed):
                with dve.Fori(0, rounds) as i:
                    chain.round(i, 6)
                    for b in range(2):
                        m = i * 2 + b + first
                        n = m + UT
                        lower(n + 1, 1 - b)
                        dve.wait_ge(evac_ok, 4 * n + 4 + 8)
                        dve.wait_ge(row_out[b], (i + (first + UT) // 2) * 16)
                        w = [cw[:, ds(m, 1), s:s + 1].rearrange("p a s -> p (a s)") for s in range(4)]
                        if transposed:
                            dve.wait_ge(tr_ok, 4 * m)
                        chain(nc.vector.tensor_scalar(conv[:, b, :], row[:, b, 3:T + 3], w[3], cb[:, ds(m, 1)],
                                                      ALU.mult, ALU.add))
                        for s in (2, 1, 0):
                            ins = nc.vector.scalar_tensor_tensor(conv[:, b, :], row[:, b, s:T + s], w[s], conv[:, b, :],
                                                                 ALU.mult, ALU.add)
                            if s:
                                chain(ins)
                            else:
                                step(dve, ins, acc_ok, m + 3)
                        if transposed:
                            for q in range(4):
                                half = q // 2
                                dve.wait_ge(tr_ok, 4 * m + q + 1)
                                if q % 2 == 0:
                                    dve.wait_ge(tok_out[half], m * 16)
                                step(dve, nc.vector.tensor_copy(
                                    tok[:, half, q % 2 * 4:q % 2 * 4 + 4, :].rearrange("p a m -> p (a m)"),
                                    tr_banks[:, q % 2, :]), tok_ok, 4 * m + q + 1)
                chain.end(rounds)

            conv_tiles(0, r_t, True)
            conv_tiles(CTT, r_c, False)

        @block.tensor
        def _(pe):
            pe.sem_inc(mm_ok, 8)
            pe.wait_ge(const_in, 48)

            def products(n, b):
                pe.wait_ge(wlo_ok, n + 3)
                for q in range(BLK):
                    pe.wait_ge(evac_ok, 4 * n + q + 1 + 4)
                    for k in range(KD):
                        for j, (w, h) in enumerate(((w_hi, h_hi), (w_hi, h_lo), (w_lo, h_hi))):
                            last = nc.tensor.matmul(banks[:, q, :], w[:, b, k, :], h[:, k, q * NB:(q + 1) * NB],
                                                    start=k == 0 and j == 0, stop=k == KD - 1 and j == 2)
                    last.then_inc(mm_ok, 1)

            def transposes(m, b):
                pe.wait_ge(silu_ok, m + 3)
                for q in range(4):
                    if q < 2:
                        pe.wait_ge(tok_ok, 4 * m)
                    else:
                        pe.wait_ge(tok_ok, 4 * m + q - 1)
                    for a in range(4):
                        last = nc.tensor.transpose(tr_banks[:, q % 2, a * P:(a + 1) * P],
                                                   conv[:, b, (q * 4 + a) * P:(q * 4 + a + 1) * P], ident_sb[:])
                    last.then_inc(tr_ok, 1)

            with pe.Fori(0, r_u) as i:
                for b in range(2):
                    products(i * 2 + b, b)
            products(UT, 0)
            with pe.Fori(0, r_t - 1) as i:
                for b in range(2):
                    m = i * 2 + b
                    products(m + UT + 1, 1 - b)
                    transposes(m, b)
            products(CTT - 1 + UT, 1)
            transposes(CTT - 2, 0)
            products(CTT + UT, 0)
            transposes(CTT - 1, 1)
            with pe.Fori(0, r_c - 1) as i:
                for b in range(2):
                    products(i * 2 + b + 1 + CTT + UT, 1 - b)
            products(CT + UT - 1, 1)
            products(GATE, 0)

def phase_tokens(nc, w_tok, h_hi, h_lo, tokmaj_dram):
    PAIR = 2
    with ExitStack() as ctx:
        sb, ps, sem = scope(nc, ctx)
        w_raw = sb("t_w_raw", [P, KD, TOKC])
        w_hi, w_lo = sb("t_w_hi", [P, 2, KD, TOKC], F32R), sb("t_w_lo", [P, 2, KD, TOKC], F32R)
        out = sb("t_out", [P, 2, PAIR, TOKC])
        banks = ps("t_banks", [P, 4, NB])
        w_in, whi_ok, wlo_ok, mm_ok, evac_ok, sent0, sent1 = (
            sem("t_" + s) for s in ("w_in", "whi_ok", "wlo_ok", "mm_ok", "evac_ok", "sent0", "sent1"))
        sent = (sent0, sent1)
        block = ctx.enter_context(nc.Block())
        kinds = (ACT.Silu, ACT.Sigmoid, ACT.Copy)
        blocks = 2 * len(kinds)

        @block.sync
        def _(sp):
            def load(n):
                sp.wait_ge(wlo_ok, n)
                sp.dma_start(w_raw[:].rearrange("p k m -> p (k m)"),
                             w_tok[ds(n, 1)].rearrange("a p m -> (a p) m")).then_inc(w_in, 16)

            with sp.Fori(0, blocks) as n:
                load(n)

        @block.gpsimd
        def _(pool):
            with pool.Fori(0, blocks) as n:
                for s in range(TT // PAIR):
                    pool.wait_ge(evac_ok, n * TT + (s + 1) * PAIR + 4)
                    pool.dma_start(tokmaj_dram[s * PAIR * P:(s + 1) * PAIR * P, ds(n * TOKC, TOKC)]
                                   .rearrange("(a p) m -> p a m", p=P), out[:, s % 2]).then_inc(sent[s % 2], 16)
            for b in range(2):
                pool.wait_ge(sent[b], blocks * (TT // PAIR // 2) * 16)

        @block.scalar
        def _(act):
            act.sem_inc(evac_ok, 4)

            def upper(n):
                act.wait_ge(w_in, n * 16 + 16)
                if n >= 2:
                    act.wait_ge(mm_ok, (n - 1) * TT)
                step(act, nc.scalar.activation(w_hi[:, n % 2], w_raw[:], ACT.Copy), whi_ok, n + 1)

            upper(0)
            for n in range(blocks):
                if n + 1 < blocks:
                    upper(n + 1)
                with act.Fori(0, TT // 4) as i:
                    for t in range(4):
                        m = i * 4 + (n * TT + t)
                        act.wait_ge(mm_ok, m + 1)
                        if t % PAIR == 0:
                            act.wait_ge(sent[t // PAIR], i * 16 + n * TT // 4 * 16)
                        step(act, nc.scalar.activation(out[:, t // PAIR, t % PAIR, :], banks[:, t, 0:TOKC],
                                                       kinds[n // 2]), evac_ok, m + 1 + 4)

        @block.vector
        def _(dve):
            for n in range(blocks):
                dve.wait_ge(whi_ok, n + 1)
                step(dve, nc.vector.tensor_tensor(w_lo[:, n % 2], w_raw[:], w_hi[:, n % 2].bitcast(F32), ALU.subtract),
                     wlo_ok, n + 1)

        @block.tensor
        def _(pe):
            with pe.Fori(0, blocks // 2) as i:
                for b in range(2):
                    n = i * 2 + b
                    pe.wait_ge(wlo_ok, n + 1)
                    for t in range(TT):
                        pe.wait_ge(evac_ok, n * TT + t + 1)
                        for k in range(KD):
                            for j, (h, w) in enumerate(((h_hi, w_hi), (h_lo, w_hi), (h_hi, w_lo))):
                                last = nc.tensor.matmul(banks[:, t % 4, 0:TOKC], h[:, k, t * P:(t + 1) * P],
                                                        w[:, b, k, :], start=k == 0 and j == 0,
                                                        stop=k == KD - 1 and j == 2)
                        last.then_inc(mm_ok, 1)

ROWS = 64
FR, IR = 32, 64
NBC = HS + HM


def phase_gates(nc, gate_rows, gate_bias, gate_sign, gate_log, ident, tok_cols, rows_dram, decay_dram):
    with ExitStack() as ctx:
        sb, ps, sem = scope(nc, ctx)
        x, e, u, lnu, sp_, cum = (sb("g_" + s, [ROWS, T]) for s in ("x", "e", "u", "ln", "softplus", "cum"))
        mask, beta, run_max = sb("g_mask", [ROWS, T]), sb("g_beta", [ROWS, T]), sb("g_max", [ROWS, T])
        col_b, col_c, col_d = (sb("g_col_" + s, [ROWS, T]) for s in "bcd")
        bias, sign, alog, neg_a = sb("g_bias", [P, 1]), sb("g_sign", [ROWS, 1]), sb("g_log", [ROWS, 1]), sb("g_neg_a", [ROWS, 1])
        m_prev, decay = sb("g_m_prev", [ROWS, TT]), sb("g_decay", [ROWS, TT])
        ident_sb = sb("g_ident", [P, P])
        banks = ps("g_banks", [P, 2, 2, 4, ROWS])
        const_in, out, act_chain, dve_chain = (sem("g_" + s) for s in ("const_in", "out", "act_chain", "dve_chain"))
        neg_a_ok, abs_ok, exp_ok, one_plus_ok, ln_ok, args_ok, factors_ok, tr_ok, tok_ok = (
            sem("g_" + s) for s in ("neg_a_ok", "abs_ok", "exp_ok", "one_plus_ok", "ln_ok", "args_ok", "factors_ok",
                                    "tr_ok", "tok_ok"))
        block = ctx.enter_context(nc.Block())
        f, s = slice(FR, FR + HM), slice(0, HS)

        def chunks(a):
            return a.rearrange("p (c t) -> p c t", t=P)

        def wide(a, n):
            return a.unsqueeze(2).to_broadcast([n, TT, P])

        @block.sync
        def _(sp):
            for dst, src in ((bias, gate_bias), (sign, gate_sign), (alog, gate_log), (ident_sb, ident)):
                sp.dma_start(dst[:], src).then_inc(const_in, 16)
            sp.wait_ge(args_ok, 1)
            sp.dma_start(rows_dram[:, 0:HS, :].rearrange("c r t -> r c t"), chunks(cum[s, :])).then_inc(out, 16)
            sp.dma_start(rows_dram[:, HS:NBC, :].rearrange("c r t -> r c t"), chunks(lnu[f, :])).then_inc(out, 16)
            sp.wait_ge(factors_ok, 1)
            sp.dma_start(decay_dram[0:HS, :], decay[s, :]).then_inc(out, 16)
            sp.dma_start(decay_dram[HS:NBC, :], decay[f, :]).then_inc(out, 16)
            sp.wait_ge(out, 64)

        @block.scalar
        def _(act):
            chain = Chain(act, act_chain)
            act.wait_ge(const_in, 64)
            nc.scalar.activation(neg_a[:], alog[:], ACT.Exp).then_inc(neg_a_ok, 1)
            act.wait_ge(abs_ok, 1)
            nc.scalar.activation(e[:], lnu[:], ACT.Exp, scale=-1.0).then_inc(exp_ok, 1)
            act.wait_ge(one_plus_ok, 1)
            nc.scalar.activation(lnu[:], u[:], ACT.Ln).then_inc(ln_ok, 1)
            act.wait_ge(args_ok, 1)
            chain(nc.scalar.activation(col_b[f, :], x[f, :], ACT.Exp))
            chain(nc.scalar.activation(col_c[:], col_c[:], ACT.Exp))
            chain(nc.scalar.activation(col_d[:], col_d[:], ACT.Exp))
            nc.scalar.activation(decay[:], decay[:], ACT.Exp).then_inc(factors_ok, 1)
            for n in range(TT // 2):
                act.wait_ge(tr_ok, n + 1)
                step(act, nc.scalar.activation(tok_cols[:, 2 * n:2 * n + 2], banks[:, n % 2], ACT.Copy), tok_ok, n + 1)

        @block.vector
        def _(dve):
            chain = Chain(dve, dve_chain)
            dve.wait_ge(const_in, 64)
            chain(nc.vector.tensor_scalar(x[:], gate_rows[0:ROWS, :], bias[0:ROWS, :], sign[:], ALU.add, ALU.mult))
            step(dve, nc.vector.scalar_tensor_tensor(lnu[:], x[:], -1.0, x[:], ALU.mult, ALU.max), abs_ok, 1)
            dve.wait_ge(exp_ok, 1)
            step(dve, nc.vector.tensor_scalar(u[:], e[:], 1.0, None, ALU.add), one_plus_ok, 1)
            chain(nc.vector.scalar_tensor_tensor(e[:], u[:], -1.0, e[:], ALU.add, ALU.subtract))
            dve.wait_ge(ln_ok, 1)
            chain(nc.vector.scalar_tensor_tensor(sp_[:], x[:], 0.0, lnu[:], ALU.max, ALU.add))
            chain(nc.vector.tensor_tensor(sp_[:], sp_[:], e[:], ALU.subtract))
            dve.wait_ge(neg_a_ok, 1)
            chain(nc.vector.tensor_scalar(x[:], sp_[:], neg_a[:], -1.0, ALU.mult, ALU.mult))
            chain(nc.vector.memset(mask[:], 1.0))
            chain(nc.vector.memset(chunks(mask[:])[:, :, 0:1], 0.0))
            chain(nc.vector.tensor_tensor_scan(cum[:], mask[:], x[:], 0.0, ALU.mult, ALU.add))
            end = chunks(cum[:])[:, :, P - 1]
            end_f = chunks(cum[f, :])[:, :, P - 1]
            chain(nc.vector.tensor_scalar(u[f, :], gate_rows[IR:IR + HM, :], bias[IR:IR + HM, :], None, ALU.add))
            chain(nc.vector.tensor_tensor(sp_[f, :], u[f, :], cum[f, :], ALU.subtract))
            chain(nc.vector.memset(beta[:], 0.0))
            chain(nc.vector.tensor_copy(chunks(beta[f, :])[:, 1:TT, 0], end_f[:, 0:TT - 1]))
            chain(nc.vector.tensor_tensor_scan(run_max[f, :], beta[f, :], sp_[f, :], 0.0, ALU.add, ALU.max))
            m_end = chunks(run_max[f, :])[:, :, P - 1]
            chain(nc.vector.memset(m_prev[:], 0.0))
            chain(nc.vector.tensor_tensor(m_prev[f, 1:TT], m_end[:, 0:TT - 1], end_f[:, 0:TT - 1], ALU.add))
            chain(nc.vector.tensor_tensor(chunks(x[f, :]), wide(m_prev[f, :], HM), chunks(run_max[f, :]), ALU.subtract))
            chain(nc.vector.tensor_scalar(col_b[:], cum[:], -1.0, None, ALU.mult))
            chain(nc.vector.tensor_scalar(lnu[f, :], run_max[f, :], -1.0, None, ALU.mult))
            chain(nc.vector.tensor_copy(col_c[:], cum[:]))
            chain(nc.vector.tensor_tensor(chunks(col_c[f, :]), chunks(sp_[f, :]), wide(m_end, HM), ALU.subtract))
            chain(nc.vector.tensor_tensor(chunks(col_d[:]), wide(end, ROWS), chunks(cum[:]), ALU.subtract))
            chain(nc.vector.tensor_tensor(col_d[f, :], lnu[f, :], cum[f, :], ALU.subtract))
            chain(nc.vector.tensor_copy(decay[:], end))
            step(dve, nc.vector.tensor_tensor(decay[f, :], m_prev[f, :], m_end, ALU.subtract), args_ok, 1)
            dve.wait_ge(factors_ok, 1)
            chain(nc.vector.tensor_scalar(col_c[f, :], col_c[f, :], DK ** -0.5, None, ALU.mult))
            step(dve, nc.vector.tensor_tensor(col_d[s, :], col_d[s, :], sp_[s, :], ALU.mult), args_ok, 2)

        @block.tensor
        def _(pe):
            pe.wait_ge(const_in, 64)
            pe.wait_ge(args_ok, 2)
            for n in range(TT // 2):
                if n >= 2:
                    pe.wait_ge(tok_ok, n - 1)
                for c in range(2):
                    for k, rows in enumerate((sp_, col_b, col_c, col_d)):
                        last = nc.tensor.transpose(banks[:, n % 2, c, k, :], rows[:, (2 * n + c) * P:(2 * n + c + 1) * P],
                                                   ident_sb[0:ROWS, 0:ROWS])
                last.then_inc(tr_ok, 1)

Q = S5G // 2
TWO_PI = 2 * math.pi
TURN = (6.28125, float(np.float32(TWO_PI - 6.28125)), float(TWO_PI - 6.28125 - np.float32(TWO_PI - 6.28125)))
MAGIC = 1.5 * 2.0 ** 23
PADK = (2 * J - 1) * S5H


def phase_s5_setup(nc, lam_re, lam_im, log_step, b_re, b_im, c_re, c_im, skip, ident, table, rho, ca, wt, kern_dram):
    with ExitStack() as ctx:
        sb, ps, sem = scope(nc, ctx)
        lre, lim, lst = (sb("s_" + s, [P, Q]) for s in ("lre", "lim", "lst"))
        br, bi, cr, ci, bbr, bbi = (sb("s_" + s, [P, Q, S5H]) for s in ("br", "bi", "cr", "ci", "bbr", "bbi"))
        ident_sb, skip_sb = sb("s_ident", [P, P]), sb("s_skip", [S5H, S5G])
        stp, mag, ang, turns, red_s, red_c, sin, cos, t0, t1, t2, t3, f_re, f_im, den = (
            sb("s_" + s, [P, Q]) for s in ("step", "mag", "ang", "turns", "red_s", "red_c", "sin", "cos", "t0", "t1", "t2",
                                           "t3", "f_re", "f_im", "den"))
        pow_re, pow_im = sb("s_pow_re", [P, Q, J + 1]), sb("s_pow_im", [P, Q, J + 1])
        w_re, w_im, tmp = (sb("s_" + s, [P, Q, J, S5H]) for s in ("w_re", "w_im", "tmp"))
        tmp2 = sb("s_tmp2", [P, Q, (J + 1) * S5H])
        kern = sb("s_kern", [S5H, S5G, PADK])
        banks, kbanks = ps("s_banks", [P, 2, NB]), ps("s_kbanks", [S5H, 2, 2, NB])
        const_in, out, dve_chain, act_chain = (sem("s_" + s) for s in ("const_in", "out", "dve_chain", "act_chain"))
        step_ok, expo_ok, mag_ok, angle_ok, trig_ok, w_ok, ca_ok, wt_tr, wt_ok, k_mm, k_ok, kern_ok = (
            sem("s_" + s) for s in ("step_ok", "expo_ok", "mag_ok", "angle_ok", "trig_ok", "w_ok", "ca_ok", "wt_tr",
                                    "wt_ok", "k_mm", "k_ok", "kern_ok"))
        block = ctx.enter_context(nc.Block())
        loads = ((lre, lam_re), (lim, lam_im), (lst, log_step), (br, b_re), (bi, b_im), (cr, c_re), (ci, c_im),
                 (ident_sb, ident), (skip_sb, skip))

        @block.sync
        def _(sp):
            for dst, src in loads:
                sp.dma_start(dst[:], src).then_inc(const_in, 16)
            sp.wait_ge(kern_ok, 1)
            sp.dma_start(kern_dram.rearrange("g h m -> h g m"), kern[:]).then_inc(out, 16)
            sp.wait_ge(out, 16)

        @block.scalar
        def _(act):
            act.wait_ge(const_in, 16 * len(loads))
            nc.scalar.activation(stp[:], lst[:], ACT.Exp).then_inc(step_ok, 1)
            act.wait_ge(expo_ok, 1)
            nc.scalar.activation(mag[:], t0[:], ACT.Exp).then_inc(mag_ok, 1)
            act.wait_ge(angle_ok, 1)
            nc.scalar.activation(sin[:], red_s[:], ACT.Sin).then_inc(trig_ok, 1)
            nc.scalar.activation(cos[:], red_c[:], ACT.Sin).then_inc(trig_ok, 1)
            for n in range(Q // 2):
                act.wait_ge(wt_tr, n + 1)
                step(act, nc.scalar.activation(wt[:, 2 * n:2 * n + 2].rearrange("p q r m -> p (q r m)"), banks[:, n % 2, :],
                                               ACT.Copy), wt_ok, n + 1)

        @block.vector
        def _(dve):
            chain = Chain(dve, dve_chain)
            tt, ts, stt = nc.vector.tensor_tensor, nc.vector.tensor_scalar, nc.vector.scalar_tensor_tensor
            mul, add, sub = ALU.mult, ALU.add, ALU.subtract
            dve.wait_ge(const_in, 16 * len(loads))
            dve.wait_ge(step_ok, 1)
            step(dve, tt(t0[:], lre[:], stp[:], mul), expo_ok, 1)
            chain(tt(ang[:], lim[:], stp[:], mul))
            for red, quarter in ((red_s, 0.0), (red_c, 0.25)):
                chain(ts(turns[:], ang[:], 1 / TWO_PI, quarter, mul, add))
                chain(ts(turns[:], turns[:], MAGIC, None, add))
                chain(ts(turns[:], turns[:], -MAGIC, None, add))
                chain(stt(red[:], turns[:], -TURN[0], ang[:], mul, add))
                chain(stt(red[:], turns[:], -TURN[1], red[:], mul, add))
                chain(stt(red[:], turns[:], -TURN[2], red[:], mul, add))
                if quarter:
                    chain(ts(red[:], red[:], math.pi / 2, None, add))
                ins = ts(red[:], red[:], 3.1415925, -3.1415925, ALU.min, ALU.max)
                if quarter:
                    step(dve, ins, angle_ok, 1)
                else:
                    chain(ins)
            dve.wait_ge(mag_ok, 1)
            dve.wait_ge(trig_ok, 2)

            def product(o_re, o_im, a_re, a_im, b_re_, b_im_, t):
                chain(tt(t, a_im, b_im_, mul))
                chain(tt(o_re, a_re, b_re_, mul))
                chain(tt(o_re, o_re, t, sub))
                chain(tt(t, a_re, b_im_, mul))
                chain(tt(o_im, a_im, b_re_, mul))
                chain(tt(o_im, o_im, t, add))

            chain(nc.vector.memset(pow_re[:, :, 0], 1.0))
            chain(nc.vector.memset(pow_im[:, :, 0], 0.0))
            chain(tt(pow_re[:, :, 1], mag[:], cos[:], mul))
            chain(tt(pow_im[:, :, 1], mag[:], sin[:], mul))
            for j in range(2, J + 1):
                product(pow_re[:, :, j], pow_im[:, :, j], pow_re[:, :, j - 1], pow_im[:, :, j - 1], pow_re[:, :, 1],
                        pow_im[:, :, 1], t0[:])
            chain(ts(t1[:], pow_re[:, :, 1], -1.0, None, add))
            chain(tt(t0[:], lre[:], lre[:], mul))
            chain(tt(den[:], lim[:], lim[:], mul))
            chain(tt(den[:], den[:], t0[:], add))
            chain(nc.vector.reciprocal(den[:], den[:]))
            chain(tt(t0[:], pow_im[:, :, 1], lim[:], mul))
            chain(tt(f_re[:], t1[:], lre[:], mul))
            chain(tt(f_re[:], f_re[:], t0[:], add))
            chain(tt(f_re[:], f_re[:], den[:], mul))
            chain(tt(t0[:], t1[:], lim[:], mul))
            chain(tt(f_im[:], pow_im[:, :, 1], lre[:], mul))
            chain(tt(f_im[:], f_im[:], t0[:], sub))
            chain(tt(f_im[:], f_im[:], den[:], mul))

            def over_h(a):
                return a.unsqueeze(2).to_broadcast([P, Q, S5H])

            product(bbr[:], bbi[:], over_h(f_re[:]), over_h(f_im[:]), br[:], bi[:], tmp[:, :, 0, :])
            for j in range(J):
                pr, pi = (over_h(a[:, :, J - 1 - j]) for a in (pow_re, pow_im))
                product(w_re[:, :, j, :], w_im[:, :, j, :], pr, pi, bbr[:], bbi[:], tmp[:, :, j, :])
            dve.sem_inc(w_ok, 1)
            for tau in range(J + 1):
                pr, pi = (over_h(a[:, :, tau]) for a in (pow_re, pow_im))
                at = slice(tau * S5H, (tau + 1) * S5H)
                product(ca[:, :, 0, at], ca[:, :, 1, at], pr, pi, cr[:], ci[:], tmp2[:, :, at])
            step(dve, ts(ca[:, :, 1], ca[:, :, 1], -1.0, None, mul), ca_ok, 1)
            chain(tt(t0[:], mag[:], mag[:], mul))
            chain(tt(t1[:], t0[:], t0[:], mul))
            chain(tt(rho[:], t1[:], t1[:], mul))
            now, nxt = (cos, sin), (t1, t2)
            for _ in range(3):
                product(nxt[0][:], nxt[1][:], now[0][:], now[1][:], now[0][:], now[1][:], t3[:])
                now, nxt = nxt, (now if now[0] is not cos else (f_re, f_im))
            chain(nc.vector.memset(table[:, :, 0, 0:1], 1.0))
            chain(nc.vector.memset(table[:, :, 1, 0:1], 0.0))
            n = 1
            while n < NCH:
                c, s = (a[:].unsqueeze(2).to_broadcast([P, Q, n]) for a in now)
                product(table[:, :, 0, n:2 * n], table[:, :, 1, n:2 * n], c, s, table[:, :, 0, 0:n], table[:, :, 1, 0:n],
                        tmp[:].rearrange("p q j h -> p q (j h)")[:, :, 0:n])
                n *= 2
                if n < NCH:
                    product(nxt[0][:], nxt[1][:], now[0][:], now[1][:], now[0][:], now[1][:], t3[:])
                    now, nxt = nxt, now
            chain(nc.vector.memset(kern[:], 0.0))
            for n in range(Q // 4):
                for e in range(2):
                    dve.wait_ge(k_mm, 2 * n + e + 1)
                    step(dve, nc.vector.tensor_copy(
                        kern[:].rearrange("h (q e) m -> h q e m", e=2)[:, 4 * n:4 * n + 4, e, (J - 1) * S5H:],
                        kbanks[:, n % 2, e, :].rearrange("h (q m) -> h q m", q=4)), k_ok, 2 * n + e + 1)
            zero_lag = kern[:, :, (J - 1) * S5H:J * S5H]
            t = w_re[0:S5H].rearrange("p q j h -> p (q j h)")[:, 0:S5G * S5H].rearrange("p (g h) -> p g h", h=S5H)
            dve.wait_ge(wt_ok, Q // 2)
            chain(tt(t, ident_sb[0:S5H, 0:S5H].unsqueeze(1).to_broadcast([S5H, S5G, S5H]),
                     skip_sb[:].unsqueeze(2).to_broadcast([S5H, S5G, S5H]), mul))
            step(dve, tt(zero_lag, zero_lag, t, add), kern_ok, 1)

        @block.tensor
        def _(pe):
            pe.wait_ge(w_ok, 1)
            pe.wait_ge(const_in, 16 * len(loads))
            for n in range(Q // 2):
                if n >= 2:
                    pe.wait_ge(wt_ok, n - 1)
                for q in range(2):
                    for r, w in enumerate((w_re, w_im)):
                        last = nc.tensor.transpose(banks[:, n % 2, (2 * q + r) * P:(2 * q + r + 1) * P],
                                                   w[:, 2 * n + q].rearrange("p j h -> p (j h)"), ident_sb[:])
                last.then_inc(wt_tr, 1)
            pe.wait_ge(ca_ok, 1)
            for n in range(Q // 4):
                if n >= 2:
                    pe.wait_ge(k_ok, 2 * n - 2)
                for e in range(2):
                    lanes = slice(e * S5P, (e + 1) * S5P)
                    for q in range(4):
                        for r, b in enumerate((bbr, bbi)):
                            last = nc.tensor.matmul(kbanks[:, n % 2, e, q * P:(q + 1) * P], b[lanes, 4 * n + q, :],
                                                    ca[lanes, 4 * n + q, r, 0:J * S5H], start=r == 0, stop=r == 1)
                    last.then_inc(k_mm, 1)


def phase_s5(nc, table, rho, ca, wt, kern_dram, u_dram, g_dram):
    with ExitStack() as ctx:
        sb, ps, sem = scope(nc, ctx)
        x, y = sb("r_x", [P, 2, 2, NCH]), sb("r_y", [P, S5G, NCH])
        w = sb("r_w", [P, 2, 4, P])
        kern = sb("r_kern", [P, 2, 2, P])
        prod, rot = sb("r_prod", [P, 4, NCH]), sb("r_rot", [P, 2, NCH])
        state, prod2 = sb("r_state", [P, 2, NCH]), sb("r_prod2", [P, 4, NCH])
        before = sb("r_before", [P, 2, 2, NCH])
        banks_in, banks_out = ps("r_banks_in", [P, 2, 2, NCH]), ps("r_banks_out", [P, 2, 2, NB])
        w_ok, in_mm, before_ok, out_mm, gelu_ok, prod_ok = (
            sem("r_" + s) for s in ("w_ok", "in_mm", "before_ok", "out_mm", "gelu_ok", "prod_ok"))
        x_in, kern_in, sent, dve_chain, pool_chain = (
            (sem("r_x_in0"), sem("r_x_in1")), (sem("r_kern_in0"), sem("r_kern_in1")), sem("r_sent"), sem("r_dve_chain"), sem("r_pool_chain"))
        block = ctx.enter_context(nc.Block())
        GT = S5G // UT

        @block.sync
        def _(sp):
            with sp.Fori(0, Q // 2) as i:
                for b in range(2):
                    q = i * 2 + b
                    sp.wait_ge(out_mm, q + 1)
                    for j in range(J):
                        sp.dma_start(x[j * S5H:(j + 1) * S5H, b], u_dram[j, ds(q * 2 * S5H, 2 * S5H), :]
                                     .rearrange("(g h) c -> h g c", h=S5H)).then_inc(x_in[b], 16)

        @block.gpsimd
        def _(pool):
            pool.sem_inc(w_ok, 2)
            with pool.Fori(0, Q // 2) as i:
                for b in range(2):
                    q = i * 2 + b
                    pool.wait_ge(out_mm, q + 1)
                    for step_i in range(J):
                        pool.dma_start(kern[step_i * S5H:(step_i + 1) * S5H, b],
                                       kern_dram[ds(q * 2, 2), :, (J - 1 - step_i) * S5H:(2 * J - 1 - step_i) * S5H]
                                       .rearrange("g h m -> h g m")).then_inc(kern_in[b], 16)
                    nc.gpsimd.tensor_copy(w[:, b, 0:2, :], wt[:, ds(q, 1)].rearrange("p a r m -> p (a r) m")
                                          ).then_inc(pool_chain, 1)
                    pool.wait_ge(pool_chain, q + 1)
                    step(pool, nc.gpsimd.tensor_copy(w[:, b, 2:4, :], ca[:, ds(q, 1), :, S5H:(J + 1) * S5H]
                                                     .rearrange("p a r m -> p (a r) m")), w_ok, q + 3)

        @block.tensor
        def _(pe):
            pe.sem_inc(in_mm, 2)
            pe.sem_inc(out_mm, 2)

            def states_in(q, b, nth):
                pe.wait_ge(x_in[b], nth * 16 * J)
                pe.wait_ge(w_ok, q + 3)
                pe.wait_ge(prod_ok, q + 1)
                for e in range(2):
                    for r in range(2):
                        last = nc.tensor.matmul(banks_in[e * S5P:(e + 1) * S5P, b, r, :], w[:, b, r, e * S5P:(e + 1) * S5P],
                                                x[:, b, e, :],
                                                start=r == 0, stop=True, skip_group_check=True)
                last.then_inc(in_mm, 1)

            def outputs(q, b, nth):
                pe.wait_ge(kern_in[b], nth * 16 * J)
                pe.wait_ge(gelu_ok, q + 1)
                for e in range(2):
                    nc.tensor.matmul(banks_out[:, b, e, 0:NCH], kern[:, b, e, :],
                                     x[:, b, e, :], start=True, stop=False)
                pe.wait_ge(before_ok, q + 3)
                for r in range(2):
                    for e in range(2):
                        lanes = slice(e * S5P, (e + 1) * S5P)
                        last = nc.tensor.matmul(banks_out[:, b, e, 0:NCH], w[lanes, b, 2 + r, :], before[lanes, b, r, :],
                                                start=False, stop=r == 1)
                last.then_inc(out_mm, 1)

            states_in(0, 0, 1)
            with pe.Fori(0, Q // 2 - 1) as i:
                for b in range(2):
                    states_in(i * 2 + b + 1, 1 - b, i + 1 + b)
                    outputs(i * 2 + b, b, i + 1)
            states_in(Q - 1, 1, Q // 2)
            outputs(Q - 2, 0, Q // 2)
            outputs(Q - 1, 1, Q // 2)

        @block.vector
        def _(dve):
            dve.sem_inc(prod_ok, 2)
            dve.sem_inc(before_ok, 2)
            chain = Chain(dve, dve_chain)
            tt = nc.vector.tensor_tensor
            chain(nc.vector.memset(before[:], 0.0))
            with dve.Fori(0, Q // 2) as i:
                chain.round(i, 2 * 9)
                for b in range(2):
                    q = i * 2 + b
                    cos, sin = (table[:, ds(q, 1), r, :].rearrange("p a c -> p (a c)") for r in range(2))
                    pair = table[:, ds(q, 1)].rearrange("p a r c -> p (a r) c")
                    dve.wait_ge(in_mm, q + 3)
                    for r in range(2):
                        chain(tt(prod[:, 2 * r:2 * r + 2, :],
                                 banks_in[:, b, r, :].unsqueeze(1).to_broadcast([P, 2, NCH]), pair, ALU.mult))
                    dve.sem_inc(prod_ok, 1)
                    chain(tt(rot[:, 0, :], prod[:, 0, :], prod[:, 3, :], ALU.add))
                    chain(tt(rot[:, 1, :], prod[:, 2, :], prod[:, 1, :], ALU.subtract))
                    r8 = rho[:, ds(q, 1)].to_broadcast([P, NCH])
                    for r in range(2):
                        chain(nc.vector.tensor_tensor_scan(state[:, r, :], r8, rot[:, r, :], 0.0, ALU.mult, ALU.add))
                    for r in range(2):
                        chain(tt(prod2[:, 2 * r:2 * r + 2, :], state[:, r, :].unsqueeze(1).to_broadcast([P, 2, NCH]),
                                 pair, ALU.mult))
                    dve.wait_ge(out_mm, q + 1)
                    n = NCH - 1
                    chain(tt(before[:, b, 0, 1:NCH], prod2[:, 0, 0:n], prod2[:, 3, 0:n], ALU.subtract))
                    step(dve, tt(before[:, b, 1, 1:NCH], prod2[:, 2, 0:n], prod2[:, 1, 0:n], ALU.add), before_ok, q + 3)
            chain.end(Q // 2)

        @block.scalar
        def _(act):
            act.sem_inc(gelu_ok, 2)
            with act.Fori(0, Q // 2) as i:
                for b in range(2):
                    q = i * 2 + b
                    act.wait_ge(out_mm, q + 3)
                    step(act, nc.scalar.activation(y[:, ds(q * 2, 2), :], banks_out[:, b, :, 0:NCH], ACT.Gelu_apprx_tanh),
                         gelu_ok, q + 3)
            for t in range(UT):
                for j in range(J):
                    act.dma_start(g_dram[j, t * P:(t + 1) * P].rearrange("(g h) c -> h g c", h=S5H),
                                  y[j * S5H:(j + 1) * S5H, t * GT:(t + 1) * GT, :]).then_inc(sent, 16)
            act.wait_ge(sent, 16 * UT * J)


def phase_s5_glu(nc, w_glu, b_glu, g_dram, yt_dram):
    with ExitStack() as ctx:
        sb, ps, sem = scope(nc, ctx)
        g, y = sb("u_g", [P, UT, T]), sb("u_y", [P, 2, T])
        wg, bg = sb("u_w", [P, UT, S5W]), sb("u_b", [P, UT])
        gate = sb("u_gate", [P, 2, NB])
        banks = ps("u_banks", [P, 2, NB])
        const_in, mm_ok, gate_ok, y_ok = (sem("u_" + s) for s in ("const_in", "mm_ok", "gate_ok", "y_ok"))
        sent = (sem("u_sent0"), sem("u_sent1"))
        block = ctx.enter_context(nc.Block())

        @block.sync
        def _(sp):
            sp.dma_start(wg[:], w_glu).then_inc(const_in, 16)
            sp.dma_start(bg[:], b_glu).then_inc(const_in, 16)
            for t in range(UT):
                sp.dma_start(g[:, t].rearrange("p (j c) -> p j c", j=J), g_dram[:, t * P:(t + 1) * P].rearrange("j p c -> p j c")
                             ).then_inc(const_in, 16)
            for m in range(UT):
                sp.wait_ge(y_ok, BLK * (m + 1))
                sp.dma_start(yt_dram[m], y[:, m % 2]).then_inc(sent[m % 2], 16)
            for b in range(2):
                sp.wait_ge(sent[b], 16 * UT // 2)

        @block.tensor
        def _(pe):
            pe.wait_ge(const_in, 16 * (2 + UT))
            for m in range(UT):
                for q in range(BLK):
                    n = m * BLK + q
                    if n >= 2:
                        pe.wait_ge(gate_ok, n - 1)
                    for k in range(UT):
                        last = nc.tensor.matmul(banks[:, n % 2, :], wg[:, k, m * P:(m + 1) * P],
                                                g[:, k, q * NB:(q + 1) * NB], start=k == 0, stop=k == UT - 1)
                    last.then_inc(mm_ok, 1)

        @block.scalar
        def _(act):
            for n in range(UT * BLK):
                m = n // BLK
                act.wait_ge(mm_ok, n + 1)
                if n >= 2:
                    act.wait_ge(y_ok, n - 1)
                step(act, nc.scalar.activation(gate[:, n % 2, :], banks[:, n % 2, :], ACT.Sigmoid, bias=bg[:, m:m + 1]),
                     gate_ok, n + 1)

        @block.vector
        def _(dve):
            per = NB // NCH
            for n in range(UT * BLK):
                m, q = n // BLK, n % BLK
                dve.wait_ge(gate_ok, n + 1)
                if q == 0 and m >= 2:
                    dve.wait_ge(sent[m % 2], 16 * (m // 2))
                step(dve, nc.vector.tensor_tensor(
                    y[:, m % 2].rearrange("p (c j) -> p j c", j=J)[:, q * per:(q + 1) * per, :],
                    g[:, m, q * NB:(q + 1) * NB].rearrange("p (j c) -> p j c", j=per),
                    gate[:, n % 2, :].rearrange("p (j c) -> p j c", j=per), ALU.mult), y_ok, n + 1)

CH0 = 6
B_T, C_T, K_T, Q_T = (0, 1), (2, 6), 3, 7
X_C, B_C, K_C = 0, XW, XW + NG * NS + NS
HG = HS // NG
GW = HG * HD
HP = HM // 2
DA = DV + 1
NT = (XW + VW) // P
LOADS = 5


def phase_mixers(nc, tok_cols, rows_dram, decay_dram, conv_dram, tok_dram, tokmaj_dram, ssd_skip, norm_gain, ident,
                 yt_dram):
    with ExitStack() as ctx:
        sb, ps, sem = scope(nc, ctx)
        ch = sb("m_ch", [P, 2, CT - CH0, P])
        tk = sb("m_tk", [P, 2, CTT * P])
        zo = sb("m_zo", [P, 2, XW + VW])
        va = sb("m_va", [P, 2, HM, DA])
        bc = sb("m_bc", [P, 2, NBC, P])
        decay = sb("m_decay", [P, HS, TT])
        decay_m = sb("m_decay_m", [P, HP, TT])
        skip, gain, ident_sb = sb("m_skip", [P, HS]), sb("m_gain", [P, XW // P]), sb("m_ident", [P, P])
        expo = sb("m_expo", [P, 2, NBC, P])
        xdt, xde, xskip = (sb("m_" + s, [P, HS, HD]) for s in ("xdt", "xde", "xskip"))
        ve = sb("m_ve", [P, HM, DA])
        off, y = sb("m_off", [P, HS, HD]), sb("m_y", [P, 2, XW + VW])
        sq = sb("m_sq", [P, GW])
        stat = sb("m_stat", [P, 4, NG])
        h_state, h_old = sb("m_h", [P, HS, HD]), sb("m_h_old", [P, HS, HD])
        c_state, c_old = sb("m_c", [P, HP, DA]), sb("m_c_old", [P, HP, DA])
        inter, num = sb("m_inter", [P, 2, HP, DA]), sb("m_num", [P, 2, HP, DA])
        den = sb("m_den", [P, 3, 2, HP])
        mask = sb("m_mask", [P, P])
        yt = sb("m_yt", [P, 2, NT, P])
        cb_bank, qk_banks, in_banks, off_banks, tr_bank = (
            ps("m_cb", [P, NB]), ps("m_qk", [P, 2, NB]), ps("m_in", [P, 2, NB]), ps("m_offb", [P, 2, NB]), ps("m_tr", [P, NB]))
        names = ("expo_ok", "mask_ok", "xde_ok", "xskip_ok", "ve_ok", "score_mm", "off_mm", "diag_mm", "state_mm",
                 "inter_mm", "pv_mm", "c_mm", "xdt_ok", "g_ok", "gm_ok", "off_read", "diag_read", "gated_ok", "h_ok",
                 "inter_read", "num_ok", "c_ok", "mean_ok", "ssq_ok", "rstd_ok", "y_ok")
        S = {n: sem("m_" + n) for n in names}
        (expo_ok, mask_ok, xde_ok, xskip_ok, ve_ok, score_mm, off_mm, diag_mm, state_mm, inter_mm, pv_mm, c_mm, xdt_ok,
         g_ok, gm_ok, off_read, diag_read, gated_ok, h_ok, inter_read, num_ok, c_ok, mean_ok, ssq_ok, rstd_ok,
         y_ok) = S.values()
        tr_ok, yt_ok = sem("m_tr_ok"), sem("m_yt_ok")
        const_in, in_, sent = sem("m_const_in"), (sem("m_in0"), sem("m_in1")), (sem("m_sent0"), sem("m_sent1"))
        dve_chain, act_chain, pool_chain, set_ok = (sem("m_" + s) for s in ("dve_chain", "act_chain", "pool_chain", "set_ok"))
        block = ctx.enter_context(nc.Block())

        def over(a, n):
            return a.unsqueeze(2).to_broadcast([P, a.shape[1], n])

        def col(c, k, first, n):
            return tok_cols[:, ds(c, 1), k, first:first + n].rearrange("p a n -> p (a n)")

        def col_eo(c, k):
            return col(c, k, FR, HM).rearrange("p (i e) -> p e i", e=2)

        def over_eo(a, n):
            return a.unsqueeze(3).to_broadcast([P, 2, HP, n])

        @block.sync
        def _(sp):
            for dst, src in ((skip[:], ssd_skip.partition_broadcast(P)), (gain[:], norm_gain), (ident_sb[:], ident),
                             (decay[:].rearrange("p h c -> p (h c)"),
                              decay_dram[0:HS].rearrange("h c -> (h c)").partition_broadcast(P))):
                sp.dma_start(dst, src).then_inc(const_in, 16)
            for e in range(2):
                sp.dma_start(decay_m[e * DK:(e + 1) * DK],
                             decay_dram[HS:NBC].rearrange("(i e) c -> e i c", e=2)[e].partition_broadcast(DK)
                             ).then_inc(const_in, 16)
            with sp.Fori(0, TT // 2) as i:
                for b in range(2):
                    c = i * 2 + b
                    sp.wait_ge(y_ok, c + 1)
                    tok = ds(c * P, P)
                    sp.dma_start(ch[:, b], conv_dram[CH0:CT, :, tok].rearrange("a p t -> p a t")).then_inc(in_[b], 16)
                    sp.dma_start(tk[:, b], tok_dram[tok, :]).then_inc(in_[b], 16)
                    sp.dma_start(bc[:, b].rearrange("p r t -> p (r t)"),
                                 rows_dram[ds(c, 1)].rearrange("a r t -> (a r t)").partition_broadcast(P)).then_inc(in_[b], 16)
                    sp.dma_start(va[:, b, :, 0:DV], tokmaj_dram[tok, XW + VW:].rearrange("t (h v) -> t h v", h=HM)
                                 ).then_inc(in_[b], 16)
                    sp.dma_start(zo[:, b], tokmaj_dram[tok, 0:XW + VW]).then_inc(in_[b], 16)

        @block.scalar
        def _(act):
            for s in (expo_ok, ssq_ok, rstd_ok):
                act.sem_inc(s, 2)
            chain = Chain(act, act_chain)
            rounds = TT // 2

            def chunk(c, b):
                act.wait_ge(mask_ok, c + 3)
                act.wait_ge(pv_mm, c + 1)
                for h in range(HS):
                    ins = nc.scalar.activation(expo[:, b, h, :], bc[:, b, h, :], ACT.Exp, bias=col(c, 1, h, 1))
                for h in range(HM):
                    at = HS + h % 2 * HP + h // 2
                    ins = nc.scalar.activation(expo[:, b, at, :], bc[:, b, HS + h, :], ACT.Exp, bias=col(c, 0, FR + h, 1))
                ins.then_inc(expo_ok, 1)
                act.wait_ge(gated_ok, c + 3)
                for g in range(NG):
                    ins = nc.scalar.activation(sq[:], y[:, b, g * GW:(g + 1) * GW], ACT.Square,
                                               accum_out=stat[:, 0, g:g + 1])
                    if g < NG - 1:
                        chain(ins)
                    else:
                        step(act, ins, ssq_ok, c + 3)
                act.wait_ge(mean_ok, c + 3)
                chain(nc.scalar.activation(stat[:, 2, :], stat[:, 1, :], ACT.Ln))
                step(act, nc.scalar.activation(stat[:, 3, :], stat[:, 2, :], ACT.Exp, scale=-0.5), rstd_ok, c + 3)

            def out(c, b):
                for n in range(NT // 4):
                    act.wait_ge(tr_ok, c * 3 + n + 1)
                    if n == 0:
                        act.wait_ge(sent[b], (c - b) * 8)
                    for a in range(4):
                        t = n * 4 + a
                        g = gain[:, t:t + 1] if t < XW // P else 1.0
                        ins = nc.scalar.activation(yt[:, b, t, :], tr_bank[:, a * P:(a + 1) * P], ACT.Copy, scale=g)
                    step(act, ins, yt_ok, c * 3 + n + 1)

            act.wait_ge(const_in, 16 * 6)
            with act.Fori(0, rounds) as i:
                chain.round(i, 4)
                for b in range(2):
                    c = i * 2 + b
                    act.wait_ge(in_[b], (i + 1) * 16 * LOADS)
                    chunk(c, b)
                    out(c, b)
            chain.end(rounds)

        @block.gpsimd
        def _(pool):
            for s in (mask_ok, xde_ok, xskip_ok, ve_ok):
                pool.sem_inc(s, 2)
            step(pool, nc.gpsimd.memset(mask[:], 0.0), pool_chain, 1)
            step(pool, nc.gpsimd.affine_select(out=mask[:], in_=mask[:], compare_op=ALU.is_ge, fill=-1e30, base=0,
                                               pattern=[[1, P]], channel_multiplier=-1), pool_chain, 2)
            step(pool, nc.gpsimd.memset(va[:, :, :, DV:DA], 1.0), set_ok, 1)
            pool.wait_ge(const_in, 16 * 6)
            with pool.Fori(0, TT // 2) as i:
                for b in range(2):
                    c = i * 2 + b
                    pool.wait_ge(in_[b], (i + 1) * 16 * LOADS)
                    step(pool, nc.gpsimd.tensor_tensor(bc[:, b], bc[:, b], mask[:].unsqueeze(1).to_broadcast([P, NBC, P]),
                                                       ALU.add), mask_ok, c + 3)
                    x = tk[:, b, X_C:X_C + XW].rearrange("p (h d) -> p h d", h=HS)
                    pool.wait_ge(state_mm, c + 2)
                    step(pool, nc.gpsimd.tensor_tensor(xde[:], x, over(col(c, 3, 0, HS), HD), ALU.mult), xde_ok, c + 3)
                    pool.wait_ge(gated_ok, c + 2)
                    step(pool, nc.gpsimd.tensor_tensor(xskip[:], x, over(skip[:], HD), ALU.mult), xskip_ok, c + 3)
                    pool.wait_ge(c_mm, c + 2)
                    step(pool, nc.gpsimd.tensor_tensor(ve[:], va[:, b], over(col(c, 2, FR, HM), DA), ALU.mult),
                         ve_ok, c + 3)
                    pool.wait_ge(yt_ok, c * 3 + 3)
                    pool.dma_start(yt_dram[UT:, :, ds(c * P, P)].rearrange("a p t -> p a t"), yt[:, b]
                                   ).then_inc(sent[b], 16)
            for b in range(2):
                pool.wait_ge(sent[b], 16 * TT // 2)

        @block.vector
        def _(dve):
            for s in (xdt_ok, g_ok, gm_ok, off_read, diag_read, gated_ok, inter_read, num_ok, mean_ok, y_ok):
                dve.sem_inc(s, 2)
            chain = Chain(dve, dve_chain)
            tt = nc.vector.tensor_tensor
            mul, add = ALU.mult, ALU.add
            chain(nc.vector.memset(h_state[:], 0.0))
            chain(nc.vector.memset(c_state[:], 0.0))
            dve.sem_inc(h_ok, 2)
            dve.sem_inc(c_ok, 2)
            dve.wait_ge(const_in, 16 * 6)
            dve.wait_ge(set_ok, 1)
            with dve.Fori(0, TT // 2) as i:
                chain.round(i, 2 * 9)
                for b in range(2):
                    c = i * 2 + b
                    dve.wait_ge(in_[b], (i + 1) * 16 * LOADS)
                    x = tk[:, b, X_C:X_C + XW].rearrange("p (h d) -> p h d", h=HS)
                    dve.wait_ge(diag_mm, c + 2)
                    step(dve, tt(xdt[:], x, over(col(c, 0, 0, HS), HD), mul), xdt_ok, c + 3)
                    dve.wait_ge(score_mm, c + 3)
                    dve.wait_ge(expo_ok, c + 3)
                    for g in range(NG):
                        e = expo[:, b, g * HG:(g + 1) * HG, :]
                        ins = tt(e, e, cb_bank[:, g * P:(g + 1) * P].unsqueeze(1).to_broadcast([P, HG, P]), mul)
                        if g < NG - 1:
                            chain(ins)
                        else:
                            step(dve, ins, g_ok, c + 3)
                    e = expo[:, b, HS:, :].rearrange("p (e i) t -> p e (i t)", e=2)
                    step(dve, nc.vector.scalar_tensor_tensor(e, e, DK ** -0.5, qk_banks[:, :, 0:HP * P], mul, mul),
                         gm_ok, c + 3)
                    dve.wait_ge(off_mm, c + 3)
                    o4 = off[:].rearrange("p (g h) d -> p g h d", g=NG)
                    f4 = col(c, 2, 0, HS).rearrange("p (g h) -> p g h", g=NG).unsqueeze(3).to_broadcast([P, NG, HG, HD])
                    step(dve, tt(o4, off_banks[:, :, 0:GW].rearrange("p g (h d) -> p g h d", h=HG), f4, mul),
                         off_read, c + 3)
                    dve.wait_ge(diag_mm, c + 3)
                    yg = y[:, b, 0:XW].rearrange("p (g m) -> p g m", g=NG)
                    dve.wait_ge(tr_ok, c * 3 - b * 3)
                    step(dve, tt(yg, in_banks[:, :, 0:GW], off[:].rearrange("p (g h) d -> p g (h d)", g=NG), add),
                         diag_read, c + 3)
                    dve.wait_ge(xskip_ok, c + 3)
                    chain(tt(y[:, b, 0:XW], y[:, b, 0:XW], xskip[:].rearrange("p h d -> p (h d)"), add))
                    step(dve, tt(y[:, b, 0:XW], y[:, b, 0:XW], zo[:, b, 0:XW], mul), gated_ok, c + 3)
                    dec = decay[:, :, ds(c, 1)].to_broadcast([P, HS, HD])
                    chain(tt(h_old[:], h_state[:], dec, mul))
                    dve.wait_ge(state_mm, c + 3)
                    step(dve, tt(h_state[:].rearrange("p (g h) d -> p g (h d)", g=NG),
                                 h_old[:].rearrange("p (g h) d -> p g (h d)", g=NG), qk_banks[:, :, 0:GW], add), h_ok, c + 3)
                    dve.wait_ge(ssq_ok, c + 3)
                    step(dve, nc.vector.tensor_scalar(stat[:, 1, :], stat[:, 0, :], 1.0 / GW, EPS, mul, add), mean_ok, c + 3)
                    dve.wait_ge(inter_mm, c + 3)
                    step(dve, tt(inter[:], off_banks[:, :, 0:HP * DA].rearrange("p e (i v) -> p e i v", i=HP),
                                 over_eo(col_eo(c, 1), DA), mul), inter_read, c + 3)
                    dve.wait_ge(pv_mm, c + 3)
                    step(dve, tt(num[:], in_banks[:, :, 0:HP * DA].rearrange("p e (i v) -> p e i v", i=HP), inter[:], add),
                         num_ok, c + 3)
                    d = num[:, :, :, DV]
                    chain(nc.vector.scalar_tensor_tensor(den[:, 0], d, -1.0, d, mul, ALU.max))
                    chain(tt(den[:, 1], den[:, 0], col_eo(c, 3), ALU.max))
                    chain(nc.vector.reciprocal(den[:, 2], den[:, 1]))
                    chain(tt(num[:], num[:], over_eo(den[:, 2], DA), mul))
                    chain(tt(y[:, b, XW:].rearrange("p (i e v) -> p e i v", e=2, i=HP), num[:, :, :, 0:DV],
                             zo[:, b, XW:].rearrange("p (i e v) -> p e i v", e=2, i=HP), mul))
                    chain(tt(c_old[:], c_state[:], decay_m[:, :, ds(c, 1)].to_broadcast([P, HP, DA]), mul))
                    dve.wait_ge(c_mm, c + 3)
                    step(dve, tt(c_state[:], c_old[:], cb_bank[:, 0:HP * DA].rearrange("p (i v) -> p i v", i=HP), add),
                         c_ok, c + 3)
                    dve.wait_ge(rstd_ok, c + 3)
                    step(dve, tt(yg, yg, over(stat[:, 3, :], GW), mul), y_ok, c + 3)
            chain.end(TT // 2)

        @block.tensor
        def _(pe):
            for s in (score_mm, off_mm, diag_mm, state_mm, inter_mm, pv_mm, c_mm):
                pe.sem_inc(s, 2)
            mm = nc.tensor.matmul
            pe.wait_ge(const_in, 16 * 6)

            def scores(c, b, seen):
                pe.wait_ge(in_[b], seen * 16 * LOADS)
                pe.wait_ge(c_ok, c + 2)
                for g in range(NG):
                    mm(cb_bank[:, g * P:(g + 1) * P], ch[:, b, B_T[g], :], ch[:, b, C_T[g], :], start=True, stop=True)
                pe.wait_ge(h_ok, c + 2)
                for i in range(HP):
                    for e in range(2):
                        rows = slice(e * DK, (e + 1) * DK)
                        last = mm(qk_banks[:, e, i * P:(i + 1) * P], ch[rows, b, K_T + i, :], ch[rows, b, Q_T + i, :],
                                  start=True, stop=True)
                last.then_inc(score_mm, 1)
                pe.wait_ge(inter_read, c + 2)
                for g in range(NG):
                    last = mm(off_banks[:, g, 0:GW], ch[:, b, C_T[g], :],
                              h_state[:].rearrange("p h d -> p (h d)")[:, g * GW:(g + 1) * GW], start=True, stop=True)
                last.then_inc(off_mm, 1)

            def rest(c, b):
                pe.wait_ge(num_ok, c + 2)
                pe.wait_ge(g_ok, c + 3)
                for h in range(HS):
                    last = mm(in_banks[:, h // HG, h % HG * HD:(h % HG + 1) * HD], expo[:, b, h, :], xdt[:, h, :],
                              start=True, stop=True)
                last.then_inc(diag_mm, 1)
                pe.wait_ge(gm_ok, c + 3)
                pe.wait_ge(xde_ok, c + 3)
                for g in range(NG):
                    last = mm(qk_banks[:, g, 0:GW], tk[:, b, B_C + g * NS:B_C + (g + 1) * NS],
                              xde[:].rearrange("p h d -> p (h d)")[:, g * GW:(g + 1) * GW], start=True, stop=True)
                last.then_inc(state_mm, 1)
                pe.wait_ge(off_read, c + 3)
                for i in range(HP):
                    for e in range(2):
                        rows = slice(e * DK, (e + 1) * DK)
                        last = mm(off_banks[:, e, i * DA:(i + 1) * DA], ch[rows, b, Q_T + i, :], c_state[rows, i, :],
                                  start=True, stop=True)
                last.then_inc(inter_mm, 1)
                pe.wait_ge(diag_read, c + 3)
                for h in range(HM):
                    e, i = h % 2, h // 2
                    last = mm(in_banks[:, e, i * DA:(i + 1) * DA], expo[:, b, HS + e * HP + i, :], va[:, b, h, :],
                              start=True, stop=True)
                last.then_inc(pv_mm, 1)
                pe.wait_ge(ve_ok, c + 3)
                for h in range(HM):
                    e, i = h % 2, h // 2
                    last = mm(cb_bank[e * DK:(e + 1) * DK, i * DA:(i + 1) * DA], tk[:, b, K_C + h * DK:K_C + (h + 1) * DK],
                              ve[:, h, :], start=True, stop=True)
                last.then_inc(c_mm, 1)

            def transposes(c, b):
                pe.wait_ge(y_ok, c + 3)
                for n in range(NT // 4):
                    pe.wait_ge(yt_ok, c * 3 + n)
                    for a in range(4):
                        t = n * 4 + a
                        last = nc.tensor.transpose(tr_bank[:, a * P:(a + 1) * P], y[:, b, t * P:(t + 1) * P], ident_sb[:])
                    last.then_inc(tr_ok, 1)

            scores(0, 0, 1)
            rest(0, 0)
            with pe.Fori(0, TT // 2 - 1) as i:
                for b in range(2):
                    c = i * 2 + b + 1
                    scores(c, 1 - b, i + 1 + b)
                    transposes(c - 1, b)
                    rest(c, 1 - b)
            scores(TT - 1, 1, TT // 2)
            transposes(TT - 2, 0)
            rest(TT - 1, 1)
            transposes(TT - 1, 1)

KM = DMIX // P


def phase_out(nc, x, w_out, gain_mix, gain_ffn, ident, yt_dram, x1_dram, h2_dram):
    x_tiles = x[0].rearrange("(n p) d -> n p d", p=P)
    with ExitStack() as ctx:
        sb, ps, sem = scope(nc, ctx)
        w_hi, w_lo = sb("o_w_hi", [P, KM, D], F32R), sb("o_w_lo", [P, KM, D], F32R)
        raw = sb("o_raw", [P, 2, D])
        y_hi, y_lo = sb("o_y_hi", [P, 2, KM, P], F32R), sb("o_y_lo", [P, 2, KM, P], F32R)
        xt, x1 = sb("o_x", [P, D]), sb("o_x1", [P, D])
        work, ht = sb("o_work", [P, D]), sb("o_ht", [P, KD, P])
        gain_row, gain_col = sb("o_gain_row", [P, D]), sb("o_gain_col", [P, KD])
        ident_sb, stat = sb("o_ident", [P, P]), sb("o_stat", [P, 8])
        banks, tr_banks = ps("o_banks", [P, 2, 2, NB]), ps("o_tr", [P, 2, NB])
        const_in, wraw_in = sem("o_const_in"), (sem("o_wraw_in0"), sem("o_wraw_in1"))
        whi_ok, wlo_ok, y_in, x_in, x1_sent, h_sent, act_chain, dve_chain = (
            sem("o_" + s) for s in ("whi_ok", "wlo_ok", "y_in", "x_in", "x1_sent", "h_sent", "act_chain", "dve_chain"))
        yhi_ok, ylo_ok, mm_ok, ssq_ok, mean_ok, rstd_ok, x1_ok, ssq2_ok, mean2_ok, rstd2_ok, xn_ok, tr_ok, ht_ok, add_ok = (
            sem("o_" + s) for s in ("yhi_ok", "ylo_ok", "mm_ok", "ssq_ok", "mean_ok", "rstd_ok", "x1_ok", "ssq2_ok",
                                    "mean2_ok", "rstd2_ok", "xn_ok", "tr_ok", "ht_ok", "add_ok"))
        block = ctx.enter_context(nc.Block())
        y_raw = raw[:].rearrange("p a (k t) -> p (a k) t", t=P)

        @block.sync
        def _(sp):
            for dst, src in ((gain_row[:], gain_mix.partition_broadcast(P)), (gain_col[:], gain_ffn), (ident_sb[:], ident)):
                sp.dma_start(dst, src).then_inc(const_in, 16)
            with sp.Fori(0, KM // 2) as i:
                for b in range(2):
                    sp.wait_ge(wlo_ok, i * 2)
                    sp.dma_start(raw[:, b, :], w_out[ds((i * 2 + b) * P, P), :]).then_inc(wraw_in[b], 16)
            sp.wait_ge(wlo_ok, KM)
            with sp.Fori(0, TT) as n:
                sp.wait_ge(ylo_ok, n + 2)
                sp.dma_start(y_raw, yt_dram[:, :, ds(n * P, P)].rearrange("a p t -> p a t")).then_inc(y_in, 16)
                sp.wait_ge(add_ok, n + 2)
                sp.dma_start(xt[:], x_tiles[ds(n, 1)].rearrange("a p d -> (a p) d")).then_inc(x_in, 16)

        @block.gpsimd
        def _(pool):
            with pool.Fori(0, TT) as n:
                pool.wait_ge(x1_ok, n + 3)
                pool.dma_start(x1_dram[ds(n * P, P), :], x1[:]).then_inc(x1_sent, 16)
                pool.wait_ge(ht_ok, n + 3)
                pool.dma_start(h2_dram[:, :, ds(n * P, P)].rearrange("a p t -> p a t"), ht[:]).then_inc(h_sent, 16)
            pool.wait_ge(x1_sent, 16 * TT)
            pool.wait_ge(h_sent, 16 * TT)

        @block.scalar
        def _(act):
            for s in (yhi_ok, ssq_ok, rstd_ok, ssq2_ok, rstd2_ok, ht_ok):
                act.sem_inc(s, 2)
            chain = Chain(act, act_chain)
            act.wait_ge(const_in, 48)
            with act.Fori(0, KM // 2) as i:
                for b in range(2):
                    k = i * 2 + b
                    act.wait_ge(wraw_in[b], i * 16 + 16)
                    step(act, nc.scalar.activation(w_hi[:, ds(k, 1), :].rearrange("p a m -> p (a m)"), raw[:, b, :],
                                                   ACT.Copy), whi_ok, k + 1)

            def upper(n, b, before):
                act.wait_ge(y_in, n * 16 + 16)
                act.wait_ge(mm_ok, before)
                step(act, nc.scalar.activation(y_hi[:, b], y_raw, ACT.Copy), yhi_ok, n + 3)

            def norm(src, dst, ok, mean, rstd, n):
                step(act, nc.scalar.activation(work[:], src, ACT.Square, accum_out=stat[:, dst:dst + 1]), ok, n + 3)
                act.wait_ge(mean, n + 3)
                chain(nc.scalar.activation(stat[:, dst + 2:dst + 3], stat[:, dst + 1:dst + 2], ACT.Ln))
                step(act, nc.scalar.activation(stat[:, dst + 2:dst + 3], stat[:, dst + 2:dst + 3], ACT.Exp, scale=-0.5),
                     rstd, n + 3)

            def tile(n, b):
                act.wait_ge(mm_ok, n + 3)
                act.wait_ge(tr_ok, n + 2)
                norm(banks[:, b].rearrange("p a m -> p (a m)"), 0, ssq_ok, mean_ok, rstd_ok, n)
                act.wait_ge(x1_ok, n + 3)
                norm(x1[:], 3, ssq2_ok, mean2_ok, rstd2_ok, n)
                act.wait_ge(tr_ok, n + 3)
                act.wait_ge(h_sent, n * 16)
                for k in range(KD):
                    ins = nc.scalar.activation(ht[:, k, :], tr_banks[:, k // 4, k % 4 * P:(k % 4 + 1) * P], ACT.Copy,
                                               scale=gain_col[:, k:k + 1])
                step(act, ins, ht_ok, n + 3)

            act.wait_ge(wlo_ok, KM)
            upper(0, 0, 0)
            with act.Fori(0, TT // 2 - 1) as i:
                chain.round(i, 4)
                for b in range(2):
                    n = i * 2 + b
                    upper(n + 1, 1 - b, n + 2)
                    tile(n, b)
            chain.end(TT // 2 - 1)
            upper(TT - 1, 1, TT)
            tile(TT - 2, 0)
            tile(TT - 1, 1)

        @block.vector
        def _(dve):
            for s in (ylo_ok, mean_ok, x1_ok, mean2_ok, xn_ok, add_ok):
                dve.sem_inc(s, 2)
            chain = Chain(dve, dve_chain)
            tt, ts = nc.vector.tensor_tensor, nc.vector.tensor_scalar
            dve.wait_ge(const_in, 48)
            with dve.Fori(0, KM // 2) as i:
                for b in range(2):
                    k = i * 2 + b
                    dve.wait_ge(whi_ok, k + 1)
                    step(dve, tt(w_lo[:, ds(k, 1), :].rearrange("p a m -> p (a m)"), raw[:, b, :],
                                 w_hi[:, ds(k, 1), :].rearrange("p a m -> p (a m)").bitcast(F32), ALU.subtract), wlo_ok, k + 1)

            def lower(n, b):
                dve.wait_ge(yhi_ok, n + 3)
                step(dve, tt(y_lo[:, b], y_raw, y_hi[:, b].bitcast(F32), ALU.subtract), ylo_ok, n + 3)

            def tile(n, b):
                dve.wait_ge(ssq_ok, n + 3)
                step(dve, ts(stat[:, 1:2], stat[:, 0:1], 1.0 / D, EPS, ALU.mult, ALU.add), mean_ok, n + 3)
                dve.wait_ge(rstd_ok, n + 3)
                chain(nc.vector.scalar_tensor_tensor(work[:], banks[:, b].rearrange("p a m -> p (a m)"), stat[:, 2:3],
                                                     gain_row[:], ALU.mult, ALU.mult))
                dve.wait_ge(x_in, n * 16 + 16)
                dve.wait_ge(x1_sent, n * 16)
                step(dve, tt(x1[:], work[:], xt[:], ALU.add), x1_ok, n + 3)
                dve.sem_inc(add_ok, 1)
                dve.wait_ge(ssq2_ok, n + 3)
                step(dve, ts(stat[:, 4:5], stat[:, 3:4], 1.0 / D, EPS, ALU.mult, ALU.add), mean2_ok, n + 3)
                dve.wait_ge(rstd2_ok, n + 3)
                step(dve, ts(work[:], x1[:], stat[:, 5:6], None, ALU.mult), xn_ok, n + 3)

            lower(0, 0)
            with dve.Fori(0, TT // 2 - 1) as i:
                chain.round(i, 2)
                for b in range(2):
                    n = i * 2 + b
                    lower(n + 1, 1 - b)
                    tile(n, b)
            chain.end(TT // 2 - 1)
            lower(TT - 1, 1)
            tile(TT - 2, 0)
            tile(TT - 1, 1)

        @block.tensor
        def _(pe):
            pe.sem_inc(mm_ok, 2)
            pe.sem_inc(tr_ok, 2)
            pe.wait_ge(const_in, 48)
            pe.wait_ge(wlo_ok, KM)

            def products(n, b):
                pe.wait_ge(ylo_ok, n + 3)
                pe.wait_ge(x1_ok, n + 1)
                for half in range(2):
                    cols = slice(half * NB, (half + 1) * NB)
                    for k in range(KM):
                        for j, (y, w) in enumerate(((y_hi, w_hi), (y_lo, w_hi), (y_hi, w_lo))):
                            last = nc.tensor.matmul(banks[:, b, half, :], y[:, b, k, :], w[:, k, cols],
                                                    start=k == 0 and j == 0, stop=k == KM - 1 and j == 2)
                last.then_inc(mm_ok, 1)

            def transposes(n):
                pe.wait_ge(xn_ok, n + 3)
                pe.wait_ge(ht_ok, n + 2)
                for k in range(KD):
                    last = nc.tensor.transpose(tr_banks[:, k // 4, k % 4 * P:(k % 4 + 1) * P],
                                               work[:, k * P:(k + 1) * P], ident_sb[:])
                last.then_inc(tr_ok, 1)

            products(0, 0)
            with pe.Fori(0, TT // 2 - 1) as i:
                for b in range(2):
                    products(i * 2 + b + 1, 1 - b)
                    transposes(i * 2 + b)
            products(TT - 1, 1)
            transposes(TT - 2)
            transposes(TT - 1)


def phase_ffn_up(nc, w_gu, h2_dram, a_dram):
    with ExitStack() as ctx:
        sb, ps, sem = scope(nc, ctx)
        h_hi, h_lo = sb("f_h_hi", [P, KD, T], F32R), sb("f_h_lo", [P, KD, T], F32R)
        w_raw = sb("f_w_raw", [P, 2, KD, P])
        w_hi, w_lo = sb("f_w_hi", [P, 2, 2, KD, P], F32R), sb("f_w_lo", [P, 2, 2, KD, P], F32R)
        gate, a = sb("f_gate", [P, 2, NB]), sb("f_a", [P, 2, T])
        banks = ps("f_banks", [P, 2, 2, NB])
        h_in, w_in = (sem("f_h_in0"), sem("f_h_in1")), sem("f_w_in")
        sent = (sem("f_sent0"), sem("f_sent1"))
        hhi_ok, hlo_ok = sem("f_hhi_ok"), sem("f_hlo_ok")
        whi_ok, wlo_ok, mm_ok, gate_ok, a_ok = (sem("f_" + s) for s in ("whi_ok", "wlo_ok", "mm_ok", "gate_ok", "a_ok"))
        block = ctx.enter_context(nc.Block())

        @block.sync
        def _(sp):
            with sp.Fori(0, KD // 2) as i:
                for b in range(2):
                    sp.wait_ge(hlo_ok, i * 2)
                    sp.dma_start(a[:, b, :], h2_dram[ds(i * 2 + b, 1)].rearrange("a p t -> (a p) t")).then_inc(h_in[b], 16)
            with sp.Fori(0, FT) as n:
                sp.wait_ge(wlo_ok, n + 2)
                sp.dma_start(w_raw[:].rearrange("p g k m -> p (g k m)"), w_gu[ds(n, 1)].rearrange("a p m -> (a p) m")
                             ).then_inc(w_in, 16)

        @block.gpsimd
        def _(pool):
            with pool.Fori(0, FT // 2) as i:
                for b in range(2):
                    n = i * 2 + b
                    pool.wait_ge(a_ok, n * BLK + BLK + 2)
                    pool.dma_start(a_dram[ds(n, 1)].rearrange("a p t -> (a p) t"), a[:, b, :]).then_inc(sent[b], 16)
            for b in range(2):
                pool.wait_ge(sent[b], 16 * FT // 2)

        @block.scalar
        def _(act):
            act.sem_inc(whi_ok, 2)
            act.sem_inc(gate_ok, 2)
            with act.Fori(0, KD // 2) as i:
                for b in range(2):
                    k = i * 2 + b
                    act.wait_ge(h_in[b], i * 16 + 16)
                    step(act, nc.scalar.activation(h_hi[:, ds(k, 1), :].rearrange("p a t -> p (a t)"), a[:, b, :],
                                                   ACT.Copy), hhi_ok, k + 1)

            def upper(n, b, first=False):
                act.wait_ge(w_in, n * 16 + 16)
                if not first:
                    act.wait_ge(mm_ok, n * BLK - BLK + 2)
                step(act, nc.scalar.activation(w_hi[:, b], w_raw[:], ACT.Copy), whi_ok, n + 3)

            def tile(n, b):
                for q in range(BLK):
                    m = n * BLK + q
                    act.wait_ge(mm_ok, m + 3)
                    act.wait_ge(a_ok, m + 1)
                    step(act, nc.scalar.activation(gate[:, q % 2, :], banks[:, q % 2, 0, :], ACT.Silu), gate_ok, m + 3)

            upper(0, 0, True)
            with act.Fori(0, FT // 2 - 1) as i:
                for b in range(2):
                    upper(i * 2 + b + 1, 1 - b)
                    tile(i * 2 + b, b)
            upper(FT - 1, 1)
            tile(FT - 2, 0)
            tile(FT - 1, 1)

        @block.vector
        def _(dve):
            dve.sem_inc(a_ok, 2)
            with dve.Fori(0, KD // 2) as i:
                for b in range(2):
                    k = i * 2 + b
                    dve.wait_ge(hhi_ok, k + 1)
                    step(dve, nc.vector.tensor_tensor(
                        h_lo[:, ds(k, 1), :].rearrange("p a t -> p (a t)"), a[:, b, :],
                        h_hi[:, ds(k, 1), :].rearrange("p a t -> p (a t)").bitcast(F32), ALU.subtract), hlo_ok, k + 1)
            dve.sem_inc(wlo_ok, 2)

            def lower(n, b):
                dve.wait_ge(whi_ok, n + 3)
                step(dve, nc.vector.tensor_tensor(w_lo[:, b], w_raw[:], w_hi[:, b].bitcast(F32), ALU.subtract),
                     wlo_ok, n + 3)

            def tile(n, b):
                for q in range(BLK):
                    m = n * BLK + q
                    dve.wait_ge(gate_ok, m + 3)
                    if q == 0:
                        dve.wait_ge(sent[b], (n - b) * 8)
                    step(dve, nc.vector.tensor_tensor(a[:, b, q * NB:(q + 1) * NB], gate[:, q % 2, :],
                                                      banks[:, q % 2, 1, :], ALU.mult), a_ok, m + 3)

            lower(0, 0)
            with dve.Fori(0, FT // 2 - 1) as i:
                for b in range(2):
                    lower(i * 2 + b + 1, 1 - b)
                    tile(i * 2 + b, b)
            lower(FT - 1, 1)
            tile(FT - 2, 0)
            tile(FT - 1, 1)

        @block.tensor
        def _(pe):
            pe.sem_inc(mm_ok, 2)
            pe.wait_ge(hlo_ok, KD)
            with pe.Fori(0, FT // 2) as i:
                for b in range(2):
                    n = i * 2 + b
                    pe.wait_ge(wlo_ok, n + 3)
                    for q in range(BLK):
                        pe.wait_ge(a_ok, n * BLK + q + 1)
                        for g in range(2):
                            for k in range(KD):
                                for j, (w, h) in enumerate(((w_hi, h_hi), (w_hi, h_lo), (w_lo, h_hi))):
                                    last = nc.tensor.matmul(banks[:, q % 2, g, :], w[:, b, g, k, :],
                                                            h[:, k, q * NB:(q + 1) * NB],
                                                            start=k == 0 and j == 0, stop=k == KD - 1 and j == 2)
                        last.then_inc(mm_ok, 1)


def phase_ffn_down(nc, w_down, gain_post, a_dram, x1_dram, out):
    out_tiles = out[0].rearrange("(n p) d -> n p d", p=P)
    with ExitStack() as ctx:
        sb, ps, sem = scope(nc, ctx)
        w_raw = sb("d_w_raw", [P, 2, NB])
        w_hi, w_lo = sb("d_w_hi", [P, FT, NB], F32R), sb("d_w_lo", [P, FT, NB], F32R)
        a_raw = sb("d_a_raw", [P, FT, P])
        a_hi, a_lo = sb("d_a_hi", [P, 2, FT, P], F32R), sb("d_a_lo", [P, 2, FT, P], F32R)
        first = sb("d_first", [P, TT, NB])
        x1, res, work = sb("d_x1", [P, D]), sb("d_res", [P, D]), sb("d_work", [P, D])
        gain_row, ssq, stat = sb("d_gain", [P, D]), sb("d_ssq", [P, TT, 1]), sb("d_stat", [P, 4])
        banks = ps("d_banks", [P, 2, NB])
        const_in, w_in = sem("d_const_in"), (sem("d_w_in0"), sem("d_w_in1"))
        whi_ok, wlo_ok, a_in, x_in, sent, act_chain, dve_chain = (
            sem("d_" + s) for s in ("whi_ok", "wlo_ok", "a_in", "x_in", "sent", "act_chain", "dve_chain"))
        ahi_ok, alo_ok, mm_ok, copy_ok, ssq2_ok, mean_ok, rstd_ok, res_ok = (
            sem("d_" + s) for s in ("ahi_ok", "alo_ok", "mm_ok", "copy_ok", "ssq2_ok", "mean_ok", "rstd_ok", "res_ok"))
        block = ctx.enter_context(nc.Block())

        @block.sync
        def _(sp):
            sp.dma_start(gain_row[:], gain_post.partition_broadcast(P)).then_inc(const_in, 16)
            for half in range(2):
                with sp.Fori(0, FT // 2) as i:
                    for b in range(2):
                        sp.wait_ge(wlo_ok, i * 2 + half * FT)
                        sp.dma_start(w_raw[:, b, :], w_down[ds((i * 2 + b) * P, P), half * NB:(half + 1) * NB]
                                     ).then_inc(w_in[b], 16)
                with sp.Fori(0, TT) as t:
                    n = t + half * TT
                    sp.wait_ge(alo_ok, n + 2)
                    sp.dma_start(a_raw[:], a_dram[:, :, ds(t * P, P)].rearrange("a p t -> p a t")).then_inc(a_in, 16)
                    if half:
                        sp.wait_ge(res_ok, t + 2)
                        sp.dma_start(x1[:], x1_dram[ds(t * P, P), :]).then_inc(x_in, 16)

        @block.gpsimd
        def _(pool):
            with pool.Fori(0, TT) as t:
                pool.wait_ge(res_ok, t + 3)
                pool.dma_start(out_tiles[ds(t, 1)].rearrange("a p d -> (a p) d"), res[:]).then_inc(sent, 16)
            pool.wait_ge(sent, 16 * TT)

        def weights(eng, half, upper):
            with eng.Fori(0, FT // 2) as i:
                for b in range(2):
                    k = i * 2 + b
                    if upper:
                        eng.wait_ge(w_in[b], (i + half * FT // 2) * 16 + 16)
                        step(eng, nc.scalar.activation(w_hi[:, ds(k, 1), :].rearrange("p a m -> p (a m)"), w_raw[:, b, :],
                                                       ACT.Copy), whi_ok, k + half * FT + 1)
                    else:
                        eng.wait_ge(whi_ok, k + half * FT + 1)
                        step(eng, nc.vector.tensor_tensor(
                            w_lo[:, ds(k, 1), :].rearrange("p a m -> p (a m)"), w_raw[:, b, :],
                            w_hi[:, ds(k, 1), :].rearrange("p a m -> p (a m)").bitcast(F32), ALU.subtract),
                            wlo_ok, k + half * FT + 1)

        @block.scalar
        def _(act):
            for s in (ahi_ok, copy_ok, ssq2_ok, rstd_ok):
                act.sem_inc(s, 2)
            chain = Chain(act, act_chain)

            def upper(n, b):
                act.wait_ge(a_in, n * 16 + 16)
                act.wait_ge(mm_ok, n + 1)
                step(act, nc.scalar.activation(a_hi[:, b], a_raw[:], ACT.Copy), ahi_ok, n + 3)

            def tile(n, t, b, half):
                act.wait_ge(mm_ok, n + 3)
                if half == 0:
                    chain(nc.scalar.activation(first[:, ds(t, 1), :].rearrange("p a m -> p (a m)"), banks[:, b, :], ACT.Copy))
                    step(act, nc.scalar.activation(work[:, 0:NB], banks[:, b, :], ACT.Square,
                                                   accum_out=ssq[:, ds(t, 1), :].rearrange("p a m -> p (a m)")),
                         copy_ok, n + 3)
                else:
                    step(act, nc.scalar.activation(work[:, 0:NB], banks[:, b, :], ACT.Square, accum_out=stat[:, 0:1]),
                         ssq2_ok, t + 3)
                    act.wait_ge(mean_ok, t + 3)
                    chain(nc.scalar.activation(stat[:, 2:3], stat[:, 1:2], ACT.Ln))
                    step(act, nc.scalar.activation(stat[:, 3:4], stat[:, 2:3], ACT.Exp, scale=-0.5), rstd_ok, t + 3)
                    act.wait_ge(res_ok, t + 3)

            for half in range(2):
                if half:
                    act.wait_ge(mm_ok, TT + 2)
                weights(act, half, True)
                upper(half * TT, 0)
                with act.Fori(0, TT // 2 - 1) as i:
                    chain.round(i, 2)
                    for b in range(2):
                        t = i * 2 + b
                        upper(t + half * TT + 1, 1 - b)
                        tile(t + half * TT, t, b, half)
                chain.end(TT // 2 - 1)
                upper(half * TT + TT - 1, 1)
                tile(half * TT + TT - 2, TT - 2, 0, half)
                tile(half * TT + TT - 1, TT - 1, 1, half)

        @block.vector
        def _(dve):
            for s in (alo_ok, mean_ok, res_ok):
                dve.sem_inc(s, 2)
            chain = Chain(dve, dve_chain)
            dve.wait_ge(const_in, 16)

            def lower(n, b):
                dve.wait_ge(ahi_ok, n + 3)
                step(dve, nc.vector.tensor_tensor(a_lo[:, b], a_raw[:], a_hi[:, b].bitcast(F32), ALU.subtract),
                     alo_ok, n + 3)

            def tile(t, b):
                dve.wait_ge(ssq2_ok, t + 3)
                chain(nc.vector.tensor_tensor(stat[:, 1:2], stat[:, 0:1], ssq[:, ds(t, 1), :].rearrange("p a m -> p (a m)"),
                                              ALU.add))
                step(dve, nc.vector.tensor_scalar(stat[:, 1:2], stat[:, 1:2], 1.0 / D, EPS, ALU.mult, ALU.add),
                     mean_ok, t + 3)
                dve.wait_ge(rstd_ok, t + 3)
                for half, f in enumerate((first[:, ds(t, 1), :].rearrange("p a m -> p (a m)"), banks[:, b, :])):
                    cols = slice(half * NB, (half + 1) * NB)
                    chain(nc.vector.scalar_tensor_tensor(work[:, cols], f, stat[:, 3:4], gain_row[:, cols],
                                                         ALU.mult, ALU.mult))
                dve.wait_ge(x_in, t * 16 + 16)
                dve.wait_ge(sent, t * 16)
                step(dve, nc.vector.tensor_tensor(res[:], work[:], x1[:], ALU.add), res_ok, t + 3)

            for half in range(2):
                weights(dve, half, False)
                lower(half * TT, 0)
                with dve.Fori(0, TT // 2 - 1) as i:
                    if half:
                        chain.round(i, 6)
                    for b in range(2):
                        lower(i * 2 + b + half * TT + 1, 1 - b)
                        if half:
                            tile(i * 2 + b, b)
                if half:
                    chain.end(TT // 2 - 1)
                lower(half * TT + TT - 1, 1)
                if half:
                    tile(TT - 2, 0)
                    tile(TT - 1, 1)

        @block.tensor
        def _(pe):
            pe.sem_inc(mm_ok, 2)
            for half in range(2):
                pe.wait_ge(wlo_ok, (half + 1) * FT)
                with pe.Fori(0, TT // 2) as i:
                    for b in range(2):
                        t = i * 2 + b
                        n = t + half * TT
                        pe.wait_ge(alo_ok, n + 3)
                        if half == 0:
                            pe.wait_ge(copy_ok, n + 1)
                        else:
                            pe.wait_ge(copy_ok, TT + 2)
                            pe.wait_ge(res_ok, t + 1)
                        for k in range(FT):
                            for j, (a, w) in enumerate(((a_hi, w_hi), (a_lo, w_hi), (a_hi, w_lo))):
                                last = nc.tensor.matmul(banks[:, b, :], a[:, b, k, :], w[:, k, :],
                                                        start=k == 0 and j == 0, stop=k == FT - 1 and j == 2)
                        last.then_inc(mm_ok, 1)

def layer(nc, x, w_chan, w_tok, conv_w, conv_b, gate_bias, gate_sign, gate_log, ident, gain_pre,
          lam_re, lam_im, log_step, s5_b_re, s5_b_im, s5_c_re, s5_c_im, s5_skip, w_glu, b_glu,
          ssd_skip, norm_gain, w_out, gain_mix, gain_ffn, w_gu, w_down, gain_post, out):
    def dram(name, shape):
        return nc.dram_tensor(name, shape, F32).ap()

    u_dram, g_dram = dram("u", [J, S5W, NCH]), dram("g", [J, S5W, NCH])
    kern_dram = dram("kern", [S5G, S5H, PADK])
    conv_dram, tok_dram = dram("conv", [CT, P, T]), dram("tok", [T, CTT * P])
    tokmaj_dram = dram("tokmaj", [T, XW + 2 * VW])
    rows_dram, decay_dram = dram("rows", [TT, NBC, P]), dram("decay", [NBC, TT])
    yt_dram = dram("yt", [DMIX // P, P, T])
    x1_dram, h2_dram, a_dram = dram("x1", [T, D]), dram("h2", [KD, P, T]), dram("a", [FT, P, T])

    with ExitStack() as gates:
        gate_rows = gates.enter_context(nc.sbuf_tensor("gate_rows", [P, T], F32))
        with ExitStack() as ctx:
            sb, _, _ = scope(nc, ctx)
            h_hi, h_lo = sb("h_hi", [P, KD, T], F32R), sb("h_lo", [P, KD, T], F32R)
            phase_norm(nc, x, gain_pre, ident, h_hi, h_lo)
            phase_channels(nc, w_chan, conv_w, conv_b, ident, h_hi, h_lo, u_dram, conv_dram, tok_dram, gate_rows)
            phase_tokens(nc, w_tok, h_hi, h_lo, tokmaj_dram)
        tok_cols = gates.enter_context(nc.sbuf_tensor("tok_cols", [P, TT, 4, ROWS], F32))
        phase_gates(nc, gate_rows, gate_bias, gate_sign, gate_log, ident, tok_cols, rows_dram, decay_dram)
        with ExitStack() as ctx:
            sb, _, _ = scope(nc, ctx)
            table, rho = sb("table", [P, Q, 2, NCH]), sb("rho", [P, Q])
            ca, wt = sb("ca", [P, Q, 2, (J + 1) * S5H]), sb("wt", [P, Q, 2, P])
            phase_s5_setup(nc, lam_re, lam_im, log_step, s5_b_re, s5_b_im, s5_c_re, s5_c_im, s5_skip, ident,
                           table, rho, ca, wt, kern_dram)
            phase_s5(nc, table, rho, ca, wt, kern_dram, u_dram, g_dram)
        phase_s5_glu(nc, w_glu, b_glu, g_dram, yt_dram)
        phase_mixers(nc, tok_cols, rows_dram, decay_dram, conv_dram, tok_dram, tokmaj_dram, ssd_skip, norm_gain,
                     ident, yt_dram)
    phase_out(nc, x, w_out, gain_mix, gain_ffn, ident, yt_dram, x1_dram, h2_dram)
    phase_ffn_up(nc, w_gu, h2_dram, a_dram)
    phase_ffn_down(nc, w_down, gain_post, a_dram, x1_dram, out)


def laid_out(I):
    def by_rows(v):
        return v.reshape(-1, P).T

    def by_tiles(w, width):
        k, n = w.shape[0] // P, w.shape[1] // width
        return w.reshape(k, P, n, width).transpose(2, 1, 0, 3).reshape(n, P, k * width)

    def padded(shape, **parts):
        a = np.zeros(shape, np.float32)
        for part, at in ((parts["dt"], 0), (parts["f"], FR), (parts["i"], IR)):
            a[..., at:at + part.shape[-1]] = part
        return a

    def lanes(a):
        a = np.moveaxis(a.reshape((Q, 2) + a.shape[1:]), 0, 2)
        return a.reshape((P,) + a.shape[2:])

    p = {name: v[0] for name, v in I.items()}
    edges = np.cumsum([0, S5W, XW, XW + 2 * NG * NS, HS, 2 * HM * DK, VW, HM, HM, VW])
    u, z, xbc, dt, qk, v, i_, f_, o_ = (p["w_in"][:, a:b] for a, b in zip(edges, edges[1:]))

    def conv_order(ssd, mlstm):
        split, half = XW + (NG + 1) * NS, HM * DK
        return np.concatenate([ssd[..., :split], mlstm[..., half:], ssd[..., split:], mlstm[..., :half]], -1)

    gates = padded((D, P), dt=dt, f=f_, i=i_)
    return {
        "x": I["x"],
        "w_chan": by_tiles(np.concatenate([u, conv_order(xbc, qk), gates], 1), P),
        "w_tok": by_tiles(np.concatenate([z, o_, v], 1), TOKC),
        "conv_w": conv_order(p["ssd_conv_w"], p["mlstm_conv_w"]).T.reshape(CT, P, 4).transpose(1, 0, 2),
        "conv_b": by_rows(conv_order(p["ssd_conv_b"], p["mlstm_conv_b"])),
        "gate_bias": padded((P,), dt=p["ssd_dt_bias"], f=p["mlstm_b_f"], i=p["mlstm_b_i"])[:, None],
        "gate_sign": np.repeat(np.array([1, -1], np.float32), FR)[:, None],
        "gate_log": np.concatenate([p["ssd_a_log"], np.zeros(ROWS - HS, np.float32)])[:, None],
        "ident": np.eye(P, dtype=np.float32),
        "gain_pre": by_rows(p["norm_pre_mix"]),
        "lam_re": lanes(p["s5_lambda_re"]),
        "lam_im": lanes(p["s5_lambda_im"]),
        "log_step": lanes(np.repeat(p["s5_log_step"][:, None], S5P, 1)),
        "s5_b_re": lanes(p["s5_b_re"]),
        "s5_b_im": lanes(p["s5_b_im"]),
        "s5_c_re": lanes(p["s5_c_re"].transpose(0, 2, 1)),
        "s5_c_im": lanes(p["s5_c_im"].transpose(0, 2, 1)),
        "s5_skip": p["s5_d"].T,
        "w_glu": p["s5_w_glu"].reshape(UT, P, S5W).transpose(1, 0, 2),
        "b_glu": by_rows(p["s5_b_glu"]),
        "ssd_skip": p["ssd_d"],
        "norm_gain": by_rows(p["ssd_norm"]),
        "w_out": p["w_out"],
        "gain_mix": p["norm_post_mix"],
        "gain_ffn": by_rows(p["norm_pre_ffn"]),
        "w_gu": np.concatenate([by_tiles(p["w_gate"], P), by_tiles(p["w_up"], P)], 2),
        "w_down": p["w_down"],
        "gain_post": p["norm_post_ffn"],
    }


def kernel(**inputs):
    import concourse.bacc as _bacc
    from concourse.bass_utils import run_bass_kernel_spmd as _run

    arrays = {name: np.ascontiguousarray(a) for name, a in laid_out(
        {name: np.asarray(a) for name, a in inputs.items()}).items()}
    nc = _bacc.Bacc("TRN2", target_bir_lowering=False, num_devices=1)
    args = {name: nc.dram_tensor("in_" + name, a.shape, F32, kind="ExternalInput").ap() for name, a in arrays.items()}
    out = nc.dram_tensor("out_x", [1, T, D], F32, kind="ExternalOutput").ap()
    layer(nc, out=out, **args)
    r = _run(nc, [{"in_" + name: a for name, a in arrays.items()}], core_ids=[0])
    return r.results[0]["out_x"]
```

```python
import math
from contextlib import ExitStack

import concourse.bass as bass
import numpy as np
from concourse import mybir

F32 = mybir.dt.float32
F32R = mybir.dt.float32r
ALU = mybir.AluOpType
ACT = mybir.ActivationFunctionType
ds = bass.ds

P = 128
T, D = 2048, 1024
KD = D // P
TT = T // P
NB = 512
BLK = T // NB
EPS = 1e-6
S5W, S5G, S5H, S5P = 512, 32, 16, 64
XW, HS, HD, NG, NS = 768, 12, 64, 2, 128
VW, HM, DK, DV = 768, 6, 64, 128
DMIX = 2048
FF = 2816
FT = FF // P
UT, CT, CTT = 4, 16, 12
TOKC = 384
J = 8
NCH = T // J


def scope(nc, ctx):
    sems = []

    def give_back():
        if sems:
            nc.clear_and_free_semaphores(sems)
            nc.all_engine_barrier()

    ctx.callback(give_back)

    def sb(name, shape, dt=F32):
        return ctx.enter_context(nc.sbuf_tensor(name, shape, dt))

    def ps(name, shape, dt=F32):
        return ctx.enter_context(nc.psum_tensor(name, shape, dt))

    def sem(name):
        sems.append(nc.alloc_semaphore(name=name))
        return sems[-1]

    return sb, ps, sem


def step(eng, ins, sem, value):
    ins.then_inc(sem, 1)
    eng.wait_ge(sem, value)


def arrived(pool, dma, sent, value, free):
    dma.then_inc(sent, 16)
    pool.wait_ge(sent, value)
    pool.sem_inc(free, 1)


class Chain:

    def __init__(self, eng, sem):
        self.eng, self.sem, self.base, self.k = eng, sem, 0, 0

    def round(self, i, per_round):
        self.start = self.base + self.k
        self.base, self.k, self.per_round = self.start + i * per_round, 0, per_round

    def end(self, rounds):
        assert self.k == self.per_round, (self.k, self.per_round)
        self.base, self.k = self.start + rounds * self.per_round, 0

    def __call__(self, ins):
        self.k += 1
        step(self.eng, ins, self.sem, self.base + self.k)

def phase_norm(nc, x, gain_pre, ident, h_hi, h_lo):
    x_tiles = x[0].rearrange("(n p) d -> n p d", p=P)
    with ExitStack() as ctx:
        sb, ps, sem = scope(nc, ctx)
        xt, xn, junk, hraw = (sb("n_" + s, [P, 2, D]) for s in ("x", "xn", "junk", "hraw"))
        gain, ident_sb = sb("n_gain", [P, KD]), sb("n_ident", [P, P])
        stat = sb("n_stat", [P, 2, 4])
        banks = ps("n_banks", [P, 2, 2, NB])
        ssq_ok, mean_ok, root_ok, xn_ok, tr_ok, hraw_ok, hi_ok, lo_ok = (
            sem("n_" + s) for s in ("ssq_ok", "mean_ok", "root_ok", "xn_ok", "tr_ok", "hraw_ok", "hi_ok", "lo_ok"))
        const_in, x_in, dve_chain = sem("n_const_in"), (sem("n_x_in0"), sem("n_x_in1")), sem("n_dve_chain")
        block = ctx.enter_context(nc.Block())
        half = TT // 2

        @block.sync
        def _(sp):
            sp.dma_start(gain[:], gain_pre).then_inc(const_in, 16)
            sp.dma_start(ident_sb[:], ident).then_inc(const_in, 16)
            with sp.Fori(0, half) as i:
                for b in range(2):
                    n = i * 2 + b
                    sp.wait_ge(xn_ok, n + 1)
                    sp.dma_start(xt[:, b, :], x_tiles[ds(n, 1)].rearrange("a p d -> (a p) d")).then_inc(x_in[b], 16)

        @block.scalar
        def _(act):
            for s in (ssq_ok, root_ok, hi_ok):
                act.sem_inc(s, 2)

            def statistics(n, b, nth):
                act.wait_ge(x_in[b], nth * 16)
                act.wait_ge(xn_ok, n + 1)
                step(act, nc.scalar.activation(junk[:, b, :], xt[:, b, :], ACT.Square,
                                               accum_out=stat[:, b, 0:1]), ssq_ok, n + 3)
                act.wait_ge(mean_ok, n + 3)
                step(act, nc.scalar.activation(stat[:, b, 2:3], stat[:, b, 1:2], ACT.Sqrt), root_ok, n + 3)

            def upper(n, b):
                act.wait_ge(hraw_ok, n + 3)
                step(act, nc.scalar.activation(h_hi[:, :, ds(n * P, P)],
                                               hraw[:, b, :].rearrange("p (k t) -> p k t", k=KD), ACT.Copy),
                     hi_ok, n + 3)

            statistics(0, 0, 1)
            with act.Fori(0, half - 1) as i:
                for b in range(2):
                    statistics(i * 2 + b + 1, 1 - b, i + 1 + b)
                    upper(i * 2 + b, b)
            statistics(TT - 1, 1, half)
            upper(TT - 2, 0)
            upper(TT - 1, 1)

        @block.tensor
        def _(pe):
            pe.sem_inc(tr_ok, 2)
            pe.wait_ge(const_in, 32)
            with pe.Fori(0, half) as i:
                for b in range(2):
                    n = i * 2 + b
                    pe.wait_ge(xn_ok, n + 3)
                    pe.wait_ge(hraw_ok, n + 1)
                    for k in range(KD):
                        last = nc.tensor.transpose(banks[:, b, k // 4, (k % 4) * P:(k % 4 + 1) * P],
                                                   xn[:, b, k * P:(k + 1) * P], ident_sb[:])
                    last.then_inc(tr_ok, 1)

        @block.vector
        def _(dve):
            for s in (mean_ok, xn_ok, hraw_ok, lo_ok):
                dve.sem_inc(s, 2)
            chain = Chain(dve, dve_chain)
            dve.wait_ge(const_in, 32)

            def normalise(n, b):
                dve.wait_ge(ssq_ok, n + 3)
                step(dve, nc.vector.tensor_scalar(stat[:, b, 1:2], stat[:, b, 0:1], 1.0 / D, EPS, ALU.mult,
                                                  ALU.add), mean_ok, n + 3)
                dve.wait_ge(root_ok, n + 3)
                chain(nc.vector.reciprocal(stat[:, b, 3:4], stat[:, b, 2:3]))
                dve.wait_ge(tr_ok, n + 1)
                step(dve, nc.vector.tensor_scalar(xn[:, b, :], xt[:, b, :], stat[:, b, 3:4], None, ALU.mult),
                     xn_ok, n + 3)

            def split(n, b):
                dve.wait_ge(tr_ok, n + 3)
                for q in range(2):
                    g4 = gain[:, q * 4:q * 4 + 4].unsqueeze(2).to_broadcast([P, 4, P])
                    ins = nc.vector.tensor_tensor(
                        hraw[:, b, q * NB:(q + 1) * NB].rearrange("p (k t) -> p k t", k=4),
                        banks[:, b, q, :].rearrange("p (k t) -> p k t", k=4), g4, ALU.mult)
                    if q == 0:
                        chain(ins)
                    else:
                        step(dve, ins, hraw_ok, n + 3)
                dve.wait_ge(hi_ok, n + 3)
                step(dve, nc.vector.tensor_tensor(h_lo[:, :, ds(n * P, P)],
                                                  hraw[:, b, :].rearrange("p (k t) -> p k t", k=KD),
                                                  h_hi[:, :, ds(n * P, P)].bitcast(F32), ALU.subtract),
                     lo_ok, n + 3)

            normalise(0, 0)
            with dve.Fori(0, half - 1) as i:
                chain.round(i, 4)
                for b in range(2):
                    normalise(i * 2 + b + 1, 1 - b)
                    split(i * 2 + b, b)
            chain.end(half - 1)
            normalise(TT - 1, 1)
            split(TT - 2, 0)
            split(TT - 1, 1)

def phase_channels(nc, w_chan, conv_w, conv_b, ident, h_hi, h_lo, u_dram, conv_dram, tok_dram, gate_rows):
    with ExitStack() as ctx:
        sb, ps, sem = scope(nc, ctx)
        w_raw = sb("c_w_raw", [P, 2, KD, P])
        w_hi, w_lo = sb("c_w_hi", [P, 2, KD, P], F32R), sb("c_w_lo", [P, 2, KD, P], F32R)
        row = sb("c_row", [P, 2, T + 4])
        conv = sb("c_conv", [P, 2, T])
        tok = sb("c_tok", [P, 2, TT // 2, P])
        cw, cb, ident_sb = sb("c_cw", [P, CT, 4]), sb("c_cb", [P, CT]), sb("c_ident", [P, P])
        banks, tr_banks = ps("c_banks", [P, BLK, NB]), ps("c_tr_banks", [P, 2, NB])
        w_in = (sem("c_w_in0"), sem("c_w_in1"))
        const_in, whi_ok, wlo_ok, mm_ok, evac_ok, acc_ok, silu_ok, tr_ok, tok_ok = (
            sem("c_" + s) for s in ("const_in", "whi_ok", "wlo_ok", "mm_ok", "evac_ok", "acc_ok", "silu_ok",
                                    "tr_ok", "tok_ok"))
        row_out, tok_out = (sem("c_row_out0"), sem("c_row_out1")), (sem("c_tok_out0"), sem("c_tok_out1"))
        row_free, tok_free = (sem("c_row_free0"), sem("c_row_free1")), (sem("c_tok_free0"), sem("c_tok_free1"))
        dve_chain = sem("c_dve_chain")
        block = ctx.enter_context(nc.Block())
        TILES = UT + CT + 1
        GATE = TILES - 1
        r_u, r_t, r_c = UT // 2, CTT // 2, (CT - CTT) // 2

        @block.sync
        def _(sp):
            sp.dma_start(cw[:], conv_w).then_inc(const_in, 16)
            sp.dma_start(cb[:], conv_b).then_inc(const_in, 16)
            sp.dma_start(ident_sb[:], ident).then_inc(const_in, 16)

            def load(n, b):
                sp.wait_ge(wlo_ok, n + 1)
                sp.dma_start(w_raw[:, b].rearrange("p k m -> p (k m)"),
                             w_chan[ds(n, 1)].rearrange("a p m -> (a p) m")).then_inc(w_in[b], 16)

            with sp.Fori(0, GATE // 2) as i:
                for b in range(2):
                    load(i * 2 + b, b)
            load(GATE, 0)

        @block.gpsimd
        def _(pool):
            for s in row_free + tok_free:
                pool.sem_inc(s, 1)
            with pool.Fori(0, r_u) as i:
                for b in range(2):
                    n = i * 2 + b
                    pool.wait_ge(evac_ok, 4 * n + 4 + 8)
                    arrived(pool, pool.dma_start(u_dram[:, ds(n * P, P), :].rearrange("j p c -> p j c"),
                                                 row[:, b, 0:T].rearrange("p (j c) -> p j c", j=J)),
                            row_out[b], i * 16 + 16, row_free[b])
            with pool.Fori(0, r_t) as i:
                for b in range(2):
                    n = i * 2 + b
                    pool.wait_ge(silu_ok, n + 3)
                    arrived(pool, pool.dma_start(conv_dram[ds(n, 1)].rearrange("a p t -> (a p) t"), conv[:, b, :]),
                            row_out[b], i * 16 + 16 * (r_u + 1), row_free[b])
                    for half in range(2):
                        pool.wait_ge(tok_ok, 4 * n + 2 * half + 2)
                        arrived(pool, pool.dma_start(tok_dram[half * T // 2:(half + 1) * T // 2, ds(n * P, P)]
                                                     .rearrange("(a p) m -> p a m", p=P), tok[:, half]),
                                tok_out[half], n * 16 + 16, tok_free[half])
            with pool.Fori(0, r_c) as i:
                for b in range(2):
                    n = i * 2 + b + CTT
                    pool.wait_ge(silu_ok, n + 3)
                    arrived(pool, pool.dma_start(conv_dram[ds(n, 1)].rearrange("a p t -> (a p) t"), conv[:, b, :]),
                            row_out[b], i * 16 + 16 * (r_u + r_t + 1), row_free[b])
            for b in range(2):
                pool.wait_ge(row_out[b], 16 * (UT + CT) // 2)
                pool.wait_ge(tok_out[b], 16 * CTT)

        @block.scalar
        def _(act):
            act.sem_inc(whi_ok, 2)
            act.sem_inc(evac_ok, 8)
            act.sem_inc(silu_ok, 2)

            def upper(n, b, nth):
                act.wait_ge(w_in[b], nth * 16)
                act.wait_ge(mm_ok, 4 * n + 4)
                step(act, nc.scalar.activation(w_hi[:, b], w_raw[:, b], ACT.Copy), whi_ok, n + 3)

            upper(0, 0, 1)
            with act.Fori(0, r_u) as i:
                for b in range(2):
                    n = i * 2 + b
                    upper(n + 1, 1 - b, i + 1 + b)
                    act.wait_ge(row_free[b], i + 1)
                    for q in range(BLK):
                        act.wait_ge(mm_ok, 4 * n + q + 1 + 8)
                        step(act, nc.scalar.activation(
                            row[:, b, 0:T].rearrange("p (j c) -> p c j", j=J)[:, q * NB // J:(q + 1) * NB // J, :],
                            banks[:, q, :].rearrange("p (c j) -> p c j", j=J), ACT.Copy), evac_ok, 4 * n + q + 1 + 8)

            def conv_tiles(first, rounds):
                with act.Fori(0, rounds) as i:
                    for b in range(2):
                        m = i * 2 + b + first
                        n = m + UT
                        upper(n + 1, 1 - b, i + (first + UT) // 2 + 1 + b)
                        act.wait_ge(acc_ok, m + 1)
                        if first == 0:
                            act.wait_ge(row_free[b], r_u + 1)
                            act.wait_ge(acc_ok, 2)
                        for q in range(BLK):
                            act.wait_ge(mm_ok, 4 * n + q + 1 + 8)
                            step(act, nc.scalar.activation(row[:, b, 3 + q * NB:3 + (q + 1) * NB], banks[:, q, :],
                                                           ACT.Copy), evac_ok, 4 * n + q + 1 + 8)
                        act.wait_ge(acc_ok, m + 3)
                        step(act, nc.scalar.activation(conv[:, b, :], conv[:, b, :], ACT.Silu), silu_ok, m + 3)

            conv_tiles(0, r_t)
            conv_tiles(CTT, r_c)
            for q in range(BLK):
                act.wait_ge(mm_ok, 4 * GATE + q + 1 + 8)
                step(act, nc.scalar.activation(gate_rows[:, q * NB:(q + 1) * NB], banks[:, q, :], ACT.Copy),
                     evac_ok, 4 * GATE + q + 1 + 8)

        @block.vector
        def _(dve):
            dve.sem_inc(wlo_ok, 2)
            chain = Chain(dve, dve_chain)

            def lower(n, b):
                dve.wait_ge(whi_ok, n + 3)
                dve.wait_ge(mm_ok, 4 * n + 4)
                step(dve, nc.vector.tensor_tensor(w_lo[:, b], w_raw[:, b], w_hi[:, b].bitcast(F32), ALU.subtract),
                     wlo_ok, n + 3)

            lower(0, 0)
            with dve.Fori(0, r_u) as i:
                for b in range(2):
                    lower(i * 2 + b + 1, 1 - b)
            for b in range(2):
                dve.wait_ge(row_free[b], r_u + 1)
                chain(nc.vector.memset(row[:, b, 0:3], 0.0))
            dve.sem_inc(acc_ok, 2)
            dve.wait_ge(const_in, 48)

            def conv_tiles(first, rounds, transposed):
                with dve.Fori(0, rounds) as i:
                    chain.round(i, 6)
                    for b in range(2):
                        m = i * 2 + b + first
                        n = m + UT
                        lower(n + 1, 1 - b)
                        dve.wait_ge(evac_ok, 4 * n + 4 + 8)
                        dve.wait_ge(row_free[b], i + (first + UT) // 2 + 1)
                        w = [cw[:, ds(m, 1), s:s + 1].rearrange("p a s -> p (a s)") for s in range(4)]
                        if transposed:
                            dve.wait_ge(tr_ok, 4 * m)
                        chain(nc.vector.tensor_scalar(conv[:, b, :], row[:, b, 3:T + 3], w[3], cb[:, ds(m, 1)],
                                                      ALU.mult, ALU.add))
                        for s in (2, 1, 0):
                            ins = nc.vector.scalar_tensor_tensor(conv[:, b, :], row[:, b, s:T + s], w[s], conv[:, b, :],
                                                                 ALU.mult, ALU.add)
                            if s:
                                chain(ins)
                            else:
                                step(dve, ins, acc_ok, m + 3)
                        if transposed:
                            for q in range(4):
                                half = q // 2
                                dve.wait_ge(tr_ok, 4 * m + q + 1)
                                if q % 2 == 0:
                                    dve.wait_ge(tok_free[half], m + 1)
                                step(dve, nc.vector.tensor_copy(
                                    tok[:, half, q % 2 * 4:q % 2 * 4 + 4, :].rearrange("p a m -> p (a m)"),
                                    tr_banks[:, q % 2, :]), tok_ok, 4 * m + q + 1)
                chain.end(rounds)

            conv_tiles(0, r_t, True)
            conv_tiles(CTT, r_c, False)

        @block.tensor
        def _(pe):
            pe.sem_inc(mm_ok, 8)
            pe.wait_ge(const_in, 48)

            def products(n, b):
                pe.wait_ge(wlo_ok, n + 3)
                for q in range(BLK):
                    pe.wait_ge(evac_ok, 4 * n + q + 1 + 4)
                    for k in range(KD):
                        for j, (w, h) in enumerate(((w_hi, h_hi), (w_hi, h_lo), (w_lo, h_hi))):
                            last = nc.tensor.matmul(banks[:, q, :], w[:, b, k, :], h[:, k, q * NB:(q + 1) * NB],
                                                    start=k == 0 and j == 0, stop=k == KD - 1 and j == 2)
                    last.then_inc(mm_ok, 1)

            def transposes(m, b):
                pe.wait_ge(silu_ok, m + 3)
                for q in range(4):
                    if q < 2:
                        pe.wait_ge(tok_ok, 4 * m)
                    else:
                        pe.wait_ge(tok_ok, 4 * m + q - 1)
                    for a in range(4):
                        last = nc.tensor.transpose(tr_banks[:, q % 2, a * P:(a + 1) * P],
                                                   conv[:, b, (q * 4 + a) * P:(q * 4 + a + 1) * P], ident_sb[:])
                    last.then_inc(tr_ok, 1)

            with pe.Fori(0, r_u) as i:
                for b in range(2):
                    products(i * 2 + b, b)
            products(UT, 0)
            with pe.Fori(0, r_t - 1) as i:
                for b in range(2):
                    m = i * 2 + b
                    products(m + UT + 1, 1 - b)
                    transposes(m, b)
            products(CTT - 1 + UT, 1)
            transposes(CTT - 2, 0)
            products(CTT + UT, 0)
            transposes(CTT - 1, 1)
            with pe.Fori(0, r_c - 1) as i:
                for b in range(2):
                    products(i * 2 + b + 1 + CTT + UT, 1 - b)
            products(CT + UT - 1, 1)
            products(GATE, 0)

def phase_tokens(nc, w_tok, h_hi, h_lo, tokmaj_dram):
    PAIR = 2
    with ExitStack() as ctx:
        sb, ps, sem = scope(nc, ctx)
        w_raw = sb("t_w_raw", [P, KD, TOKC])
        w_hi, w_lo = sb("t_w_hi", [P, 2, KD, TOKC], F32R), sb("t_w_lo", [P, 2, KD, TOKC], F32R)
        out = sb("t_out", [P, 2, PAIR, TOKC])
        banks = ps("t_banks", [P, 4, NB])
        w_in, whi_ok, wlo_ok, mm_ok, evac_ok, sent0, sent1 = (
            sem("t_" + s) for s in ("w_in", "whi_ok", "wlo_ok", "mm_ok", "evac_ok", "sent0", "sent1"))
        sent = (sent0, sent1)
        free = (sem("t_free0"), sem("t_free1"))
        block = ctx.enter_context(nc.Block())
        kinds = (ACT.Silu, ACT.Sigmoid, ACT.Copy)
        blocks = 2 * len(kinds)

        @block.sync
        def _(sp):
            def load(n):
                sp.wait_ge(wlo_ok, n)
                sp.dma_start(w_raw[:].rearrange("p k m -> p (k m)"),
                             w_tok[ds(n, 1)].rearrange("a p m -> (a p) m")).then_inc(w_in, 16)

            sp.dma_start(w_raw[:].rearrange("p k m -> p (k m)"), w_tok[0]).then_inc(w_in, 16)
            with sp.Fori(0, blocks - 1) as i:
                load(i + 1)

        @block.gpsimd
        def _(pool):
            for s in free:
                pool.sem_inc(s, 1)
            with pool.Fori(0, blocks) as n:
                for s in range(TT // PAIR):
                    pool.wait_ge(evac_ok, n * TT + (s + 1) * PAIR + 4)
                    arrived(pool, pool.dma_start(tokmaj_dram[s * PAIR * P:(s + 1) * PAIR * P, ds(n * TOKC, TOKC)]
                                                 .rearrange("(a p) m -> p a m", p=P), out[:, s % 2]),
                            sent[s % 2], (n * (TT // PAIR // 2) + s // 2) * 16 + 16, free[s % 2])
            for b in range(2):
                pool.wait_ge(sent[b], blocks * (TT // PAIR // 2) * 16)

        @block.scalar
        def _(act):
            act.sem_inc(evac_ok, 4)

            def upper(n):
                act.wait_ge(w_in, n * 16 + 16)
                if n >= 2:
                    act.wait_ge(mm_ok, (n - 1) * TT)
                step(act, nc.scalar.activation(w_hi[:, n % 2], w_raw[:], ACT.Copy), whi_ok, n + 1)

            upper(0)
            for n in range(blocks):
                if n + 1 < blocks:
                    upper(n + 1)
                with act.Fori(0, TT // 4) as i:
                    for t in range(4):
                        m = i * 4 + (n * TT + t)
                        act.wait_ge(mm_ok, m + 1)
                        if t % PAIR == 0:
                            act.wait_ge(free[t // PAIR], i + n * TT // 4 + 1)
                        step(act, nc.scalar.activation(out[:, t // PAIR, t % PAIR, :], banks[:, t, 0:TOKC],
                                                       kinds[n // 2]), evac_ok, m + 1 + 4)

        @block.vector
        def _(dve):
            for n in range(blocks):
                dve.wait_ge(whi_ok, n + 1)
                step(dve, nc.vector.tensor_tensor(w_lo[:, n % 2], w_raw[:], w_hi[:, n % 2].bitcast(F32), ALU.subtract),
                     wlo_ok, n + 1)

        @block.tensor
        def _(pe):
            with pe.Fori(0, blocks // 2) as i:
                for b in range(2):
                    n = i * 2 + b
                    pe.wait_ge(wlo_ok, n + 1)
                    for t in range(TT):
                        pe.wait_ge(evac_ok, n * TT + t + 1)
                        for k in range(KD):
                            for j, (h, w) in enumerate(((h_hi, w_hi), (h_lo, w_hi), (h_hi, w_lo))):
                                last = nc.tensor.matmul(banks[:, t % 4, 0:TOKC], h[:, k, t * P:(t + 1) * P],
                                                        w[:, b, k, :], start=k == 0 and j == 0,
                                                        stop=k == KD - 1 and j == 2)
                        last.then_inc(mm_ok, 1)

ROWS = 64
FR, IR = 32, 64
NBC = HS + HM


def phase_gates(nc, gate_rows, gate_bias, gate_sign, gate_log, ident, tok_cols, rows_dram, decay_dram):
    with ExitStack() as ctx:
        sb, ps, sem = scope(nc, ctx)
        x, e, u, lnu, sp_, cum = (sb("g_" + s, [ROWS, T]) for s in ("x", "e", "u", "ln", "softplus", "cum"))
        mask, beta, run_max = sb("g_mask", [ROWS, T]), sb("g_beta", [ROWS, T]), sb("g_max", [ROWS, T])
        col_b, col_c, col_d = (sb("g_col_" + s, [ROWS, T]) for s in "bcd")
        bias, sign, alog, neg_a = sb("g_bias", [P, 1]), sb("g_sign", [ROWS, 1]), sb("g_log", [ROWS, 1]), sb("g_neg_a", [ROWS, 1])
        m_prev, decay = sb("g_m_prev", [ROWS, TT]), sb("g_decay", [ROWS, TT])
        ident_sb = sb("g_ident", [P, P])
        banks = ps("g_banks", [P, 2, 2, 4, ROWS])
        const_in, out, act_chain, dve_chain = (sem("g_" + s) for s in ("const_in", "out", "act_chain", "dve_chain"))
        neg_a_ok, abs_ok, exp_ok, one_plus_ok, ln_ok, args_ok, factors_ok, tr_ok, tok_ok = (
            sem("g_" + s) for s in ("neg_a_ok", "abs_ok", "exp_ok", "one_plus_ok", "ln_ok", "args_ok", "factors_ok",
                                    "tr_ok", "tok_ok"))
        block = ctx.enter_context(nc.Block())
        f, s = slice(FR, FR + HM), slice(0, HS)

        def chunks(a):
            return a.rearrange("p (c t) -> p c t", t=P)

        def wide(a, n):
            return a.unsqueeze(2).to_broadcast([n, TT, P])

        @block.sync
        def _(sp):
            for dst, src in ((bias, gate_bias), (sign, gate_sign), (alog, gate_log), (ident_sb, ident)):
                sp.dma_start(dst[:], src).then_inc(const_in, 16)
            sp.wait_ge(args_ok, 1)
            sp.dma_start(rows_dram[:, 0:HS, :].rearrange("c r t -> r c t"), chunks(cum[s, :])).then_inc(out, 16)
            sp.dma_start(rows_dram[:, HS:NBC, :].rearrange("c r t -> r c t"), chunks(lnu[f, :])).then_inc(out, 16)
            sp.wait_ge(factors_ok, 1)
            sp.dma_start(decay_dram[0:HS, :], decay[s, :]).then_inc(out, 16)
            sp.dma_start(decay_dram[HS:NBC, :], decay[f, :]).then_inc(out, 16)
            sp.wait_ge(out, 64)

        @block.scalar
        def _(act):
            chain = Chain(act, act_chain)
            act.wait_ge(const_in, 64)
            nc.scalar.activation(neg_a[:], alog[:], ACT.Exp).then_inc(neg_a_ok, 1)
            act.wait_ge(abs_ok, 1)
            nc.scalar.activation(e[:], lnu[:], ACT.Exp, scale=-1.0).then_inc(exp_ok, 1)
            act.wait_ge(one_plus_ok, 1)
            nc.scalar.activation(lnu[:], u[:], ACT.Ln).then_inc(ln_ok, 1)
            act.wait_ge(args_ok, 1)
            chain(nc.scalar.activation(col_b[f, :], x[f, :], ACT.Exp))
            chain(nc.scalar.activation(col_c[:], col_c[:], ACT.Exp))
            chain(nc.scalar.activation(col_d[:], col_d[:], ACT.Exp))
            nc.scalar.activation(decay[:], decay[:], ACT.Exp).then_inc(factors_ok, 1)
            for n in range(TT // 2):
                act.wait_ge(tr_ok, n + 1)
                step(act, nc.scalar.activation(tok_cols[:, 2 * n:2 * n + 2], banks[:, n % 2], ACT.Copy), tok_ok, n + 1)

        @block.vector
        def _(dve):
            chain = Chain(dve, dve_chain)
            dve.wait_ge(const_in, 64)
            chain(nc.vector.tensor_scalar(x[:], gate_rows[0:ROWS, :], bias[0:ROWS, :], sign[:], ALU.add, ALU.mult))
            step(dve, nc.vector.scalar_tensor_tensor(lnu[:], x[:], -1.0, x[:], ALU.mult, ALU.max), abs_ok, 1)
            dve.wait_ge(exp_ok, 1)
            step(dve, nc.vector.tensor_scalar(u[:], e[:], 1.0, None, ALU.add), one_plus_ok, 1)
            chain(nc.vector.scalar_tensor_tensor(e[:], u[:], -1.0, e[:], ALU.add, ALU.subtract))
            dve.wait_ge(ln_ok, 1)
            chain(nc.vector.scalar_tensor_tensor(sp_[:], x[:], 0.0, lnu[:], ALU.max, ALU.add))
            chain(nc.vector.tensor_tensor(sp_[:], sp_[:], e[:], ALU.subtract))
            dve.wait_ge(neg_a_ok, 1)
            chain(nc.vector.tensor_scalar(x[:], sp_[:], neg_a[:], -1.0, ALU.mult, ALU.mult))
            chain(nc.vector.memset(mask[:], 1.0))
            chain(nc.vector.memset(chunks(mask[:])[:, :, 0:1], 0.0))
            chain(nc.vector.tensor_tensor_scan(cum[:], mask[:], x[:], 0.0, ALU.mult, ALU.add))
            end = chunks(cum[:])[:, :, P - 1]
            end_f = chunks(cum[f, :])[:, :, P - 1]
            chain(nc.vector.tensor_scalar(u[f, :], gate_rows[IR:IR + HM, :], bias[IR:IR + HM, :], None, ALU.add))
            chain(nc.vector.tensor_tensor(sp_[f, :], u[f, :], cum[f, :], ALU.subtract))
            chain(nc.vector.memset(beta[:], 0.0))
            chain(nc.vector.tensor_copy(chunks(beta[f, :])[:, 1:TT, 0], end_f[:, 0:TT - 1]))
            chain(nc.vector.tensor_tensor_scan(run_max[f, :], beta[f, :], sp_[f, :], 0.0, ALU.add, ALU.max))
            m_end = chunks(run_max[f, :])[:, :, P - 1]
            chain(nc.vector.memset(m_prev[:], 0.0))
            chain(nc.vector.tensor_tensor(m_prev[f, 1:TT], m_end[:, 0:TT - 1], end_f[:, 0:TT - 1], ALU.add))
            chain(nc.vector.tensor_tensor(chunks(x[f, :]), wide(m_prev[f, :], HM), chunks(run_max[f, :]), ALU.subtract))
            chain(nc.vector.tensor_scalar(col_b[:], cum[:], -1.0, None, ALU.mult))
            chain(nc.vector.tensor_scalar(lnu[f, :], run_max[f, :], -1.0, None, ALU.mult))
            chain(nc.vector.tensor_copy(col_c[:], cum[:]))
            chain(nc.vector.tensor_tensor(chunks(col_c[f, :]), chunks(sp_[f, :]), wide(m_end, HM), ALU.subtract))
            chain(nc.vector.tensor_tensor(chunks(col_d[:]), wide(end, ROWS), chunks(cum[:]), ALU.subtract))
            chain(nc.vector.tensor_tensor(col_d[f, :], lnu[f, :], cum[f, :], ALU.subtract))
            chain(nc.vector.tensor_copy(decay[:], end))
            step(dve, nc.vector.tensor_tensor(decay[f, :], m_prev[f, :], m_end, ALU.subtract), args_ok, 1)
            dve.wait_ge(factors_ok, 1)
            chain(nc.vector.tensor_scalar(col_c[f, :], col_c[f, :], DK ** -0.5, None, ALU.mult))
            step(dve, nc.vector.tensor_tensor(col_d[s, :], col_d[s, :], sp_[s, :], ALU.mult), args_ok, 2)

        @block.tensor
        def _(pe):
            pe.wait_ge(const_in, 64)
            pe.wait_ge(args_ok, 2)
            for n in range(TT // 2):
                if n >= 2:
                    pe.wait_ge(tok_ok, n - 1)
                for c in range(2):
                    for k, rows in enumerate((sp_, col_b, col_c, col_d)):
                        last = nc.tensor.transpose(banks[:, n % 2, c, k, :], rows[:, (2 * n + c) * P:(2 * n + c + 1) * P],
                                                   ident_sb[0:ROWS, 0:ROWS])
                last.then_inc(tr_ok, 1)

Q = S5G // 2
TWO_PI = 2 * math.pi
TURN = (6.28125, float(np.float32(TWO_PI - 6.28125)), float(TWO_PI - 6.28125 - np.float32(TWO_PI - 6.28125)))
MAGIC = 1.5 * 2.0 ** 23
PADK = (2 * J - 1) * S5H


def phase_s5_setup(nc, lam_re, lam_im, log_step, b_re, b_im, c_re, c_im, skip, ident, table, rho, ca, wt, kern_dram):
    with ExitStack() as ctx:
        sb, ps, sem = scope(nc, ctx)
        lre, lim, lst = (sb("s_" + s, [P, Q]) for s in ("lre", "lim", "lst"))
        br, bi, cr, ci, bbr, bbi = (sb("s_" + s, [P, Q, S5H]) for s in ("br", "bi", "cr", "ci", "bbr", "bbi"))
        ident_sb, skip_sb = sb("s_ident", [P, P]), sb("s_skip", [S5H, S5G])
        stp, mag, ang, turns, red_s, red_c, sin, cos, t0, t1, t2, t3, f_re, f_im, den = (
            sb("s_" + s, [P, Q]) for s in ("step", "mag", "ang", "turns", "red_s", "red_c", "sin", "cos", "t0", "t1", "t2",
                                           "t3", "f_re", "f_im", "den"))
        pow_re, pow_im = sb("s_pow_re", [P, Q, J + 1]), sb("s_pow_im", [P, Q, J + 1])
        w_re, w_im, tmp = (sb("s_" + s, [P, Q, J, S5H]) for s in ("w_re", "w_im", "tmp"))
        tmp2 = sb("s_tmp2", [P, Q, (J + 1) * S5H])
        kern = sb("s_kern", [S5H, S5G, PADK])
        banks, kbanks = ps("s_banks", [P, 2, NB]), ps("s_kbanks", [S5H, 2, 2, NB])
        const_in, out, dve_chain = (sem("s_" + s) for s in ("const_in", "out", "dve_chain"))
        step_ok, expo_ok, mag_ok, angle_ok, trig_ok, w_ok, ca_ok, wt_tr, wt_ok, k_mm, k_ok, kern_ok = (
            sem("s_" + s) for s in ("step_ok", "expo_ok", "mag_ok", "angle_ok", "trig_ok", "w_ok", "ca_ok", "wt_tr",
                                    "wt_ok", "k_mm", "k_ok", "kern_ok"))
        block = ctx.enter_context(nc.Block())
        loads = ((lre, lam_re), (lim, lam_im), (lst, log_step), (br, b_re), (bi, b_im), (cr, c_re), (ci, c_im),
                 (ident_sb, ident), (skip_sb, skip))

        @block.sync
        def _(sp):
            for dst, src in loads:
                sp.dma_start(dst[:], src).then_inc(const_in, 16)
            sp.wait_ge(kern_ok, 1)
            sp.dma_start(kern_dram.rearrange("g h m -> h g m"), kern[:]).then_inc(out, 16)
            sp.wait_ge(out, 16)

        @block.scalar
        def _(act):
            act.wait_ge(const_in, 16 * len(loads))
            nc.scalar.activation(stp[:], lst[:], ACT.Exp).then_inc(step_ok, 1)
            act.wait_ge(expo_ok, 1)
            nc.scalar.activation(mag[:], t0[:], ACT.Exp).then_inc(mag_ok, 1)
            act.wait_ge(angle_ok, 1)
            nc.scalar.activation(sin[:], red_s[:], ACT.Sin).then_inc(trig_ok, 1)
            nc.scalar.activation(cos[:], red_c[:], ACT.Sin).then_inc(trig_ok, 1)
            for n in range(Q // 2):
                act.wait_ge(wt_tr, n + 1)
                step(act, nc.scalar.activation(wt[:, 2 * n:2 * n + 2].rearrange("p q r m -> p (q r m)"), banks[:, n % 2, :],
                                               ACT.Copy), wt_ok, n + 1)

        @block.vector
        def _(dve):
            chain = Chain(dve, dve_chain)
            tt, ts, stt = nc.vector.tensor_tensor, nc.vector.tensor_scalar, nc.vector.scalar_tensor_tensor
            mul, add, sub = ALU.mult, ALU.add, ALU.subtract
            dve.wait_ge(const_in, 16 * len(loads))
            dve.wait_ge(step_ok, 1)
            step(dve, tt(t0[:], lre[:], stp[:], mul), expo_ok, 1)
            chain(tt(ang[:], lim[:], stp[:], mul))
            for red, quarter in ((red_s, 0.0), (red_c, 0.25)):
                chain(ts(turns[:], ang[:], 1 / TWO_PI, quarter, mul, add))
                chain(ts(turns[:], turns[:], MAGIC, None, add))
                chain(ts(turns[:], turns[:], -MAGIC, None, add))
                chain(stt(red[:], turns[:], -TURN[0], ang[:], mul, add))
                chain(stt(red[:], turns[:], -TURN[1], red[:], mul, add))
                chain(stt(red[:], turns[:], -TURN[2], red[:], mul, add))
                if quarter:
                    chain(ts(red[:], red[:], math.pi / 2, None, add))
                ins = ts(red[:], red[:], 3.1415925, -3.1415925, ALU.min, ALU.max)
                if quarter:
                    step(dve, ins, angle_ok, 1)
                else:
                    chain(ins)
            dve.wait_ge(mag_ok, 1)
            dve.wait_ge(trig_ok, 2)

            def product(o_re, o_im, a_re, a_im, b_re_, b_im_, t):
                chain(tt(t, a_im, b_im_, mul))
                chain(tt(o_re, a_re, b_re_, mul))
                chain(tt(o_re, o_re, t, sub))
                chain(tt(t, a_re, b_im_, mul))
                chain(tt(o_im, a_im, b_re_, mul))
                chain(tt(o_im, o_im, t, add))

            chain(nc.vector.memset(pow_re[:, :, 0], 1.0))
            chain(nc.vector.memset(pow_im[:, :, 0], 0.0))
            chain(tt(pow_re[:, :, 1], mag[:], cos[:], mul))
            chain(tt(pow_im[:, :, 1], mag[:], sin[:], mul))
            for j in range(2, J + 1):
                product(pow_re[:, :, j], pow_im[:, :, j], pow_re[:, :, j - 1], pow_im[:, :, j - 1], pow_re[:, :, 1],
                        pow_im[:, :, 1], t0[:])
            chain(ts(t1[:], pow_re[:, :, 1], -1.0, None, add))
            chain(tt(t0[:], lre[:], lre[:], mul))
            chain(tt(den[:], lim[:], lim[:], mul))
            chain(tt(den[:], den[:], t0[:], add))
            chain(nc.vector.reciprocal(den[:], den[:]))
            chain(tt(t0[:], pow_im[:, :, 1], lim[:], mul))
            chain(tt(f_re[:], t1[:], lre[:], mul))
            chain(tt(f_re[:], f_re[:], t0[:], add))
            chain(tt(f_re[:], f_re[:], den[:], mul))
            chain(tt(t0[:], t1[:], lim[:], mul))
            chain(tt(f_im[:], pow_im[:, :, 1], lre[:], mul))
            chain(tt(f_im[:], f_im[:], t0[:], sub))
            chain(tt(f_im[:], f_im[:], den[:], mul))

            def over_h(a):
                return a.unsqueeze(2).to_broadcast([P, Q, S5H])

            product(bbr[:], bbi[:], over_h(f_re[:]), over_h(f_im[:]), br[:], bi[:], tmp[:, :, 0, :])
            for j in range(J):
                pr, pi = (over_h(a[:, :, J - 1 - j]) for a in (pow_re, pow_im))
                product(w_re[:, :, j, :], w_im[:, :, j, :], pr, pi, bbr[:], bbi[:], tmp[:, :, j, :])
            dve.sem_inc(w_ok, 1)
            for tau in range(J + 1):
                pr, pi = (over_h(a[:, :, tau]) for a in (pow_re, pow_im))
                at = slice(tau * S5H, (tau + 1) * S5H)
                product(ca[:, :, 0, at], ca[:, :, 1, at], pr, pi, cr[:], ci[:], tmp2[:, :, at])
            step(dve, ts(ca[:, :, 1], ca[:, :, 1], -1.0, None, mul), ca_ok, 1)
            chain(tt(t0[:], mag[:], mag[:], mul))
            chain(tt(t1[:], t0[:], t0[:], mul))
            chain(tt(rho[:], t1[:], t1[:], mul))
            now, nxt = (cos, sin), (t1, t2)
            for _ in range(3):
                product(nxt[0][:], nxt[1][:], now[0][:], now[1][:], now[0][:], now[1][:], t3[:])
                now, nxt = nxt, (now if now[0] is not cos else (f_re, f_im))
            chain(nc.vector.memset(table[:, :, 0, 0:1], 1.0))
            chain(nc.vector.memset(table[:, :, 1, 0:1], 0.0))
            n = 1
            while n < NCH:
                c, s = (a[:].unsqueeze(2).to_broadcast([P, Q, n]) for a in now)
                product(table[:, :, 0, n:2 * n], table[:, :, 1, n:2 * n], c, s, table[:, :, 0, 0:n], table[:, :, 1, 0:n],
                        tmp[:].rearrange("p q j h -> p q (j h)")[:, :, 0:n])
                n *= 2
                if n < NCH:
                    product(nxt[0][:], nxt[1][:], now[0][:], now[1][:], now[0][:], now[1][:], t3[:])
                    now, nxt = nxt, now
            chain(nc.vector.memset(kern[:], 0.0))
            for n in range(Q // 4):
                for e in range(2):
                    dve.wait_ge(k_mm, 2 * n + e + 1)
                    step(dve, nc.vector.tensor_copy(
                        kern[:].rearrange("h (q e) m -> h q e m", e=2)[:, 4 * n:4 * n + 4, e, (J - 1) * S5H:],
                        kbanks[:, n % 2, e, :].rearrange("h (q m) -> h q m", q=4)), k_ok, 2 * n + e + 1)
            zero_lag = kern[:, :, (J - 1) * S5H:J * S5H]
            t = w_re[0:S5H].rearrange("p q j h -> p (q j h)")[:, 0:S5G * S5H].rearrange("p (g h) -> p g h", h=S5H)
            dve.wait_ge(wt_ok, Q // 2)
            chain(tt(t, ident_sb[0:S5H, 0:S5H].unsqueeze(1).to_broadcast([S5H, S5G, S5H]),
                     skip_sb[:].unsqueeze(2).to_broadcast([S5H, S5G, S5H]), mul))
            step(dve, tt(zero_lag, zero_lag, t, add), kern_ok, 1)

        @block.tensor
        def _(pe):
            pe.wait_ge(w_ok, 1)
            pe.wait_ge(const_in, 16 * len(loads))
            for n in range(Q // 2):
                if n >= 2:
                    pe.wait_ge(wt_ok, n - 1)
                for q in range(2):
                    for r, w in enumerate((w_re, w_im)):
                        last = nc.tensor.transpose(banks[:, n % 2, (2 * q + r) * P:(2 * q + r + 1) * P],
                                                   w[:, 2 * n + q].rearrange("p j h -> p (j h)"), ident_sb[:])
                last.then_inc(wt_tr, 1)
            pe.wait_ge(ca_ok, 1)
            for n in range(Q // 4):
                if n >= 2:
                    pe.wait_ge(k_ok, 2 * n - 2)
                for e in range(2):
                    lanes = slice(e * S5P, (e + 1) * S5P)
                    for q in range(4):
                        for r, b_in in enumerate((bbr, bbi)):
                            last = nc.tensor.matmul(kbanks[:, n % 2, e, q * P:(q + 1) * P], b_in[lanes, 4 * n + q, :],
                                                    ca[lanes, 4 * n + q, r, 0:J * S5H], start=r == 0, stop=r == 1)
                    last.then_inc(k_mm, 1)


def phase_s5(nc, table, rho, ca, wt, kern_dram, u_dram, g_dram):
    with ExitStack() as ctx:
        sb, ps, sem = scope(nc, ctx)
        XB = 4
        x, y = sb("r_x", [P, XB, 2, NCH]), sb("r_y", [P, S5G, NCH])
        w = sb("r_w", [P, XB, 4, P])
        kern_all, kern = sb("r_kern_all", [P, S5G, P]), sb("r_kern", [P, XB, 2, P])
        prod, rot = sb("r_prod", [P, 4, NCH]), sb("r_rot", [P, 2, NCH])
        state, prod2 = sb("r_state", [P, 2, NCH]), sb("r_prod2", [P, 4, NCH])
        before = sb("r_before", [P, 2, 2, NCH])
        banks_in, banks_out = ps("r_banks_in", [P, 2, 2, NCH]), ps("r_banks_out", [P, 2, 2, NB])
        w_ok, kern_ok, in_mm, before_ok, out_mm, gelu_ok, prod_ok = (
            sem("r_" + s) for s in ("w_ok", "kern_ok", "in_mm", "before_ok", "out_mm", "gelu_ok", "prod_ok"))
        x_in, kern_in, sent = tuple(sem("r_x_in%d" % b) for b in range(XB)), sem("r_kern_in"), (sem("r_sent0"), sem("r_sent1"))
        dve_chain, pool_chain = sem("r_dve_chain"), sem("r_pool_chain")
        block = ctx.enter_context(nc.Block())
        GT = S5G // UT

        def send(eng, part):
            for j in range(part, J, 2):
                for t in range(UT):
                    eng.dma_start(g_dram[j, t * P:(t + 1) * P].rearrange("(g h) c -> h g c", h=S5H),
                                  y[j * S5H:(j + 1) * S5H, t * GT:(t + 1) * GT, :]).then_inc(sent[part], 16)
            eng.wait_ge(sent[part], 16 * UT * J // 2)

        @block.sync
        def _(sp):
            with sp.Fori(0, Q // XB) as i:
                for b in range(XB):
                    q = i * XB + b
                    sp.wait_ge(out_mm, q + 1)
                    for j in range(J):
                        sp.dma_start(x[j * S5H:(j + 1) * S5H, b], u_dram[j, ds(q * 2 * S5H, 2 * S5H), :]
                                     .rearrange("(g h) c -> h g c", h=S5H)).then_inc(x_in[b], 16)
            sp.wait_ge(gelu_ok, Q + 2)
            send(sp, 1)

        @block.gpsimd
        def _(pool):
            pool.sem_inc(w_ok, 2)
            with pool.Fori(0, Q // XB) as i:
                for b in range(XB):
                    q = i * XB + b
                    pool.wait_ge(out_mm, q + 1)
                    nc.gpsimd.tensor_copy(w[:, b, 0:2, :], wt[:, ds(q, 1)].rearrange("p a r m -> p (a r) m")
                                          ).then_inc(pool_chain, 1)
                    pool.wait_ge(pool_chain, q + 1)
                    step(pool, nc.gpsimd.tensor_copy(w[:, b, 2:4, :], ca[:, ds(q, 1), :, S5H:(J + 1) * S5H]
                                                     .rearrange("p a r m -> p (a r) m")), w_ok, q + 3)

        @block.tensor
        def _(pe):
            pe.sem_inc(in_mm, 2)
            pe.sem_inc(out_mm, XB)

            def states_in(q, a, nth):
                b = a % 2
                pe.wait_ge(x_in[a], nth * 16 * J)
                pe.wait_ge(w_ok, q + 3)
                pe.wait_ge(prod_ok, q + 1)
                for e in range(2):
                    for r in range(2):
                        last = nc.tensor.matmul(banks_in[e * S5P:(e + 1) * S5P, b, r, :], w[:, a, r, e * S5P:(e + 1) * S5P],
                                                x[:, a, e, :],
                                                start=r == 0, stop=True, skip_group_check=True)
                last.then_inc(in_mm, 1)

            def outputs(q, a):
                b = a % 2
                pe.wait_ge(kern_ok, q + 3)
                pe.wait_ge(gelu_ok, q + 1)
                for e in range(2):
                    nc.tensor.matmul(banks_out[:, b, e, 0:NCH], kern[:, a, e, :],
                                     x[:, a, e, :], start=True, stop=False)
                pe.wait_ge(before_ok, q + 3)
                for r in range(2):
                    for e in range(2):
                        lanes = slice(e * S5P, (e + 1) * S5P)
                        last = nc.tensor.matmul(banks_out[:, b, e, 0:NCH], w[lanes, a, 2 + r, :], before[lanes, b, r, :],
                                                start=False, stop=r == 1)
                last.then_inc(out_mm, 1)

            states_in(0, 0, 1)
            with pe.Fori(0, Q // XB - 1) as i:
                for a in range(XB):
                    states_in(i * XB + a + 1, (a + 1) % XB, i + 1 + (a + 1) // XB)
                    outputs(i * XB + a, a)
            for a in range(XB):
                if a < XB - 1:
                    states_in(Q - XB + a + 1, a + 1, Q // XB)
                outputs(Q - XB + a, a)

        @block.vector
        def _(dve):
            dve.sem_inc(prod_ok, 2)
            dve.sem_inc(before_ok, 2)
            chain = Chain(dve, dve_chain)
            tt = nc.vector.tensor_tensor
            chain(nc.vector.memset(before[:], 0.0))
            with dve.Fori(0, Q // 2) as i:
                chain.round(i, 2 * 9)
                for b in range(2):
                    q = i * 2 + b
                    pair = table[:, ds(q, 1)].rearrange("p a r c -> p (a r) c")
                    dve.wait_ge(in_mm, q + 3)
                    for r in range(2):
                        chain(tt(prod[:, 2 * r:2 * r + 2, :],
                                 banks_in[:, b, r, :].unsqueeze(1).to_broadcast([P, 2, NCH]), pair, ALU.mult))
                    dve.sem_inc(prod_ok, 1)
                    chain(tt(rot[:, 0, :], prod[:, 0, :], prod[:, 3, :], ALU.add))
                    chain(tt(rot[:, 1, :], prod[:, 2, :], prod[:, 1, :], ALU.subtract))
                    r8 = rho[:, ds(q, 1)].to_broadcast([P, NCH])
                    for r in range(2):
                        chain(nc.vector.tensor_tensor_scan(state[:, r, :], r8, rot[:, r, :], 0.0, ALU.mult, ALU.add))
                    for r in range(2):
                        chain(tt(prod2[:, 2 * r:2 * r + 2, :], state[:, r, :].unsqueeze(1).to_broadcast([P, 2, NCH]),
                                 pair, ALU.mult))
                    dve.wait_ge(out_mm, q + XB - 1)
                    n = NCH - 1
                    chain(tt(before[:, b, 0, 1:NCH], prod2[:, 0, 0:n], prod2[:, 3, 0:n], ALU.subtract))
                    step(dve, tt(before[:, b, 1, 1:NCH], prod2[:, 2, 0:n], prod2[:, 1, 0:n], ALU.add), before_ok, q + 3)
            chain.end(Q // 2)

        @block.scalar
        def _(act):
            act.sem_inc(gelu_ok, 2)
            act.sem_inc(kern_ok, 2)
            for j in range(J):
                act.dma_start(kern_all[j * S5H:(j + 1) * S5H],
                              kern_dram[:, :, (J - 1 - j) * S5H:(2 * J - 1 - j) * S5H].rearrange("g h m -> h g m")
                              ).then_inc(kern_in, 16)

            def kernels(q, a):
                act.wait_ge(out_mm, q + 1)
                step(act, nc.scalar.activation(kern[:, a], kern_all[:, ds(q * 2, 2), :], ACT.Copy), kern_ok, q + 3)

            def outputs(q, b):
                act.wait_ge(out_mm, q + XB + 1)
                step(act, nc.scalar.activation(y[:, ds(q * 2, 2), :], banks_out[:, b, :, 0:NCH], ACT.Gelu_apprx_tanh),
                     gelu_ok, q + 3)

            act.wait_ge(kern_in, 16 * J)
            kernels(0, 0)
            kernels(1, 1)
            with act.Fori(0, Q // XB - 1) as i:
                for a in range(XB):
                    kernels(i * XB + a + 2, (a + 2) % XB)
                    outputs(i * XB + a, a % 2)
            for a in range(XB):
                if a < XB - 2:
                    kernels(Q - XB + a + 2, a + 2)
                outputs(Q - XB + a, a % 2)
            send(act, 0)


def phase_s5_glu(nc, w_glu, b_glu, g_dram, yt_dram):
    with ExitStack() as ctx:
        sb, ps, sem = scope(nc, ctx)
        g, y = sb("u_g", [P, UT, T]), sb("u_y", [P, 2, T])
        wg, bg = sb("u_w", [P, UT, S5W]), sb("u_b", [P, UT])
        gate = sb("u_gate", [P, 2, NB])
        banks = ps("u_banks", [P, 2, NB])
        const_in, mm_ok, gate_ok, y_ok = (sem("u_" + s) for s in ("const_in", "mm_ok", "gate_ok", "y_ok"))
        sent = (sem("u_sent0"), sem("u_sent1"))
        block = ctx.enter_context(nc.Block())

        @block.sync
        def _(sp):
            sp.dma_start(wg[:], w_glu).then_inc(const_in, 16)
            sp.dma_start(bg[:], b_glu).then_inc(const_in, 16)
            for t in range(UT):
                sp.dma_start(g[:, t].rearrange("p (j c) -> p j c", j=J), g_dram[:, t * P:(t + 1) * P].rearrange("j p c -> p j c")
                             ).then_inc(const_in, 16)
            for m in range(UT):
                sp.wait_ge(y_ok, BLK * (m + 1))
                sp.dma_start(yt_dram[m], y[:, m % 2]).then_inc(sent[m % 2], 16)
            for b in range(2):
                sp.wait_ge(sent[b], 16 * UT // 2)

        @block.tensor
        def _(pe):
            pe.wait_ge(const_in, 16 * (2 + UT))
            for m in range(UT):
                for q in range(BLK):
                    n = m * BLK + q
                    if n >= 2:
                        pe.wait_ge(gate_ok, n - 1)
                    for k in range(UT):
                        last = nc.tensor.matmul(banks[:, n % 2, :], wg[:, k, m * P:(m + 1) * P],
                                                g[:, k, q * NB:(q + 1) * NB], start=k == 0, stop=k == UT - 1)
                    last.then_inc(mm_ok, 1)

        @block.scalar
        def _(act):
            for n in range(UT * BLK):
                m = n // BLK
                act.wait_ge(mm_ok, n + 1)
                if n >= 2:
                    act.wait_ge(y_ok, n - 1)
                step(act, nc.scalar.activation(gate[:, n % 2, :], banks[:, n % 2, :], ACT.Sigmoid, bias=bg[:, m:m + 1]),
                     gate_ok, n + 1)

        @block.vector
        def _(dve):
            per = NB // NCH
            for n in range(UT * BLK):
                m, q = n // BLK, n % BLK
                dve.wait_ge(gate_ok, n + 1)
                if q == 0 and m >= 2:
                    dve.wait_ge(sent[m % 2], 16 * (m // 2))
                step(dve, nc.vector.tensor_tensor(
                    y[:, m % 2].rearrange("p (c j) -> p j c", j=J)[:, q * per:(q + 1) * per, :],
                    g[:, m, q * NB:(q + 1) * NB].rearrange("p (j c) -> p j c", j=per),
                    gate[:, n % 2, :].rearrange("p (j c) -> p j c", j=per), ALU.mult), y_ok, n + 1)

CH0 = 6
B_T, C_T, K_T, Q_T = (0, 1), (2, 6), 3, 7
X_C, B_C, K_C = 0, XW, XW + NG * NS + NS
HG = HS // NG
GW = HG * HD
HP = HM // 2
DA = DV + 1
NT = (XW + VW) // P
LOADS = 5


def phase_mixers(nc, tok_cols, rows_dram, decay_dram, conv_dram, tok_dram, tokmaj_dram, ssd_skip, norm_gain, ident,
                 yt_dram):
    with ExitStack() as ctx:
        sb, ps, sem = scope(nc, ctx)
        ch = sb("m_ch", [P, 2, CT - CH0, P])
        tk = sb("m_tk", [P, 2, CTT * P])
        zo = sb("m_zo", [P, 2, XW + VW])
        va = sb("m_va", [P, 2, HM, DA])
        bc = sb("m_bc", [P, 2, NBC, P])
        decay = sb("m_decay", [P, HS, TT])
        decay_m = sb("m_decay_m", [P, HP, TT])
        skip, gain, ident_sb = sb("m_skip", [P, HS]), sb("m_gain", [P, XW // P]), sb("m_ident", [P, P])
        expo = sb("m_expo", [P, 2, NBC, P])
        xdt, xde, xskip = (sb("m_" + s, [P, HS, HD]) for s in ("xdt", "xde", "xskip"))
        ve = sb("m_ve", [P, HM, DA])
        off, y = sb("m_off", [P, HS, HD]), sb("m_y", [P, 2, XW + VW])
        sq = sb("m_sq", [P, GW])
        stat = sb("m_stat", [P, 4, NG])
        h_state, h_old = sb("m_h", [P, HS, HD]), sb("m_h_old", [P, HS, HD])
        c_state, c_old = sb("m_c", [P, HP, DA]), sb("m_c_old", [P, HP, DA])
        inter, num = sb("m_inter", [P, 2, HP, DA]), sb("m_num", [P, 2, HP, DA])
        den = sb("m_den", [P, 3, 2, HP])
        mask = sb("m_mask", [P, P])
        yt = sb("m_yt", [P, 2, NT, P])
        cb_bank, qk_banks, in_banks, off_banks, tr_bank = (
            ps("m_cb", [P, NB]), ps("m_qk", [P, 2, NB]), ps("m_in", [P, 2, NB]), ps("m_offb", [P, 2, NB]), ps("m_tr", [P, NB]))
        names = ("expo_ok", "mask_ok", "xde_ok", "xskip_ok", "ve_ok", "score_mm", "off_mm", "diag_mm", "state_mm",
                 "inter_mm", "pv_mm", "c_mm", "xdt_ok", "g_ok", "gm_ok", "off_read", "diag_read", "gated_ok", "h_ok",
                 "inter_read", "num_ok", "c_ok", "mean_ok", "ssq_ok", "rstd_ok", "y_ok")
        S = {n: sem("m_" + n) for n in names}
        (expo_ok, mask_ok, xde_ok, xskip_ok, ve_ok, score_mm, off_mm, diag_mm, state_mm, inter_mm, pv_mm, c_mm, xdt_ok,
         g_ok, gm_ok, off_read, diag_read, gated_ok, h_ok, inter_read, num_ok, c_ok, mean_ok, ssq_ok, rstd_ok,
         y_ok) = S.values()
        tr_ok, yt_ok = sem("m_tr_ok"), sem("m_yt_ok")
        const_in, in_, sent = sem("m_const_in"), (sem("m_in0"), sem("m_in1")), (sem("m_sent0"), sem("m_sent1"))
        dve_chain, act_chain, pool_chain, set_ok = (sem("m_" + s) for s in ("dve_chain", "act_chain", "pool_chain", "set_ok"))
        block = ctx.enter_context(nc.Block())

        def over(a, n):
            return a.unsqueeze(2).to_broadcast([P, a.shape[1], n])

        def col(c, k, first, n):
            return tok_cols[:, ds(c, 1), k, first:first + n].rearrange("p a n -> p (a n)")

        def col_eo(c, k):
            return col(c, k, FR, HM).rearrange("p (i e) -> p e i", e=2)

        def over_eo(a, n):
            return a.unsqueeze(3).to_broadcast([P, 2, HP, n])

        @block.sync
        def _(sp):
            for dst, src in ((skip[:], ssd_skip.partition_broadcast(P)), (gain[:], norm_gain), (ident_sb[:], ident),
                             (decay[:].rearrange("p h c -> p (h c)"),
                              decay_dram[0:HS].rearrange("h c -> (h c)").partition_broadcast(P))):
                sp.dma_start(dst, src).then_inc(const_in, 16)
            for e in range(2):
                sp.dma_start(decay_m[e * DK:(e + 1) * DK],
                             decay_dram[HS:NBC].rearrange("(i e) c -> e i c", e=2)[e].partition_broadcast(DK)
                             ).then_inc(const_in, 16)
            with sp.Fori(0, TT // 2) as i:
                for b in range(2):
                    c = i * 2 + b
                    sp.wait_ge(y_ok, c + 1)
                    tok = ds(c * P, P)
                    sp.dma_start(ch[:, b], conv_dram[CH0:CT, :, tok].rearrange("a p t -> p a t")).then_inc(in_[b], 16)
                    sp.dma_start(tk[:, b], tok_dram[tok, :]).then_inc(in_[b], 16)
                    sp.dma_start(bc[:, b].rearrange("p r t -> p (r t)"),
                                 rows_dram[ds(c, 1)].rearrange("a r t -> (a r t)").partition_broadcast(P)).then_inc(in_[b], 16)
                    sp.dma_start(va[:, b, :, 0:DV], tokmaj_dram[tok, XW + VW:].rearrange("t (h v) -> t h v", h=HM)
                                 ).then_inc(in_[b], 16)
                    sp.dma_start(zo[:, b], tokmaj_dram[tok, 0:XW + VW]).then_inc(in_[b], 16)

        @block.scalar
        def _(act):
            for s in (expo_ok, ssq_ok, rstd_ok):
                act.sem_inc(s, 2)
            for s in sent:
                act.sem_inc(s, 16)
            act.sem_inc(yt_ok, 1)
            chain = Chain(act, act_chain)
            rounds = TT // 2

            def exponentials(c, b, seen):
                act.wait_ge(in_[b], seen * 16 * LOADS)
                act.wait_ge(mask_ok, c + 3)
                act.wait_ge(pv_mm, c + 1)
                for h in range(HS):
                    ins = nc.scalar.activation(expo[:, b, h, :], bc[:, b, h, :], ACT.Exp, bias=col(c, 1, h, 1))
                for h in range(HM):
                    at = HS + h % 2 * HP + h // 2
                    ins = nc.scalar.activation(expo[:, b, at, :], bc[:, b, HS + h, :], ACT.Exp, bias=col(c, 0, FR + h, 1))
                ins.then_inc(expo_ok, 1)

            def norm(c, b):
                act.wait_ge(gated_ok, c + 3)
                for g in range(NG):
                    ins = nc.scalar.activation(sq[:], y[:, b, g * GW:(g + 1) * GW], ACT.Square,
                                               accum_out=stat[:, 0, g:g + 1])
                    if g < NG - 1:
                        chain(ins)
                    else:
                        step(act, ins, ssq_ok, c + 3)
                act.wait_ge(mean_ok, c + 3)
                chain(nc.scalar.activation(stat[:, 2, :], stat[:, 1, :], ACT.Ln))
                step(act, nc.scalar.activation(stat[:, 3, :], stat[:, 2, :], ACT.Exp, scale=-0.5), rstd_ok, c + 3)

            def out(c, b):
                for n in range(NT // 4):
                    act.wait_ge(tr_ok, c * 3 + n + 2)
                    if n == 0:
                        act.wait_ge(sent[b], (c - b) * 8 + 16)
                    for a in range(4):
                        t = n * 4 + a
                        g = gain[:, t:t + 1] if t < XW // P else 1.0
                        ins = nc.scalar.activation(yt[:, b, t, :], tr_bank[:, a * P:(a + 1) * P], ACT.Copy, scale=g)
                    step(act, ins, yt_ok, c * 3 + n + 2)
                act.dma_start(yt_dram[UT:, :, ds(c * P, P)].rearrange("a p t -> p a t"), yt[:, b]).then_inc(sent[b], 16)

            act.wait_ge(const_in, 16 * 6)
            exponentials(0, 0, 1)
            with act.Fori(0, rounds - 1) as i:
                chain.round(i, 4)
                for b in range(2):
                    c = i * 2 + b
                    exponentials(c + 1, 1 - b, i + 1 + b)
                    norm(c, b)
                    out(c, b)
            chain.end(rounds - 1)
            exponentials(TT - 1, 1, rounds)
            for b in range(2):
                norm(TT - 2 + b, b)
                out(TT - 2 + b, b)
            for b in range(2):
                act.wait_ge(sent[b], 16 * TT // 2 + 16)

        @block.gpsimd
        def _(pool):
            for s in (mask_ok, xde_ok, xskip_ok, ve_ok):
                pool.sem_inc(s, 2)
            step(pool, nc.gpsimd.memset(mask[:], 0.0), pool_chain, 1)
            step(pool, nc.gpsimd.affine_select(out=mask[:], in_=mask[:], compare_op=ALU.is_ge, fill=-1e30, base=0,
                                               pattern=[[1, P]], channel_multiplier=-1), pool_chain, 2)
            step(pool, nc.gpsimd.memset(va[:, :, :, DV:DA], 1.0), set_ok, 1)
            pool.wait_ge(const_in, 16 * 6)
            with pool.Fori(0, TT // 2) as i:
                for b in range(2):
                    c = i * 2 + b
                    pool.wait_ge(in_[b], (i + 1) * 16 * LOADS)
                    step(pool, nc.gpsimd.tensor_tensor(bc[:, b], bc[:, b], mask[:].unsqueeze(1).to_broadcast([P, NBC, P]),
                                                       ALU.add), mask_ok, c + 3)
                    x = tk[:, b, X_C:X_C + XW].rearrange("p (h d) -> p h d", h=HS)
                    pool.wait_ge(state_mm, c + 2)
                    step(pool, nc.gpsimd.tensor_tensor(xde[:], x, over(col(c, 3, 0, HS), HD), ALU.mult), xde_ok, c + 3)
                    pool.wait_ge(gated_ok, c + 2)
                    step(pool, nc.gpsimd.tensor_tensor(xskip[:], x, over(skip[:], HD), ALU.mult), xskip_ok, c + 3)
                    pool.wait_ge(c_mm, c + 2)
                    step(pool, nc.gpsimd.tensor_tensor(ve[:], va[:, b], over(col(c, 2, FR, HM), DA), ALU.mult),
                         ve_ok, c + 3)

        @block.vector
        def _(dve):
            for s in (xdt_ok, g_ok, gm_ok, off_read, diag_read, gated_ok, inter_read, num_ok, mean_ok, y_ok):
                dve.sem_inc(s, 2)
            chain = Chain(dve, dve_chain)
            tt = nc.vector.tensor_tensor
            mul, add = ALU.mult, ALU.add
            chain(nc.vector.memset(h_state[:], 0.0))
            chain(nc.vector.memset(c_state[:], 0.0))
            dve.sem_inc(h_ok, 2)
            dve.sem_inc(c_ok, 2)
            dve.wait_ge(const_in, 16 * 6)
            dve.wait_ge(set_ok, 1)
            with dve.Fori(0, TT // 2) as i:
                chain.round(i, 2 * 9)
                for b in range(2):
                    c = i * 2 + b
                    dve.wait_ge(in_[b], (i + 1) * 16 * LOADS)
                    x = tk[:, b, X_C:X_C + XW].rearrange("p (h d) -> p h d", h=HS)
                    dve.wait_ge(diag_mm, c + 2)
                    step(dve, tt(xdt[:], x, over(col(c, 0, 0, HS), HD), mul), xdt_ok, c + 3)
                    chain(tt(h_old[:], h_state[:], decay[:, :, ds(c, 1)].to_broadcast([P, HS, HD]), mul))
                    chain(tt(c_old[:], c_state[:], decay_m[:, :, ds(c, 1)].to_broadcast([P, HP, DA]), mul))
                    dve.wait_ge(score_mm, c + 3)
                    dve.wait_ge(expo_ok, c + 3)
                    for g in range(NG):
                        e = expo[:, b, g * HG:(g + 1) * HG, :]
                        ins = tt(e, e, cb_bank[:, g * P:(g + 1) * P].unsqueeze(1).to_broadcast([P, HG, P]), mul)
                        if g < NG - 1:
                            chain(ins)
                        else:
                            step(dve, ins, g_ok, c + 3)
                    e = expo[:, b, HS:, :].rearrange("p (e i) t -> p e (i t)", e=2)
                    step(dve, nc.vector.scalar_tensor_tensor(e, e, DK ** -0.5, qk_banks[:, :, 0:HP * P], mul, mul),
                         gm_ok, c + 3)
                    dve.wait_ge(off_mm, c + 3)
                    o4 = off[:].rearrange("p (g h) d -> p g h d", g=NG)
                    f4 = col(c, 2, 0, HS).rearrange("p (g h) -> p g h", g=NG).unsqueeze(3).to_broadcast([P, NG, HG, HD])
                    step(dve, tt(o4, off_banks[:, :, 0:GW].rearrange("p g (h d) -> p g h d", h=HG), f4, mul),
                         off_read, c + 3)
                    dve.wait_ge(diag_mm, c + 3)
                    yg = y[:, b, 0:XW].rearrange("p (g m) -> p g m", g=NG)
                    dve.wait_ge(tr_ok, c * 3 - b * 3 + 1)
                    step(dve, tt(yg, in_banks[:, :, 0:GW], off[:].rearrange("p (g h) d -> p g (h d)", g=NG), add),
                         diag_read, c + 3)
                    dve.wait_ge(xskip_ok, c + 3)
                    chain(tt(y[:, b, 0:XW], y[:, b, 0:XW], xskip[:].rearrange("p h d -> p (h d)"), add))
                    step(dve, tt(y[:, b, 0:XW], y[:, b, 0:XW], zo[:, b, 0:XW], mul), gated_ok, c + 3)
                    dve.wait_ge(state_mm, c + 3)
                    step(dve, tt(h_state[:].rearrange("p (g h) d -> p g (h d)", g=NG),
                                 h_old[:].rearrange("p (g h) d -> p g (h d)", g=NG), qk_banks[:, :, 0:GW], add), h_ok, c + 3)
                    dve.wait_ge(inter_mm, c + 3)
                    step(dve, tt(inter[:], off_banks[:, :, 0:HP * DA].rearrange("p e (i v) -> p e i v", i=HP),
                                 over_eo(col_eo(c, 1), DA), mul), inter_read, c + 3)
                    dve.wait_ge(pv_mm, c + 3)
                    step(dve, tt(num[:], in_banks[:, :, 0:HP * DA].rearrange("p e (i v) -> p e i v", i=HP), inter[:], add),
                         num_ok, c + 3)
                    dve.wait_ge(c_mm, c + 3)
                    step(dve, tt(c_state[:], c_old[:], cb_bank[:, 0:HP * DA].rearrange("p (i v) -> p i v", i=HP), add),
                         c_ok, c + 3)
                    dve.wait_ge(ssq_ok, c + 3)
                    step(dve, nc.vector.tensor_scalar(stat[:, 1, :], stat[:, 0, :], 1.0 / GW, EPS, mul, add), mean_ok, c + 3)
                    d = num[:, :, :, DV]
                    chain(nc.vector.scalar_tensor_tensor(den[:, 0], d, -1.0, d, mul, ALU.max))
                    chain(tt(den[:, 1], den[:, 0], col_eo(c, 3), ALU.max))
                    chain(nc.vector.reciprocal(den[:, 2], den[:, 1]))
                    chain(tt(num[:], num[:], over_eo(den[:, 2], DA), mul))
                    chain(tt(y[:, b, XW:].rearrange("p (i e v) -> p e i v", e=2, i=HP), num[:, :, :, 0:DV],
                             zo[:, b, XW:].rearrange("p (i e v) -> p e i v", e=2, i=HP), mul))
                    dve.wait_ge(rstd_ok, c + 3)
                    step(dve, tt(yg, yg, over(stat[:, 3, :], GW), mul), y_ok, c + 3)
            chain.end(TT // 2)

        @block.tensor
        def _(pe):
            for s in (score_mm, off_mm, diag_mm, state_mm, inter_mm, pv_mm, c_mm):
                pe.sem_inc(s, 2)
            pe.sem_inc(tr_ok, 1)
            mm = nc.tensor.matmul
            pe.wait_ge(const_in, 16 * 6)

            def scores(c, b, seen):
                pe.wait_ge(in_[b], seen * 16 * LOADS)
                pe.wait_ge(c_ok, c + 2)
                for g in range(NG):
                    mm(cb_bank[:, g * P:(g + 1) * P], ch[:, b, B_T[g], :], ch[:, b, C_T[g], :], start=True, stop=True)
                pe.wait_ge(h_ok, c + 2)
                for i in range(HP):
                    for e in range(2):
                        rows = slice(e * DK, (e + 1) * DK)
                        last = mm(qk_banks[:, e, i * P:(i + 1) * P], ch[rows, b, K_T + i, :], ch[rows, b, Q_T + i, :],
                                  start=True, stop=True)
                last.then_inc(score_mm, 1)
                pe.wait_ge(inter_read, c + 2)
                for g in range(NG):
                    last = mm(off_banks[:, g, 0:GW], ch[:, b, C_T[g], :],
                              h_state[:].rearrange("p h d -> p (h d)")[:, g * GW:(g + 1) * GW], start=True, stop=True)
                last.then_inc(off_mm, 1)

            def rest(c, b):
                pe.wait_ge(num_ok, c + 2)
                pe.wait_ge(g_ok, c + 3)
                for h in range(HS):
                    last = mm(in_banks[:, h // HG, h % HG * HD:(h % HG + 1) * HD], expo[:, b, h, :], xdt[:, h, :],
                              start=True, stop=True)
                last.then_inc(diag_mm, 1)
                pe.wait_ge(gm_ok, c + 3)
                pe.wait_ge(xde_ok, c + 3)
                for g in range(NG):
                    last = mm(qk_banks[:, g, 0:GW], tk[:, b, B_C + g * NS:B_C + (g + 1) * NS],
                              xde[:].rearrange("p h d -> p (h d)")[:, g * GW:(g + 1) * GW], start=True, stop=True)
                last.then_inc(state_mm, 1)
                pe.wait_ge(off_read, c + 3)
                for i in range(HP):
                    for e in range(2):
                        rows = slice(e * DK, (e + 1) * DK)
                        last = mm(off_banks[:, e, i * DA:(i + 1) * DA], ch[rows, b, Q_T + i, :], c_state[rows, i, :],
                                  start=True, stop=True)
                last.then_inc(inter_mm, 1)
                pe.wait_ge(diag_read, c + 3)
                for h in range(HM):
                    e, i = h % 2, h // 2
                    last = mm(in_banks[:, e, i * DA:(i + 1) * DA], expo[:, b, HS + e * HP + i, :], va[:, b, h, :],
                              start=True, stop=True)
                last.then_inc(pv_mm, 1)
                pe.wait_ge(ve_ok, c + 3)
                for h in range(HM):
                    e, i = h % 2, h // 2
                    last = mm(cb_bank[e * DK:(e + 1) * DK, i * DA:(i + 1) * DA], tk[:, b, K_C + h * DK:K_C + (h + 1) * DK],
                              ve[:, h, :], start=True, stop=True)
                last.then_inc(c_mm, 1)

            def transposes(c, b):
                pe.wait_ge(y_ok, c + 3)
                for n in range(NT // 4):
                    pe.wait_ge(yt_ok, c * 3 + n + 1)
                    for a in range(4):
                        t = n * 4 + a
                        last = nc.tensor.transpose(tr_bank[:, a * P:(a + 1) * P], y[:, b, t * P:(t + 1) * P], ident_sb[:])
                    last.then_inc(tr_ok, 1)

            scores(0, 0, 1)
            rest(0, 0)
            with pe.Fori(0, TT // 2 - 1) as i:
                for b in range(2):
                    c = i * 2 + b + 1
                    scores(c, 1 - b, i + 1 + b)
                    transposes(c - 1, b)
                    rest(c, 1 - b)
            scores(TT - 1, 1, TT // 2)
            transposes(TT - 2, 0)
            rest(TT - 1, 1)
            transposes(TT - 1, 1)

KM = DMIX // P
FG = 6


def phase_out(nc, x, w_out, gain_mix, gain_ffn, ident, yt_dram, x1_dram, h2_dram):
    x_tiles = x[0].rearrange("(n p) d -> n p d", p=P)
    with ExitStack() as ctx:
        sb, ps, sem = scope(nc, ctx)
        WB = 4
        w_hi, w_lo = sb("o_w_hi", [P, KM, D], F32R), sb("o_w_lo", [P, KM, D], F32R)
        raw = sb("o_raw", [P, WB, D])
        y_raw = sb("o_y_raw", [P, KM, P])
        y_hi, y_lo = sb("o_y_hi", [P, 2, KM, P], F32R), sb("o_y_lo", [P, 2, KM, P], F32R)
        xt, x1 = sb("o_x", [P, D]), sb("o_x1", [P, D])
        work, ht = sb("o_work", [P, D]), sb("o_ht", [P, KD, P])
        gain_row, gain_col = sb("o_gain_row", [P, D]), sb("o_gain_col", [P, KD])
        ident_sb, stat = sb("o_ident", [P, P]), sb("o_stat", [P, 8])
        banks, tr_banks = ps("o_banks", [P, 2, 2, NB]), ps("o_tr", [P, 2, NB])
        const_in, wraw_in = sem("o_const_in"), tuple(sem("o_wraw_in%d" % b) for b in range(WB))
        whi_ok, wlo_ok, y_in, x_in, x1_sent, h_sent, act_chain, dve_chain = (
            sem("o_" + s) for s in ("whi_ok", "wlo_ok", "y_in", "x_in", "x1_sent", "h_sent", "act_chain", "dve_chain"))
        yhi_ok, ylo_ok, mm_ok, ssq_ok, mean_ok, rstd_ok, x1_ok, ssq2_ok, mean2_ok, rstd2_ok, xn_ok, tr_ok, ht_ok, add_ok = (
            sem("o_" + s) for s in ("yhi_ok", "ylo_ok", "mm_ok", "ssq_ok", "mean_ok", "rstd_ok", "x1_ok", "ssq2_ok",
                                    "mean2_ok", "rstd2_ok", "xn_ok", "tr_ok", "ht_ok", "add_ok"))
        x1_free, h_free = sem("o_x1_free"), sem("o_h_free")
        block = ctx.enter_context(nc.Block())

        @block.sync
        def _(sp):
            for dst, src in ((gain_row[:], gain_mix.partition_broadcast(P)), (gain_col[:], gain_ffn), (ident_sb[:], ident)):
                sp.dma_start(dst, src).then_inc(const_in, 16)
            def load(n):
                sp.wait_ge(ylo_ok, n + 2)
                sp.dma_start(y_raw[:], yt_dram[:, :, ds(n * P, P)].rearrange("a p t -> p a t")).then_inc(y_in, 16)

            load(0)
            for k in range(KM):
                if k >= WB:
                    sp.wait_ge(wlo_ok, k - WB + 1)
                sp.dma_start(raw[:, k % WB, :], w_out[k * P:(k + 1) * P, :]).then_inc(wraw_in[k % WB], 16)
            with sp.Fori(0, TT - 1) as i:
                load(i + 1)

        @block.gpsimd
        def _(pool):
            pool.sem_inc(x1_free, 1)
            pool.sem_inc(h_free, 1)
            with pool.Fori(0, TT) as n:
                pool.wait_ge(add_ok, n + 2)
                pool.dma_start(xt[:], x_tiles[ds(n, 1)].rearrange("a p d -> (a p) d")).then_inc(x_in, 16)
                pool.wait_ge(x1_ok, n + 3)
                arrived(pool, pool.dma_start(x1_dram[ds(n * P, P), :], x1[:]), x1_sent, n * 16 + 16, x1_free)
                pool.wait_ge(ht_ok, n + 3)
                arrived(pool, pool.dma_start(h2_dram[:, :, ds(n * P, P)].rearrange("a p t -> p a t"), ht[:]),
                        h_sent, n * 16 + 16, h_free)
            pool.wait_ge(x1_sent, 16 * TT)
            pool.wait_ge(h_sent, 16 * TT)

        @block.scalar
        def _(act):
            for s in (yhi_ok, ssq_ok, rstd_ok, ssq2_ok, rstd2_ok, ht_ok):
                act.sem_inc(s, 2)
            chain = Chain(act, act_chain)
            act.wait_ge(const_in, 48)

            def upper(n, b):
                act.wait_ge(y_in, n * 16 + 16)
                act.wait_ge(mm_ok, n + 1)
                step(act, nc.scalar.activation(y_hi[:, b], y_raw[:], ACT.Copy), yhi_ok, n + 3)

            def norm(src, dst, ok, mean, rstd, n):
                step(act, nc.scalar.activation(work[:], src, ACT.Square, accum_out=stat[:, dst:dst + 1]), ok, n + 3)
                act.wait_ge(mean, n + 3)
                chain(nc.scalar.activation(stat[:, dst + 2:dst + 3], stat[:, dst + 1:dst + 2], ACT.Ln))
                step(act, nc.scalar.activation(stat[:, dst + 2:dst + 3], stat[:, dst + 2:dst + 3], ACT.Exp, scale=-0.5),
                     rstd, n + 3)

            def tile(n, b):
                act.wait_ge(mm_ok, n + 3)
                act.wait_ge(tr_ok, n + 2)
                norm(banks[:, b].rearrange("p a m -> p (a m)"), 0, ssq_ok, mean_ok, rstd_ok, n)
                act.wait_ge(x1_ok, n + 3)
                norm(x1[:], 3, ssq2_ok, mean2_ok, rstd2_ok, n)
                act.wait_ge(tr_ok, n + 3)
                act.wait_ge(h_free, n + 1)
                for k in range(KD):
                    ins = nc.scalar.activation(ht[:, k, :], tr_banks[:, k // 4, k % 4 * P:(k % 4 + 1) * P], ACT.Copy,
                                               scale=gain_col[:, k:k + 1])
                step(act, ins, ht_ok, n + 3)

            upper(0, 0)
            for k in range(KM):
                act.wait_ge(wraw_in[k % WB], (k // WB + 1) * 16)
                step(act, nc.scalar.activation(w_hi[:, k, :], raw[:, k % WB, :], ACT.Copy), whi_ok, k + 1)
            upper(1, 1)
            with act.Fori(0, TT // 2 - 1) as i:
                chain.round(i, 4)
                for b in range(2):
                    n = i * 2 + b
                    upper(n + 2, b)
                    tile(n, b)
            chain.end(TT // 2 - 1)
            tile(TT - 2, 0)
            tile(TT - 1, 1)

        @block.vector
        def _(dve):
            for s in (ylo_ok, mean_ok, x1_ok, mean2_ok, xn_ok, add_ok):
                dve.sem_inc(s, 2)
            chain = Chain(dve, dve_chain)
            tt, ts = nc.vector.tensor_tensor, nc.vector.tensor_scalar
            dve.wait_ge(const_in, 48)

            def lower(n, b):
                dve.wait_ge(yhi_ok, n + 3)
                step(dve, tt(y_lo[:, b], y_raw[:], y_hi[:, b].bitcast(F32), ALU.subtract), ylo_ok, n + 3)

            def tile(n, b):
                dve.wait_ge(ssq_ok, n + 3)
                step(dve, ts(stat[:, 1:2], stat[:, 0:1], 1.0 / D, EPS, ALU.mult, ALU.add), mean_ok, n + 3)
                dve.wait_ge(rstd_ok, n + 3)
                chain(nc.vector.scalar_tensor_tensor(work[:], banks[:, b].rearrange("p a m -> p (a m)"), stat[:, 2:3],
                                                     gain_row[:], ALU.mult, ALU.mult))
                dve.wait_ge(x_in, n * 16 + 16)
                dve.wait_ge(x1_free, n + 1)
                step(dve, tt(x1[:], work[:], xt[:], ALU.add), x1_ok, n + 3)
                dve.sem_inc(add_ok, 1)
                dve.wait_ge(ssq2_ok, n + 3)
                step(dve, ts(stat[:, 4:5], stat[:, 3:4], 1.0 / D, EPS, ALU.mult, ALU.add), mean2_ok, n + 3)
                dve.wait_ge(rstd2_ok, n + 3)
                step(dve, ts(work[:], x1[:], stat[:, 5:6], None, ALU.mult), xn_ok, n + 3)

            lower(0, 0)
            for k in range(KM):
                dve.wait_ge(whi_ok, k + 1)
                step(dve, tt(w_lo[:, k, :], raw[:, k % WB, :], w_hi[:, k, :].bitcast(F32), ALU.subtract), wlo_ok, k + 1)
            lower(1, 1)
            with dve.Fori(0, TT // 2 - 1) as i:
                chain.round(i, 2)
                for b in range(2):
                    n = i * 2 + b
                    lower(n + 2, b)
                    tile(n, b)
            chain.end(TT // 2 - 1)
            tile(TT - 2, 0)
            tile(TT - 1, 1)

        @block.tensor
        def _(pe):
            pe.sem_inc(mm_ok, 2)
            pe.sem_inc(tr_ok, 2)
            pe.wait_ge(const_in, 48)

            def products(n, b):
                pe.wait_ge(ylo_ok, n + 3)
                pe.wait_ge(x1_ok, n + 1)
                for half in range(2):
                    cols = slice(half * NB, (half + 1) * NB)
                    for k in range(KM):
                        if half == 0:
                            pe.wait_ge(wlo_ok, k + 1)
                        for j, (y, w) in enumerate(((y_hi, w_hi), (y_lo, w_hi), (y_hi, w_lo))):
                            last = nc.tensor.matmul(banks[:, b, half, :], y[:, b, k, :], w[:, k, cols],
                                                    start=k == 0 and j == 0, stop=k == KM - 1 and j == 2)
                last.then_inc(mm_ok, 1)

            def transposes(n):
                pe.wait_ge(xn_ok, n + 3)
                pe.wait_ge(ht_ok, n + 2)
                for k in range(KD):
                    last = nc.tensor.transpose(tr_banks[:, k // 4, k % 4 * P:(k % 4 + 1) * P],
                                               work[:, k * P:(k + 1) * P], ident_sb[:])
                last.then_inc(tr_ok, 1)

            products(0, 0)
            with pe.Fori(0, TT // 2 - 1) as i:
                for b in range(2):
                    products(i * 2 + b + 1, 1 - b)
                    transposes(i * 2 + b)
            products(TT - 1, 1)
            transposes(TT - 2)
            transposes(TT - 1)


def phase_ffn_up(nc, w_gu, h2_dram, a_dram):
    with ExitStack() as ctx:
        sb, ps, sem = scope(nc, ctx)
        h_hi, h_lo = sb("f_h_hi", [P, KD, T], F32R), sb("f_h_lo", [P, KD, T], F32R)
        w_raw = sb("f_w_raw", [P, 2, KD, P])
        w_hi, w_lo = sb("f_w_hi", [P, 2, 2, KD, P], F32R), sb("f_w_lo", [P, 2, 2, KD, P], F32R)
        gate, a = sb("f_gate", [P, 2, NB]), sb("f_a", [P, 2, T])
        banks = ps("f_banks", [P, 2, 2, NB])
        h_in, w_in = (sem("f_h_in0"), sem("f_h_in1")), sem("f_w_in")
        sent = (sem("f_sent0"), sem("f_sent1"))
        free = (sem("f_free0"), sem("f_free1"))
        hhi_ok, hlo_ok = sem("f_hhi_ok"), sem("f_hlo_ok")
        whi_ok, wlo_ok, mm_ok, gate_ok, a_ok = (sem("f_" + s) for s in ("whi_ok", "wlo_ok", "mm_ok", "gate_ok", "a_ok"))
        block = ctx.enter_context(nc.Block())
        HB = 2 * BLK
        HW = T // HB
        h_raw = a[:].rearrange("p b (k t) -> p b k t", k=KD)

        @block.sync
        def _(sp):
            for m in range(HB):
                if m >= 2:
                    sp.wait_ge(hlo_ok, m - 1)
                sp.dma_start(h_raw[:, m % 2], h2_dram[:, :, m * HW:(m + 1) * HW].rearrange("k p t -> p k t")
                             ).then_inc(h_in[m % 2], 16)
                if m == 0:
                    sp.dma_start(w_raw[:].rearrange("p g k m -> p (g k m)"), w_gu[0]).then_inc(w_in, 16)
            with sp.Fori(0, FT - 1) as i:
                n = i + 1
                sp.wait_ge(wlo_ok, n + 2)
                sp.dma_start(w_raw[:].rearrange("p g k m -> p (g k m)"), w_gu[ds(n, 1)].rearrange("a p m -> (a p) m")
                             ).then_inc(w_in, 16)

        @block.gpsimd
        def _(pool):
            for s in free:
                pool.sem_inc(s, 1)
            with pool.Fori(0, FT // 2) as i:
                for b in range(2):
                    n = i * 2 + b
                    pool.wait_ge(a_ok, n * BLK + BLK + 2)
                    arrived(pool, pool.dma_start(a_dram[ds(n, 1)].rearrange("a p t -> (a p) t"), a[:, b, :]),
                            sent[b], i * 16 + 16, free[b])
            for b in range(2):
                pool.wait_ge(sent[b], 16 * FT // 2)

        @block.scalar
        def _(act):
            act.sem_inc(whi_ok, 2)
            act.sem_inc(gate_ok, 2)

            def upper_h(m):
                act.wait_ge(h_in[m % 2], (m // 2 + 1) * 16)
                step(act, nc.scalar.activation(h_hi[:, :, m * HW:(m + 1) * HW], h_raw[:, m % 2], ACT.Copy), hhi_ok, m + 1)

            def upper(n, b, first=False):
                act.wait_ge(w_in, n * 16 + 16)
                if not first:
                    act.wait_ge(mm_ok, n * BLK - BLK + 2)
                step(act, nc.scalar.activation(w_hi[:, b], w_raw[:], ACT.Copy), whi_ok, n + 3)

            def tile(n, b):
                for q in range(BLK):
                    m = n * BLK + q
                    act.wait_ge(mm_ok, m + 3)
                    act.wait_ge(a_ok, m + 1)
                    step(act, nc.scalar.activation(gate[:, q % 2, :], banks[:, q % 2, 0, :], ACT.Silu), gate_ok, m + 3)

            upper_h(0)
            upper(0, 0, True)
            for m in range(1, HB):
                upper_h(m)
            with act.Fori(0, FT // 2 - 1) as i:
                for b in range(2):
                    upper(i * 2 + b + 1, 1 - b)
                    tile(i * 2 + b, b)
            upper(FT - 1, 1)
            tile(FT - 2, 0)
            tile(FT - 1, 1)

        @block.vector
        def _(dve):
            dve.sem_inc(a_ok, 2)
            dve.sem_inc(wlo_ok, 2)

            def lower_h(m):
                part = slice(m * HW, (m + 1) * HW)
                dve.wait_ge(hhi_ok, m + 1)
                step(dve, nc.vector.tensor_tensor(h_lo[:, :, part], h_raw[:, m % 2], h_hi[:, :, part].bitcast(F32),
                                                  ALU.subtract), hlo_ok, m + 1)

            def lower(n, b):
                dve.wait_ge(whi_ok, n + 3)
                step(dve, nc.vector.tensor_tensor(w_lo[:, b], w_raw[:], w_hi[:, b].bitcast(F32), ALU.subtract),
                     wlo_ok, n + 3)

            def tile(n, b, nth):
                for q in range(BLK):
                    m = n * BLK + q
                    dve.wait_ge(gate_ok, m + 3)
                    if q == 0:
                        dve.wait_ge(free[b], nth + 1)
                    step(dve, nc.vector.tensor_tensor(a[:, b, q * NB:(q + 1) * NB], gate[:, q % 2, :],
                                                      banks[:, q % 2, 1, :], ALU.mult), a_ok, m + 3)

            lower_h(0)
            lower(0, 0)
            for m in range(1, HB):
                lower_h(m)
            with dve.Fori(0, FT // 2 - 1) as i:
                for b in range(2):
                    lower(i * 2 + b + 1, 1 - b)
                    tile(i * 2 + b, b, i)
            lower(FT - 1, 1)
            tile(FT - 2, 0, FT // 2 - 1)
            tile(FT - 1, 1, FT // 2 - 1)

        @block.tensor
        def _(pe):
            pe.sem_inc(mm_ok, 2)
            with pe.Fori(0, FT // 2) as i:
                for b in range(2):
                    n = i * 2 + b
                    pe.wait_ge(wlo_ok, n + 3)
                    for q in range(BLK):
                        pe.wait_ge(hlo_ok, 2 * (q + 1))
                        pe.wait_ge(a_ok, n * BLK + q + 1)
                        for g in range(2):
                            for k in range(KD):
                                for j, (w, h) in enumerate(((w_hi, h_hi), (w_hi, h_lo), (w_lo, h_hi))):
                                    last = nc.tensor.matmul(banks[:, q % 2, g, :], w[:, b, g, k, :],
                                                            h[:, k, q * NB:(q + 1) * NB],
                                                            start=k == 0 and j == 0, stop=k == KD - 1 and j == 2)
                        last.then_inc(mm_ok, 1)


def phase_ffn_down(nc, w_down, gain_post, a_dram, x1_dram, first_dram, out):
    out_tiles = out[0].rearrange("(n p) d -> n p d", p=P)
    with ExitStack() as ctx:
        sb, ps, sem = scope(nc, ctx)
        GROUPS = [slice(a, min(a + FG, FT)) for a in range(0, FT, FG)]
        NGR = len(GROUPS)
        w_raw = sb("d_w_raw", [P, FT, NB])
        w_hi, w_lo = sb("d_w_hi", [P, FT, NB], F32R), sb("d_w_lo", [P, FT, NB], F32R)
        a_raw = sb("d_a_raw", [P, FT, P])
        a_hi, a_lo = sb("d_a_hi", [P, 2, FT, P], F32R), sb("d_a_lo", [P, 2, FT, P], F32R)
        first = sb("d_first", [P, NB])
        x1, res, work = sb("d_x1", [P, D]), sb("d_res", [P, D]), sb("d_work", [P, D])
        gain_row, ssq, stat = sb("d_gain", [P, D]), sb("d_ssq", [P, TT, 1]), sb("d_stat", [P, 4])
        banks = ps("d_banks", [P, 2, NB])
        const_in, w_in = sem("d_const_in"), tuple(sem("d_w_in%d" % g) for g in range(len(GROUPS)))
        whi_ok, wlo_ok, a_in, x_in, sent, act_chain, dve_chain = (
            sem("d_" + s) for s in ("whi_ok", "wlo_ok", "a_in", "x_in", "sent", "act_chain", "dve_chain"))
        ahi_ok, alo_ok, mm_ok, copy_ok, ssq2_ok, mean_ok, rstd_ok, res_ok = (
            sem("d_" + s) for s in ("ahi_ok", "alo_ok", "mm_ok", "copy_ok", "ssq2_ok", "mean_ok", "rstd_ok", "res_ok"))
        first_out = sem("d_first_out")
        first_free, free = sem("d_first_free"), sem("d_free")
        block = ctx.enter_context(nc.Block())
        w_tiles = w_down.rearrange("(k p) m -> p k m", p=P)

        @block.sync
        def _(sp):
            sp.dma_start(gain_row[:], gain_post.partition_broadcast(P)).then_inc(const_in, 16)

            def load_a(t, n):
                sp.wait_ge(alo_ok, n + 2)
                sp.dma_start(a_raw[:], a_dram[:, :, ds(t * P, P)].rearrange("a p t -> p a t")).then_inc(a_in, 16)

            def load_weights(half):
                for g, ks in enumerate(GROUPS):
                    if half:
                        sp.wait_ge(wlo_ok, g + 1)
                    sp.dma_start(w_raw[:, ks, :], w_tiles[:, ks, half * NB:(half + 1) * NB]).then_inc(w_in[g], 16)

            load_a(0, 0)
            load_weights(0)
            load_a(1, 1)
            load_weights(1)
            with sp.Fori(0, TT - 2) as i:
                load_a(i + 2, i + 2)
            with sp.Fori(0, TT) as t:
                load_a(t, t + TT)

        @block.gpsimd
        def _(pool):
            pool.sem_inc(first_free, 1)
            pool.sem_inc(free, 1)
            with pool.Fori(0, TT) as t:
                pool.wait_ge(copy_ok, t + 3)
                arrived(pool, pool.dma_start(first_dram[ds(t * P, P), :], res[:, 0:NB]), first_out, t * 16 + 16, first_free)
            pool.wait_ge(first_out, 16 * TT)
            with pool.Fori(0, TT) as t:
                pool.wait_ge(res_ok, t + 2)
                pool.dma_start(x1[:], x1_dram[ds(t * P, P), :]).then_inc(x_in, 16)
                pool.dma_start(first[:], first_dram[ds(t * P, P), :]).then_inc(x_in, 16)
                pool.wait_ge(res_ok, t + 3)
                arrived(pool, pool.dma_start(out_tiles[ds(t, 1)].rearrange("a p d -> (a p) d"), res[:]),
                        sent, t * 16 + 16, free)
            pool.wait_ge(sent, 16 * TT)

        @block.scalar
        def _(act):
            for s in (ahi_ok, copy_ok, ssq2_ok, rstd_ok):
                act.sem_inc(s, 2)
            chain = Chain(act, act_chain)

            def upper(n, b):
                act.wait_ge(a_in, n * 16 + 16)
                act.wait_ge(mm_ok, n + 1)
                step(act, nc.scalar.activation(a_hi[:, b], a_raw[:], ACT.Copy), ahi_ok, n + 3)

            def weights(half):
                for g, ks in enumerate(GROUPS):
                    act.wait_ge(w_in[g], (half + 1) * 16)
                    step(act, nc.scalar.activation(w_hi[:, ks, :], w_raw[:, ks, :], ACT.Copy), whi_ok, half * NGR + g + 1)

            def tile(n, t, b, half):
                act.wait_ge(mm_ok, n + 3)
                if half == 0:
                    act.wait_ge(first_free, t + 1)
                    chain(nc.scalar.activation(res[:, 0:NB], banks[:, b, :], ACT.Copy))
                    step(act, nc.scalar.activation(work[:, 0:NB], banks[:, b, :], ACT.Square,
                                                   accum_out=ssq[:, ds(t, 1), :].rearrange("p a m -> p (a m)")),
                         copy_ok, n + 3)
                else:
                    step(act, nc.scalar.activation(work[:, 0:NB], banks[:, b, :], ACT.Square, accum_out=stat[:, 0:1]),
                         ssq2_ok, t + 3)
                    act.wait_ge(mean_ok, t + 3)
                    chain(nc.scalar.activation(stat[:, 2:3], stat[:, 1:2], ACT.Ln))
                    step(act, nc.scalar.activation(stat[:, 3:4], stat[:, 2:3], ACT.Exp, scale=-0.5), rstd_ok, t + 3)
                    act.wait_ge(res_ok, t + 3)

            upper(0, 0)
            weights(0)
            upper(1, 1)
            with act.Fori(0, TT // 2) as i:
                chain.round(i, 2)
                for b in range(2):
                    upper(i * 2 + b + 2, b)
                    tile(i * 2 + b, i * 2 + b, b, 0)
            chain.end(TT // 2)
            weights(1)
            with act.Fori(0, TT // 2 - 1) as i:
                chain.round(i, 2)
                for b in range(2):
                    upper(i * 2 + b + TT + 2, b)
                    tile(i * 2 + b + TT, i * 2 + b, b, 1)
            chain.end(TT // 2 - 1)
            tile(2 * TT - 2, TT - 2, 0, 1)
            tile(2 * TT - 1, TT - 1, 1, 1)

        @block.vector
        def _(dve):
            for s in (alo_ok, mean_ok, res_ok):
                dve.sem_inc(s, 2)
            chain = Chain(dve, dve_chain)
            dve.wait_ge(const_in, 16)

            def lower(n, b):
                dve.wait_ge(ahi_ok, n + 3)
                step(dve, nc.vector.tensor_tensor(a_lo[:, b], a_raw[:], a_hi[:, b].bitcast(F32), ALU.subtract),
                     alo_ok, n + 3)

            def tile(t, b):
                dve.wait_ge(ssq2_ok, t + 3)
                chain(nc.vector.tensor_tensor(stat[:, 1:2], stat[:, 0:1], ssq[:, ds(t, 1), :].rearrange("p a m -> p (a m)"),
                                              ALU.add))
                step(dve, nc.vector.tensor_scalar(stat[:, 1:2], stat[:, 1:2], 1.0 / D, EPS, ALU.mult, ALU.add),
                     mean_ok, t + 3)
                dve.wait_ge(rstd_ok, t + 3)
                dve.wait_ge(x_in, t * 32 + 32)
                for half, f in enumerate((first[:], banks[:, b, :])):
                    cols = slice(half * NB, (half + 1) * NB)
                    chain(nc.vector.scalar_tensor_tensor(work[:, cols], f, stat[:, 3:4], gain_row[:, cols],
                                                         ALU.mult, ALU.mult))
                dve.wait_ge(free, t + 1)
                step(dve, nc.vector.tensor_tensor(res[:], work[:], x1[:], ALU.add), res_ok, t + 3)

            def weights(half):
                for g, ks in enumerate(GROUPS):
                    dve.wait_ge(whi_ok, half * NGR + g + 1)
                    step(dve, nc.vector.tensor_tensor(w_lo[:, ks, :], w_raw[:, ks, :], w_hi[:, ks, :].bitcast(F32),
                                                      ALU.subtract), wlo_ok, half * NGR + g + 1)

            lower(0, 0)
            weights(0)
            lower(1, 1)
            with dve.Fori(0, TT // 2) as i:
                for b in range(2):
                    lower(i * 2 + b + 2, b)
            weights(1)
            with dve.Fori(0, TT // 2 - 1) as i:
                chain.round(i, 6)
                for b in range(2):
                    lower(i * 2 + b + TT + 2, b)
                    tile(i * 2 + b, b)
            chain.end(TT // 2 - 1)
            tile(TT - 2, 0)
            tile(TT - 1, 1)

        @block.tensor
        def _(pe):
            pe.sem_inc(mm_ok, 2)
            for half in range(2):
                with pe.Fori(0, TT // 2) as i:
                    for b in range(2):
                        t = i * 2 + b
                        n = t + half * TT
                        pe.wait_ge(alo_ok, n + 3)
                        if half == 0:
                            pe.wait_ge(copy_ok, n + 1)
                        else:
                            pe.wait_ge(copy_ok, TT + 2)
                            pe.wait_ge(res_ok, t + 1)
                        for k in range(FT):
                            if k % FG == 0:
                                pe.wait_ge(wlo_ok, half * NGR + k // FG + 1)
                            for j, (a, w) in enumerate(((a_hi, w_hi), (a_lo, w_hi), (a_hi, w_lo))):
                                last = nc.tensor.matmul(banks[:, b, :], a[:, b, k, :], w[:, k, :],
                                                        start=k == 0 and j == 0, stop=k == FT - 1 and j == 2)
                        last.then_inc(mm_ok, 1)

def layer(nc, x, w_chan, w_tok, conv_w, conv_b, gate_bias, gate_sign, gate_log, ident, gain_pre,
          lam_re, lam_im, log_step, s5_b_re, s5_b_im, s5_c_re, s5_c_im, s5_skip, w_glu, b_glu,
          ssd_skip, norm_gain, w_out, gain_mix, gain_ffn, w_gu, w_down, gain_post, out):
    def dram(name, shape):
        return nc.dram_tensor(name, shape, F32).ap()

    u_dram, g_dram = dram("u", [J, S5W, NCH]), dram("g", [J, S5W, NCH])
    kern_dram = dram("kern", [S5G, S5H, PADK])
    conv_dram, tok_dram = dram("conv", [CT, P, T]), dram("tok", [T, CTT * P])
    tokmaj_dram = dram("tokmaj", [T, XW + 2 * VW])
    rows_dram, decay_dram = dram("rows", [TT, NBC, P]), dram("decay", [NBC, TT])
    yt_dram = dram("yt", [DMIX // P, P, T])
    x1_dram, h2_dram, a_dram = dram("x1", [T, D]), dram("h2", [KD, P, T]), dram("a", [FT, P, T])
    first_dram = dram("first", [T, NB])

    with ExitStack() as gates:
        gate_rows = gates.enter_context(nc.sbuf_tensor("gate_rows", [P, T], F32))
        with ExitStack() as ctx:
            sb, _, _ = scope(nc, ctx)
            h_hi, h_lo = sb("h_hi", [P, KD, T], F32R), sb("h_lo", [P, KD, T], F32R)
            phase_norm(nc, x, gain_pre, ident, h_hi, h_lo)
            phase_channels(nc, w_chan, conv_w, conv_b, ident, h_hi, h_lo, u_dram, conv_dram, tok_dram, gate_rows)
            phase_tokens(nc, w_tok, h_hi, h_lo, tokmaj_dram)
        tok_cols = gates.enter_context(nc.sbuf_tensor("tok_cols", [P, TT, 4, ROWS], F32))
        phase_gates(nc, gate_rows, gate_bias, gate_sign, gate_log, ident, tok_cols, rows_dram, decay_dram)
        with ExitStack() as ctx:
            sb, _, _ = scope(nc, ctx)
            table, rho = sb("table", [P, Q, 2, NCH]), sb("rho", [P, Q])
            ca, wt = sb("ca", [P, Q, 2, (J + 1) * S5H]), sb("wt", [P, Q, 2, P])
            phase_s5_setup(nc, lam_re, lam_im, log_step, s5_b_re, s5_b_im, s5_c_re, s5_c_im, s5_skip, ident,
                           table, rho, ca, wt, kern_dram)
            phase_s5(nc, table, rho, ca, wt, kern_dram, u_dram, g_dram)
        phase_s5_glu(nc, w_glu, b_glu, g_dram, yt_dram)
        phase_mixers(nc, tok_cols, rows_dram, decay_dram, conv_dram, tok_dram, tokmaj_dram, ssd_skip, norm_gain,
                     ident, yt_dram)
    phase_out(nc, x, w_out, gain_mix, gain_ffn, ident, yt_dram, x1_dram, h2_dram)
    phase_ffn_up(nc, w_gu, h2_dram, a_dram)
    phase_ffn_down(nc, w_down, gain_post, a_dram, x1_dram, first_dram, out)


def laid_out(I):
    def by_rows(v):
        return v.reshape(-1, P).T

    def by_tiles(w, width):
        k, n = w.shape[0] // P, w.shape[1] // width
        return w.reshape(k, P, n, width).transpose(2, 1, 0, 3).reshape(n, P, k * width)

    def padded(shape, **parts):
        a = np.zeros(shape, np.float32)
        for part, at in ((parts["dt"], 0), (parts["f"], FR), (parts["i"], IR)):
            a[..., at:at + part.shape[-1]] = part
        return a

    def lanes(a):
        a = np.moveaxis(a.reshape((Q, 2) + a.shape[1:]), 0, 2)
        return a.reshape((P,) + a.shape[2:])

    p = {name: v[0] for name, v in I.items()}
    edges = np.cumsum([0, S5W, XW, XW + 2 * NG * NS, HS, 2 * HM * DK, VW, HM, HM, VW])
    u, z, xbc, dt, qk, v, i_, f_, o_ = (p["w_in"][:, a:b] for a, b in zip(edges, edges[1:]))

    def conv_order(ssd, mlstm):
        split, half = XW + (NG + 1) * NS, HM * DK
        return np.concatenate([ssd[..., :split], mlstm[..., half:], ssd[..., split:], mlstm[..., :half]], -1)

    gates = padded((D, P), dt=dt, f=f_, i=i_)
    return {
        "x": I["x"],
        "w_chan": by_tiles(np.concatenate([u, conv_order(xbc, qk), gates], 1), P),
        "w_tok": by_tiles(np.concatenate([z, o_, v], 1), TOKC),
        "conv_w": conv_order(p["ssd_conv_w"], p["mlstm_conv_w"]).T.reshape(CT, P, 4).transpose(1, 0, 2),
        "conv_b": by_rows(conv_order(p["ssd_conv_b"], p["mlstm_conv_b"])),
        "gate_bias": padded((P,), dt=p["ssd_dt_bias"], f=p["mlstm_b_f"], i=p["mlstm_b_i"])[:, None],
        "gate_sign": np.repeat(np.array([1, -1], np.float32), FR)[:, None],
        "gate_log": np.concatenate([p["ssd_a_log"], np.zeros(ROWS - HS, np.float32)])[:, None],
        "ident": np.eye(P, dtype=np.float32),
        "gain_pre": by_rows(p["norm_pre_mix"]),
        "lam_re": lanes(p["s5_lambda_re"]),
        "lam_im": lanes(p["s5_lambda_im"]),
        "log_step": lanes(np.repeat(p["s5_log_step"][:, None], S5P, 1)),
        "s5_b_re": lanes(p["s5_b_re"]),
        "s5_b_im": lanes(p["s5_b_im"]),
        "s5_c_re": lanes(p["s5_c_re"].transpose(0, 2, 1)),
        "s5_c_im": lanes(p["s5_c_im"].transpose(0, 2, 1)),
        "s5_skip": p["s5_d"].T,
        "w_glu": p["s5_w_glu"].reshape(UT, P, S5W).transpose(1, 0, 2),
        "b_glu": by_rows(p["s5_b_glu"]),
        "ssd_skip": p["ssd_d"],
        "norm_gain": by_rows(p["ssd_norm"]),
        "w_out": p["w_out"],
        "gain_mix": p["norm_post_mix"],
        "gain_ffn": by_rows(p["norm_pre_ffn"]),
        "w_gu": np.concatenate([by_tiles(p["w_gate"], P), by_tiles(p["w_up"], P)], 2),
        "w_down": p["w_down"],
        "gain_post": p["norm_post_ffn"],
    }


def kernel(**inputs):
    import concourse.bacc as _bacc
    from concourse.bass_utils import run_bass_kernel_spmd as _run

    arrays = {name: np.ascontiguousarray(a) for name, a in laid_out(
        {name: np.asarray(a) for name, a in inputs.items()}).items()}
    nc = _bacc.Bacc("TRN2", target_bir_lowering=False, num_devices=1)
    args = {name: nc.dram_tensor("in_" + name, a.shape, F32, kind="ExternalInput").ap() for name, a in arrays.items()}
    out = nc.dram_tensor("out_x", [1, T, D], F32, kind="ExternalOutput").ap()
    layer(nc, out=out, **args)
    r = _run(nc, [{"in_" + name: a for name, a in arrays.items()}], core_ids=[0])
    return r.results[0]["out_x"]
```
